# Optimizing a Trainium2 kernel written in Bass

```python
import jax, jax.numpy as jnp
from jax import lax
import numpy as np
import math, functools

D_MODEL = 1024
BATCH = 1
SEQ = 256
DEPTH = 1

D_MIX = D_MODEL
HG_WIDTH = D_MIX // 2
HG_DK = 128
HG_DV = 128
HG_HEADS = HG_WIDTH // HG_DV
HG_CHUNK = 64
NSA_WIDTH = D_MIX - HG_WIDTH
NSA_DH = 64
NSA_HEADS = NSA_WIDTH // NSA_DH
NSA_KV_HEADS = 2
NSA_GROUP = NSA_HEADS // NSA_KV_HEADS
CMP_LEN = 32
CMP_STRIDE = 16
SLC_LEN = 64
SLC_TOPK = 16
WIN = 512
Q_BLOCK = 128
PLE_DIM = 256
PEER_HEADS = 8
PEER_NKEYS = 128
PEER_N = PEER_NKEYS * PEER_NKEYS
PEER_DKEY = 256
PEER_TOPK = 16
PEER_TOKEN_BLOCK = 128
EPS = 1e-6

KV_WIDTH = NSA_KV_HEADS * NSA_DH
SPLIT_SIZES = (HG_WIDTH, HG_WIDTH, HG_WIDTH, HG_WIDTH, NSA_WIDTH,
               KV_WIDTH, KV_WIDTH, KV_WIDTH, KV_WIDTH, KV_WIDTH, KV_WIDTH, 3 * NSA_HEADS)
SPLIT_POINTS = tuple(int(v) for v in np.cumsum(SPLIT_SIZES)[:-1])
D_IN = int(sum(SPLIT_SIZES))


def rmsnorm(x, g):
    x32 = x.astype(jnp.float32)
    y = x32 * lax.rsqrt(jnp.mean(x32 * x32, axis=-1, keepdims=True) + EPS)
    return (y * g.astype(jnp.float32)).astype(x.dtype)

def alibi_slopes(n_heads):
    return jnp.asarray(2.0 ** (-8.0 * np.arange(1, n_heads + 1) / n_heads), dtype=jnp.float32)

def masked_softmax(s, mask):
    s = jnp.where(mask, s, -jnp.inf)
    m = jnp.max(s, axis=-1, keepdims=True)
    m = jnp.where(jnp.isfinite(m), m, 0.0)
    e = jnp.where(mask, jnp.exp(s - m), 0.0)
    return e / jnp.maximum(jnp.sum(e, axis=-1, keepdims=True), 1e-30)

def hgrn2_mixer(q, f_logit, i_val, g, lb, out_gain):
    B, T, _ = q.shape
    f32 = jnp.float32
    C = HG_CHUNK
    n_chunk = T // C
    forget = lb + (1.0 - lb) * jax.nn.sigmoid(f_logit.astype(f32))
    log_f = jnp.log(forget)
    key = 1.0 - forget
    query = jax.nn.silu(q.astype(f32)) * HG_DK ** -0.5

    def chunks(a, d):
        return a.reshape(B, n_chunk, C, HG_HEADS, d).transpose(0, 3, 1, 2, 4)

    qc = chunks(query, HG_DK)
    kc = chunks(key, HG_DK)
    vc = chunks(i_val.astype(f32), HG_DV)
    G = jnp.cumsum(chunks(log_f, HG_DK), axis=3)
    G_ref = G[:, :, :, C // 2 - 1:C // 2]
    G_last = G[:, :, :, C - 1:C]
    causal = jnp.tril(jnp.ones((C, C), dtype=bool))
    a = jnp.einsum('bhntk,bhnsk->bhnts', qc * jnp.exp(G - G_ref), kc * jnp.exp(G_ref - G))
    o_intra = jnp.einsum('bhnts,bhnsv->bhntv', jnp.where(causal, a, 0.0), vc)
    q_in = jnp.moveaxis(qc * jnp.exp(G), 2, 0)
    k_in = jnp.moveaxis(kc * jnp.exp(G_last - G), 2, 0)
    v_in = jnp.moveaxis(vc, 2, 0)
    d_in = jnp.moveaxis(jnp.exp(G_last[:, :, :, 0]), 2, 0)

    def step(S, xs):
        q_t, k_t, v_t, d_t = xs
        o_t = jnp.einsum('bhtk,bhkv->bhtv', q_t, S)
        S = d_t[..., None] * S + jnp.einsum('bhtk,bhtv->bhkv', k_t, v_t)
        return S, o_t

    S0 = jnp.zeros((B, HG_HEADS, HG_DK, HG_DV), f32)
    _, o_inter = lax.scan(step, S0, (q_in, k_in, v_in, d_in))
    o = o_intra + jnp.moveaxis(o_inter, 0, 2)
    o = o.transpose(0, 2, 3, 1, 4).reshape(B, T, HG_HEADS, HG_DV)
    gate = jax.nn.silu(g.astype(f32)).reshape(B, T, HG_HEADS, HG_DV)
    return (rmsnorm(o, out_gain.reshape(HG_HEADS, HG_DV)) * gate).reshape(B, T, HG_WIDTH)

def cmp_to_slc(imp, n_slc):
    ratio = SLC_LEN // CMP_STRIDE
    span = CMP_LEN // CMP_STRIDE
    weights = np.convolve(np.ones(ratio), np.ones(span))
    n_cmp = imp.shape[-1]
    pad = n_slc * ratio + ratio + span - n_cmp
    padded = jnp.pad(imp, [(0, 0)] * (imp.ndim - 1) + [(0, pad)])
    out = float(weights[0]) * padded[..., 0:n_slc * ratio:ratio]
    for o in range(1, len(weights)):
        out = out + float(weights[o]) * padded[..., o:o + n_slc * ratio:ratio]
    return out

def nsa_mixer(q, k_cmp, v_cmp, k_slc, v_slc, k_win, v_win, gate_logit,
              q_gain, k_gain, cmp_pe, cmp_w1, cmp_w2, out_gain):
    B, T, _ = q.shape
    f32 = jnp.float32
    G, R = NSA_KV_HEADS, NSA_GROUP

    def heads(a, n):
        return a.astype(f32).reshape(B, T, n, NSA_DH).transpose(0, 2, 1, 3)

    qh = rmsnorm(heads(q, NSA_HEADS), q_gain) * NSA_DH ** -0.5
    qg = qh.reshape(B, G, R, T, NSA_DH)
    n_cmp = (T - CMP_LEN) // CMP_STRIDE + 1

    def compress(a, pe, w1, w2):
        c = a.reshape(B, G, T // CMP_STRIDE, CMP_STRIDE, NSA_DH)
        blk = jnp.concatenate([c[:, :, j:j + n_cmp] for j in range(CMP_LEN // CMP_STRIDE)], axis=3)
        blk = (blk + pe).reshape(B, G, n_cmp, CMP_LEN * NSA_DH)
        return jax.nn.gelu(blk @ w1) @ w2

    kc = rmsnorm(compress(heads(k_cmp, G), cmp_pe[0], cmp_w1[0], cmp_w2[0]), k_gain[0])
    vc = compress(heads(v_cmp, G), cmp_pe[1], cmp_w1[1], cmp_w2[1])
    cmp_end = jnp.arange(n_cmp) * CMP_STRIDE + CMP_LEN - 1
    n_slc = T // SLC_LEN
    top_n = min(SLC_TOPK, n_slc)
    k_sb = rmsnorm(heads(k_slc, G), k_gain[1]).reshape(B, G, n_slc, SLC_LEN, NSA_DH)
    v_sb = heads(v_slc, G).reshape(B, G, n_slc, SLC_LEN, NSA_DH)
    pad_w = ((0, 0), (0, 0), (WIN, 0), (0, 0))
    k_wp = jnp.pad(rmsnorm(heads(k_win, G), k_gain[2]), pad_w)
    v_wp = jnp.pad(heads(v_win, G), pad_w)
    gates = jax.nn.sigmoid(gate_logit.astype(f32)).reshape(B, T, NSA_HEADS, 3).transpose(0, 2, 1, 3)
    gates = gates.reshape(B, G, R, T, 3)
    slopes = alibi_slopes(NSA_HEADS).reshape(1, G, R, 1, 1)
    gather_blocks = jax.vmap(jax.vmap(lambda blocks, ix: blocks[ix]))

    def query_block(b):
        t0 = b * Q_BLOCK
        qb = lax.dynamic_slice_in_dim(qg, t0, Q_BLOCK, axis=3)
        gb = lax.dynamic_slice_in_dim(gates, t0, Q_BLOCK, axis=3)
        t = t0 + jnp.arange(Q_BLOCK)
        dist_c = t[:, None] - cmp_end[None, :]
        s_c = jnp.einsum('bgrtd,bgnd->bgrtn', qb, kc) - slopes * dist_c
        p_c = masked_softmax(s_c, dist_c >= 0)
        o_c = jnp.einsum('bgrtn,bgnd->bgrtd', p_c, vc)
        imp = cmp_to_slc(jnp.sum(p_c, axis=2), n_slc)
        blk_id = jnp.arange(n_slc)[None, :]
        cur = (t // SLC_LEN)[:, None]
        forced = (blk_id == 0) | (blk_id == cur) | (blk_id == cur - 1)
        imp = jnp.where(forced, jnp.inf, jnp.where(blk_id <= cur, imp, -jnp.inf))
        _, sel = lax.top_k(imp, top_n)
        ks = gather_blocks(k_sb, sel).reshape(B, G, Q_BLOCK, top_n * SLC_LEN, NSA_DH)
        vs = gather_blocks(v_sb, sel).reshape(B, G, Q_BLOCK, top_n * SLC_LEN, NSA_DH)
        pos = (sel[..., None] * SLC_LEN + jnp.arange(SLC_LEN)).reshape(B, G, Q_BLOCK, top_n * SLC_LEN)
        dist_s = (t[:, None] - pos)[:, :, None]
        s_s = jnp.einsum('bgrtd,bgtmd->bgrtm', qb, ks) - slopes * dist_s
        p_s = masked_softmax(s_s, dist_s >= 0)
        o_s = jnp.einsum('bgrtm,bgtmd->bgrtd', p_s, vs)
        kw = lax.dynamic_slice_in_dim(k_wp, t0, WIN + Q_BLOCK, axis=2)
        vw = lax.dynamic_slice_in_dim(v_wp, t0, WIN + Q_BLOCK, axis=2)
        pos_w = t0 - WIN + jnp.arange(WIN + Q_BLOCK)
        dist_w = t[:, None] - pos_w[None, :]
        valid_w = (dist_w >= 0) & (dist_w < WIN) & (pos_w[None, :] >= 0)
        s_w = jnp.einsum('bgrtd,bgsd->bgrts', qb, kw) - slopes * dist_w
        p_w = masked_softmax(s_w, valid_w)
        o_w = jnp.einsum('bgrts,bgsd->bgrtd', p_w, vw)
        return gb[..., 0:1] * o_c + gb[..., 1:2] * o_s + gb[..., 2:3] * o_w

    o = lax.map(query_block, jnp.arange(T // Q_BLOCK))
    o = o.transpose(1, 0, 4, 2, 3, 5).reshape(B, T, NSA_HEADS, NSA_DH)
    return rmsnorm(o, out_gain.reshape(NSA_HEADS, NSA_DH)).reshape(B, T, NSA_WIDTH)

def peer_ffn(h, wq, sub_keys, u, v):
    B, T, D = h.shape
    f32 = jnp.float32
    tokens = h.reshape(-1, PEER_TOKEN_BLOCK, D)

    def token_block(xt):
        q = (xt @ wq).astype(f32).reshape(PEER_TOKEN_BLOCK, PEER_HEADS, 2, PEER_DKEY // 2)
        s = jnp.einsum('thcd,hckd->thck', q, sub_keys.astype(f32))
        top_s, top_i = lax.top_k(s, PEER_TOPK)
        cand = top_s[:, :, 0, :, None] + top_s[:, :, 1, None, :]
        best_s, best_c = lax.top_k(cand.reshape(PEER_TOKEN_BLOCK, PEER_HEADS, PEER_TOPK * PEER_TOPK), PEER_TOPK)
        i1 = jnp.take_along_axis(top_i[:, :, 0], best_c // PEER_TOPK, axis=-1)
        i2 = jnp.take_along_axis(top_i[:, :, 1], best_c % PEER_TOPK, axis=-1)
        expert = i1 * PEER_NKEYS + i2
        w = jax.nn.softmax(best_s, axis=-1)
        act = jax.nn.gelu(jnp.einsum('thkd,td->thk', u[expert].astype(f32), xt.astype(f32)))
        return jnp.einsum('thk,thkd->td', w * act, v[expert].astype(f32))

    return lax.map(token_block, tokens).reshape(B, T, D).astype(h.dtype)

def first_inputs(seed: int = 0) -> dict:
    key = jax.random.key(seed)
    ks = jax.random.split(key, 21)
    n = jax.random.normal
    f32 = jnp.float32

    def gain(k, shape):
        return 1.0 + 0.02 * n(k, shape, f32)

    return {
        'x': n(ks[0], (BATCH, SEQ, D_MODEL), f32),
        'p': n(ks[1], (DEPTH, BATCH, SEQ, PLE_DIM), f32),
        'mix_norm': gain(ks[2], (DEPTH, D_MODEL)),
        'w_in': n(ks[3], (DEPTH, D_MODEL, D_IN), f32) * D_MODEL ** -0.5,
        'hg_lb_logits': 0.1 * n(ks[4], (DEPTH + 1, HG_WIDTH), f32),
        'hg_out_norm': gain(ks[5], (DEPTH, HG_WIDTH)),
        'nsa_q_norm': gain(ks[6], (DEPTH, NSA_DH)),
        'nsa_k_norm': gain(ks[7], (DEPTH, 3, NSA_DH)),
        'cmp_pe': 0.02 * n(ks[8], (DEPTH, 2, CMP_LEN, NSA_DH), f32),
        'cmp_w1': n(ks[9], (DEPTH, 2, CMP_LEN * NSA_DH, NSA_DH), f32) * (CMP_LEN * NSA_DH) ** -0.5,
        'cmp_w2': n(ks[10], (DEPTH, 2, NSA_DH, NSA_DH), f32) * NSA_DH ** -0.5,
        'nsa_out_norm': gain(ks[11], (DEPTH, NSA_WIDTH)),
        'w_out': n(ks[12], (DEPTH, D_MIX, D_MODEL), f32) * D_MIX ** -0.5,
        'ffn_norm': gain(ks[13], (DEPTH, D_MODEL)),
        'peer_wq': n(ks[14], (DEPTH, D_MODEL, PEER_HEADS * PEER_DKEY), f32) * D_MODEL ** -0.5,
        'peer_keys': n(ks[15], (DEPTH, PEER_HEADS, 2, PEER_NKEYS, PEER_DKEY // 2), f32) * (PEER_DKEY // 2) ** -0.5,
        'peer_u': n(ks[16], (DEPTH, PEER_N, D_MODEL), f32) * D_MODEL ** -0.5,
        'peer_v': n(ks[17], (DEPTH, PEER_N, D_MODEL), f32) * PEER_HEADS ** -0.5,
        'ple_proj': n(ks[18], (DEPTH, PLE_DIM, D_MODEL), f32) * PLE_DIM ** -0.5,
        'ple_gate_norm': gain(ks[19], (DEPTH, D_MODEL)),
        'ple_gate_w': n(ks[20], (DEPTH, D_MODEL, D_MODEL), f32) * D_MODEL ** -0.5,
    }

def first_block(x, p, mix_norm, w_in, hg_lb_logits, hg_out_norm, nsa_q_norm, nsa_k_norm,
              cmp_pe, cmp_w1, cmp_w2, nsa_out_norm, w_out, ffn_norm, peer_wq, peer_keys,
              peer_u, peer_v, ple_proj, ple_gate_norm, ple_gate_w):
    lb_table = jnp.cumsum(jax.nn.softmax(hg_lb_logits.astype(jnp.float32), axis=0), axis=0)
    h = x
    for i in range(DEPTH):
        a = rmsnorm(h, mix_norm[i])
        proj = a @ w_in[i]
        (hg_q, hg_f, hg_i, hg_g, n_q, n_kc, n_vc, n_ks, n_vs, n_kw, n_vw, n_gate) = jnp.split(proj, SPLIT_POINTS, axis=-1)
        o_hg = hgrn2_mixer(hg_q, hg_f, hg_i, hg_g, lb_table[i], hg_out_norm[i])
        o_nsa = nsa_mixer(n_q, n_kc, n_vc, n_ks, n_vs, n_kw, n_vw, n_gate,
                          nsa_q_norm[i], nsa_k_norm[i], cmp_pe[i], cmp_w1[i], cmp_w2[i], nsa_out_norm[i])
        mixed = jnp.concatenate([o_hg, o_nsa], axis=-1).astype(h.dtype)
        h = h + mixed @ w_out[i]
        h = h + peer_ffn(rmsnorm(h, ffn_norm[i]), peer_wq[i], peer_keys[i], peer_u[i], peer_v[i])
        gate = jax.nn.sigmoid(rmsnorm(h, ple_gate_norm[i]) @ ple_gate_w[i])
        h = h + (p[i] @ ple_proj[i]) * gate
    return h


DEPTH_2 = 2

SB_HEADS = 8
SB_HEAD_DIM = 64
SB_WIDTH = SB_HEADS * SB_HEAD_DIM
RET_HEADS = 4
RET_HEAD_DIM = 128
RET_WIDTH = RET_HEADS * RET_HEAD_DIM
EVEN_IN = 3 * SB_WIDTH + 4 * RET_WIDTH
GLA_HEADS = 4
GLA_DK = 128
GLA_DV = 256
GLA_K_WIDTH = GLA_HEADS * GLA_DK
GLA_V_WIDTH = GLA_HEADS * GLA_DV
GLA_GATE_RANK = 16
GLA_GATE_TAU = 16.0
ODD_IN = 2 * GLA_K_WIDTH + 2 * GLA_V_WIDTH + GLA_GATE_RANK
D_FF = 2816
CONV_WIDTH = 3
RET_CHUNK = 128
GLA_CHUNK = 64
ROPE_BASE = 10000.0
N_EVEN = (DEPTH_2 + 1) // 2
N_ODD = DEPTH_2 // 2


def rms_norm(x, g):
    xf = x.astype(jnp.float32)
    y = xf * lax.rsqrt(jnp.mean(xf * xf, axis=-1, keepdims=True) + EPS)
    return (y * g.astype(jnp.float32)).astype(x.dtype)

def to_heads(t, n):
    b, s, w = t.shape
    return t.reshape(b, s, n, w // n).transpose(0, 2, 1, 3)

def from_heads(t):
    b, h, s, d = t.shape
    return t.transpose(0, 2, 1, 3).reshape(b, s, h * d)

def rope(x, pos):
    d = x.shape[-1]
    half = d // 2
    inv = ROPE_BASE ** (-jnp.arange(half, dtype=jnp.float32) / half)
    ang = pos.astype(jnp.float32)[:, None] * inv[None, :]
    cos, sin = jnp.cos(ang), jnp.sin(ang)
    xf = x.astype(jnp.float32)
    x1, x2 = xf[..., :half], xf[..., half:]
    return jnp.concatenate([x1 * cos - x2 * sin, x1 * sin + x2 * cos], axis=-1).astype(x.dtype)

def stick_breaking_attention(q, k, v):
    b, h, s, d = q.shape
    nb = s // Q_BLOCK
    scale = d ** -0.5
    qb = q.reshape(b, h, nb, Q_BLOCK, d).transpose(2, 0, 1, 3, 4)
    kf = k.astype(jnp.float32)
    vf = v.astype(jnp.float32)
    key_pos = jnp.arange(s)

    def block(args):
        qi, i = args
        q_pos = i * Q_BLOCK + jnp.arange(Q_BLOCK)
        z = jnp.einsum('bhqd,bhkd->bhqk', qi.astype(jnp.float32), kf) * scale
        mask = key_pos[None, :] < q_pos[:, None]
        log_beta = jax.nn.log_sigmoid(z)
        log_1m_beta = jnp.where(mask, -jax.nn.softplus(z), 0.0)
        suffix = lax.cumsum(log_1m_beta, axis=3, reverse=True) - log_1m_beta
        w = jnp.where(mask, jnp.exp(log_beta + suffix), 0.0)
        return jnp.einsum('bhqk,bhkd->bhqd', w, vf)

    out = lax.map(block, (qb, jnp.arange(nb)))
    return out.transpose(1, 2, 0, 3, 4).reshape(b, h, s, d).astype(v.dtype)

def retention_chunkwise(q, k, v, log_gamma):
    b, h, s, d = q.shape
    c = RET_CHUNK
    nc = s // c
    qc = q.astype(jnp.float32).reshape(b, h, nc, c, d)
    kc = (k.astype(jnp.float32) * d ** -0.5).reshape(b, h, nc, c, d)
    vc = v.astype(jnp.float32).reshape(b, h, nc, c, d)
    pos = jnp.arange(c, dtype=jnp.float32)
    lg = log_gamma[:, None]
    diff = pos[:, None] - pos[None, :]
    decay_intra = jnp.where(diff >= 0, jnp.exp(lg[:, :, None] * jnp.maximum(diff, 0.0)), 0.0)
    scores = jnp.einsum('bhnid,bhnjd->bhnij', qc, kc) * decay_intra[None, :, None]
    inner = jnp.einsum('bhnij,bhnje->bhnie', scores, vc)
    zeta = jnp.exp(lg * (c - 1 - pos))
    contrib = jnp.einsum('bhnjd,hj,bhnje->bhnde', kc, zeta, vc)
    g_chunk = jnp.exp(lg * c)[None, :, :, None]

    def step(state, cn):
        return g_chunk * state + cn, state

    _, r_prev = lax.scan(step, jnp.zeros((b, h, d, d), jnp.float32), contrib.transpose(2, 0, 1, 3, 4))
    r_prev = r_prev.transpose(1, 2, 0, 3, 4)
    xi = jnp.exp(lg * (pos + 1.0))
    cross = jnp.einsum('bhnid,bhnde->bhnie', qc, r_prev) * xi[None, :, None, :, None]
    return (inner + cross).reshape(b, h, s, d).astype(v.dtype)

def gla_chunked(q, k, v, log_alpha):
    b, h, s, dk = q.shape
    dv = v.shape[-1]
    c = GLA_CHUNK
    nc = s // c
    qc = (q.astype(jnp.float32) * dk ** -0.5).reshape(b, h, nc, c, dk)
    kc = k.astype(jnp.float32).reshape(b, h, nc, c, dk)
    vc = v.astype(jnp.float32).reshape(b, h, nc, c, dv)
    cum = lax.cumsum(log_alpha.astype(jnp.float32).reshape(b, h, nc, c, dk), axis=3)
    cum_last = cum[:, :, :, -1:, :]
    q_t = qc * jnp.exp(cum)
    k_t = kc * jnp.exp(-cum)
    causal = jnp.tril(jnp.ones((c, c), dtype=bool))
    a = jnp.where(causal, jnp.einsum('bhnid,bhnjd->bhnij', q_t, k_t), 0.0)
    intra = jnp.einsum('bhnij,bhnje->bhnie', a, vc)
    contrib = jnp.einsum('bhnjd,bhnje->bhnde', kc * jnp.exp(cum_last - cum), vc)
    chunk_decay = jnp.exp(cum_last[:, :, :, 0, :])

    def step(state, inp):
        dec, cn = inp
        return dec[..., None] * state + cn, state

    _, s_prev = lax.scan(step, jnp.zeros((b, h, dk, dv), jnp.float32),
                         (chunk_decay.transpose(2, 0, 1, 3), contrib.transpose(2, 0, 1, 3, 4)))
    s_prev = s_prev.transpose(1, 2, 0, 3, 4)
    inter = jnp.einsum('bhnid,bhnde->bhnie', q_t, s_prev)
    return (intra + inter).reshape(b, h, s, dv).astype(v.dtype)

def even_mixer(hn, w_in, q_gain, k_gain, ret_gain, w_out):
    s = hn.shape[1]
    p = hn @ w_in
    cuts = [SB_WIDTH, 2 * SB_WIDTH, 3 * SB_WIDTH,
            3 * SB_WIDTH + RET_WIDTH, 3 * SB_WIDTH + 2 * RET_WIDTH, 3 * SB_WIDTH + 3 * RET_WIDTH]
    sb_q, sb_k, sb_v, r_q, r_k, r_v, r_g = jnp.split(p, cuts, axis=-1)
    qa = rms_norm(to_heads(sb_q, SB_HEADS), q_gain)
    ka = rms_norm(to_heads(sb_k, SB_HEADS), k_gain)
    out_a = from_heads(stick_breaking_attention(qa, ka, to_heads(sb_v, SB_HEADS)))
    pos = jnp.arange(s)
    qb = rope(to_heads(r_q, RET_HEADS), pos)
    kb = rope(to_heads(r_k, RET_HEADS), pos)
    log_gamma = jnp.log(1.0 - jnp.exp2(-5.0 - jnp.arange(RET_HEADS, dtype=jnp.float32)))
    ret = retention_chunkwise(qb, kb, to_heads(r_v, RET_HEADS), log_gamma)
    out_b = from_heads(rms_norm(ret, ret_gain)) * jax.nn.silu(r_g)
    return jnp.concatenate([out_a, out_b], axis=-1) @ w_out

def odd_mixer(hn, w_in, w_alpha, b_alpha, out_gain, w_out):
    p = hn @ w_in
    cuts = [GLA_K_WIDTH, 2 * GLA_K_WIDTH, 2 * GLA_K_WIDTH + GLA_V_WIDTH, 2 * GLA_K_WIDTH + 2 * GLA_V_WIDTH]
    g_q, g_k, g_v, g_r, g_a = jnp.split(p, cuts, axis=-1)
    log_alpha = jax.nn.log_sigmoid((g_a @ w_alpha + b_alpha).astype(jnp.float32)) / GLA_GATE_TAU
    o = gla_chunked(to_heads(g_q, GLA_HEADS), to_heads(g_k, GLA_HEADS),
                    to_heads(g_v, GLA_HEADS), to_heads(log_alpha, GLA_HEADS))
    return (from_heads(rms_norm(o, out_gain)) * jax.nn.silu(g_r)) @ w_out

def conv_ffn(hn, w_up, conv_w, conv_b, w_down):
    s = hn.shape[1]
    u, v = jnp.split(hn @ w_up, 2, axis=-1)
    up = jnp.pad(u, ((0, 0), (CONV_WIDTH - 1, 0), (0, 0)))
    uc = conv_b + conv_w[0] * up[:, 0:s]
    for j in range(1, CONV_WIDTH):
        uc = uc + conv_w[j] * up[:, j:j + s]
    return (jax.nn.silu(uc) * v) @ w_down

def second_inputs(seed: int = 0) -> dict:
    key = jax.random.key(seed)
    ks = jax.random.split(key, 20)
    f32 = jnp.float32

    def nrm(k, shape, scale):
        return jax.random.normal(k, shape, f32) * scale

    return {
        'x': nrm(ks[0], (BATCH, SEQ, D_MODEL), 1.0),
        'mix_norm_g': 1.0 + nrm(ks[1], (DEPTH_2, D_MODEL), 0.02),
        'even_w_in': nrm(ks[2], (N_EVEN, D_MODEL, EVEN_IN), D_MODEL ** -0.5),
        'sb_q_gain': 1.0 + nrm(ks[3], (N_EVEN, SB_HEAD_DIM), 0.02),
        'sb_k_gain': 1.0 + nrm(ks[4], (N_EVEN, SB_HEAD_DIM), 0.02),
        'ret_out_gain': 1.0 + nrm(ks[5], (N_EVEN, RET_HEAD_DIM), 0.02),
        'even_w_out': nrm(ks[6], (N_EVEN, SB_WIDTH + RET_WIDTH, D_MODEL), (SB_WIDTH + RET_WIDTH) ** -0.5),
        'odd_w_in': nrm(ks[7], (N_ODD, D_MODEL, ODD_IN), D_MODEL ** -0.5),
        'gla_w_alpha': nrm(ks[8], (N_ODD, GLA_GATE_RANK, GLA_K_WIDTH), GLA_GATE_RANK ** -0.5),
        'gla_b_alpha': nrm(ks[9], (N_ODD, GLA_K_WIDTH), 0.1),
        'gla_out_gain': 1.0 + nrm(ks[10], (N_ODD, GLA_DV), 0.02),
        'odd_w_out': nrm(ks[11], (N_ODD, GLA_V_WIDTH, D_MODEL), GLA_V_WIDTH ** -0.5),
        'ffn_norm_g': 1.0 + nrm(ks[12], (DEPTH_2, D_MODEL), 0.02),
        'ffn_w_up': nrm(ks[13], (DEPTH_2, D_MODEL, 2 * D_FF), D_MODEL ** -0.5),
        'ffn_conv_w': nrm(ks[14], (DEPTH_2, CONV_WIDTH, D_FF), CONV_WIDTH ** -0.5),
        'ffn_conv_b': nrm(ks[15], (DEPTH_2, D_FF), 0.01),
        'ffn_w_down': nrm(ks[16], (DEPTH_2, D_FF, D_MODEL), D_FF ** -0.5),
    }

def second_block(x, mix_norm_g, even_w_in, sb_q_gain, sb_k_gain, ret_out_gain, even_w_out,
              odd_w_in, gla_w_alpha, gla_b_alpha, gla_out_gain, odd_w_out,
              ffn_norm_g, ffn_w_up, ffn_conv_w, ffn_conv_b, ffn_w_down):
    h = x
    for layer in range(DEPTH_2):
        hn = rms_norm(h, mix_norm_g[layer])
        if layer % 2 == 0:
            e = layer // 2
            mix = even_mixer(hn, even_w_in[e], sb_q_gain[e], sb_k_gain[e], ret_out_gain[e], even_w_out[e])
        else:
            o = layer // 2
            mix = odd_mixer(hn, odd_w_in[o], gla_w_alpha[o], gla_b_alpha[o], gla_out_gain[o], odd_w_out[o])
        h = h + mix.astype(h.dtype)
        hn = rms_norm(h, ffn_norm_g[layer])
        h = h + conv_ffn(hn, ffn_w_up[layer], ffn_conv_w[layer], ffn_conv_b[layer], ffn_w_down[layer]).astype(h.dtype)
    return h


def setup_inputs(seed=0):
    out = dict(first_inputs(seed))
    for name, value in second_inputs(seed + 1).items():
        if name != "x":
            out[name + "_2"] = value
    return out


def reference(
    x, p, mix_norm, w_in, hg_lb_logits, hg_out_norm, nsa_q_norm, nsa_k_norm, cmp_pe, cmp_w1,
    cmp_w2, nsa_out_norm, w_out, ffn_norm, peer_wq, peer_keys, peer_u, peer_v, ple_proj,
    ple_gate_norm, ple_gate_w, mix_norm_g_2, even_w_in_2, sb_q_gain_2, sb_k_gain_2,
    ret_out_gain_2, even_w_out_2, odd_w_in_2, gla_w_alpha_2, gla_b_alpha_2, gla_out_gain_2,
    odd_w_out_2, ffn_norm_g_2, ffn_w_up_2, ffn_conv_w_2, ffn_conv_b_2, ffn_w_down_2,
):
    x = first_block(
        x, p, mix_norm, w_in, hg_lb_logits, hg_out_norm, nsa_q_norm, nsa_k_norm, cmp_pe, cmp_w1,
        cmp_w2, nsa_out_norm, w_out, ffn_norm, peer_wq, peer_keys, peer_u, peer_v, ple_proj,
        ple_gate_norm, ple_gate_w,
    )
    return second_block(
        x, mix_norm_g_2, even_w_in_2, sb_q_gain_2, sb_k_gain_2, ret_out_gain_2, even_w_out_2,
        odd_w_in_2, gla_w_alpha_2, gla_b_alpha_2, gla_out_gain_2, odd_w_out_2, ffn_norm_g_2,
        ffn_w_up_2, ffn_conv_w_2, ffn_conv_b_2, ffn_w_down_2,
    )


_drawn_inputs = setup_inputs


def setup_inputs(seed=0):
    import zlib

    import numpy as np

    out = dict(_drawn_inputs(seed))
    spreads = {}
    factors = {'hg_lb_logits': 4.315,
     'hg_out_norm': 3.004,
     'nsa_q_norm': 2.741,
     'nsa_k_norm': 2.976,
     'ple_gate_norm': 8.0,
     'sb_q_gain_2': 8.0,
     'sb_k_gain_2': 8.0,
     'ret_out_gain_2': 7.243,
     'gla_b_alpha_2': 3.708,
     'gla_out_gain_2': 7.808,
     'ffn_norm_g_2': 3.412,
     'ffn_conv_b_2': 8.0}
    for name, (base, spread) in spreads.items():
        noise = np.random.default_rng([zlib.crc32(name.encode()), seed]).standard_normal(out[name].shape)
        drawn = base * np.exp(spread * noise) if base else spread * noise
        out[name] = __import__('jax').numpy.asarray(drawn.astype(out[name].dtype))
    for name, factor in factors.items():
        out[name] = (out[name] * factor).astype(out[name].dtype)
    return out
```

```python
from contextlib import ExitStack

import numpy as np

import concourse.bass as bass
from concourse import mybir

F32 = mybir.dt.float32
U32 = mybir.dt.uint32
I32 = mybir.dt.int32
ALU = mybir.AluOpType
ACT = mybir.ActivationFunctionType
X = mybir.AxisListType.X

P = 128
T, D = 256, 1024
TT, KD = T // P, D // P
EPS = 1e-6
BIG = 1e30

CH = 64
NCH = T // CH
HH, DK = 4, 128
HG_DV, GLA_DV = 128, 256
NH, NG, DH = 8, 2, 64
CMP_LEN, CMP_STRIDE = 32, 16
NCMP = (T - CMP_LEN) // CMP_STRIDE + 1
PH, NK, TOPK = 8, 128, 16
PAIRS = PH * TOPK
GATHER_SLOTS = 8
GBODY = 2 * TOPK
DFF = 2816
FT = DFF // P
FCH = FT // 2
HQ, HF, HI, HGT, NQ, NKC, NVC, NKS, NVS, NKW, NVW, NGATE, D_IN1 = (
    0, 512, 1024, 1536, 2048, 2560, 2688, 2816, 2944, 3072, 3200, 3328, 3352)
RING = 3

G_MIX, G_OUT1, G_PLE, G_MIX2, G_FFN2 = 0, 8, 16, (24, 40), (32, 48)
G_OUT2, G_OUT3, G_SBQ, G_SBK, G_NQ, G_KC, G_KS, G_KW, G_LB, G_BAL = 56, 64, 72, 73, 74, 75, 76, 77, 78, 86
G_ROWS, G_ONE = 90, 56
CW_ROWS = 4 * FT

C_COLS = {}
_at = 0
for _name, _n in (("ident", P), ("dist", TT * T), ("cbias", TT * NH * NCMP), ("cmask", TT * NCMP),
                  ("cos", TT * 64), ("sin", TT * 64), ("decay", HH * T), ("negstrict", P), ("negones", P),
                  ("sbmask", P), ("causal", CH), ("sel", NH * NCMP), ("blk", NH), ("iota", TOPK)):
    C_COLS[_name] = (_at, _at + _n)
    _at += _n
C_WIDTH = _at

SIDE = (0, 384)
SLOPES = [2.0 ** (-8.0 * (i + 1) / NH) for i in range(NH)]


def shape_constants():
    c = np.zeros((P, C_WIDTH), np.float32)

    def put(name, a):
        lo, hi = C_COLS[name]
        c[:a.shape[0], lo:hi] = a.reshape(a.shape[0], -1)

    p = np.arange(P)
    t = p[:, None] + P * np.arange(TT)[None, :]
    put("ident", np.eye(P))
    dist = (t[:, :, None] - np.arange(T)).astype(np.float64)
    put("dist", np.where(dist >= 0, dist, BIG))
    cend = np.arange(NCMP) * CMP_STRIDE + CMP_LEN - 1
    dc = (t[:, :, None] - cend).astype(np.float64)
    sl = np.asarray(SLOPES)[None, None, :, None]
    put("cbias", np.where(dc[:, :, None] >= 0, -sl * dc[:, :, None], -BIG * sl))
    put("cmask", (dc >= 0).astype(np.float32))
    inv = np.float32(10000.0) ** (-np.arange(64, dtype=np.float32) / np.float32(64))
    ang = (t[:, :, None].astype(np.float32) * inv).astype(np.float32)
    put("cos", np.cos(ang))
    put("sin", np.sin(ang))
    lg = np.log(1.0 - np.exp2(-5.0 - np.arange(HH)))
    d = np.arange(T)[None, :] - p[:, None]
    put("decay", np.where(d[:, None] >= 0, np.exp(lg[None, :, None] * np.maximum(d, 0)[:, None]), 0.0) * DK ** -0.5)
    put("negstrict", -(p[:, None] > p[None, :]).astype(np.float32))
    put("negones", -np.ones((P, P)))
    put("sbmask", (p[:, None] < p[None, :]).astype(np.float32))
    put("causal", ((p % CH)[:, None] <= np.arange(CH)[None, :]).astype(np.float32))
    hn = np.arange(NH * NCMP)
    put("sel", (np.arange(NCMP)[:, None] == (hn % NCMP)[None, :]).astype(np.float32))
    put("blk", ((hn // NCMP)[:, None] == np.arange(NH)[None, :]).astype(np.float32))
    put("iota", np.tile(np.arange(TOPK, dtype=np.float32), (P, 1)))
    return c


def weight_chunks():
    out = [("w_in", c) for c in range(7)] + [("w_out", c) for c in range(2)]
    out += [("peer_wq", c) for c in range(4)] + [("ple_proj", 0)] + [("ple_gate_w", c) for c in range(2)]
    out += [("even_w_in", c) for c in range(7)] + [("even_w_out", c) for c in range(2)]
    out += [("up0", c) for c in range(FCH)] + [("down0", c) for c in range(FCH)]
    out += [("odd_w_in", c) for c in range(7)] + [("odd_w_out", c) for c in range(2)]
    out += [("up1", c) for c in range(FCH)] + [("down1", c) for c in range(FCH)]
    return out


CHUNKS = weight_chunks()
CHUNK_AT = {}
for _i, (_n, _c) in enumerate(CHUNKS):
    CHUNK_AT.setdefault(_n, _i)


def bank_plan():
    used, plan, turn = [0, 0], [], 0
    for name, c in CHUNKS:
        if name.startswith("down") or name == "ple_proj":
            plan.append((None, tuple(used)))
            if c == FCH - 1 or name == "ple_proj":
                used = [used[0] + 1, used[1] + 1]
        else:
            plan.append((turn, tuple(used)))
            used[turn] += 1
            turn = 1 - turn
    return plan


PLAN = bank_plan()

ROOTS = ["mix1", "nsa_qk", "hg", "kc", "nsa_o", "peer", "ple", "mix2a", "sbqk", "ret", "ffn2a", "mix2b", "gla", "ffn2b"]
TURNS = ["mix1", "out1", "peer", "ple", "mix2a", "out2", "ffn2a", "mix2b", "out3", "ffn2b"]
TURN_GAIN = {"mix1": G_MIX, "out1": G_OUT1, "peer": None, "ple": G_PLE, "mix2a": G_MIX2[0], "out2": G_OUT2,
             "ffn2a": G_FFN2[0], "mix2b": G_MIX2[1], "out3": G_OUT3, "ffn2b": G_FFN2[1]}
NORMS = ["mix1", "peer", "ple", "mix2a", "ffn2a", "mix2b", "ffn2b"]
N_ROW_DMAS = 39
UPTO = 10
LEVEL = dict(w_in=1, w_out=4, peer_wq=5, ple_proj=5, ple_gate_w=6, even_w_in=7, even_w_out=7, up0=8, down0=8,
             odd_w_in=9, odd_w_out=9, up1=10, down1=10)
END = {1: "mix1", 2: "mix1", 3: "mix1", 4: "peer", 5: "ple", 6: "mix2a", 7: "ffn2a", 8: "mix2b", 9: "ffn2b", 10: "end"}[UPTO]


def two_blocks(nc, a, consts, out):
    with ExitStack() as ctx:
        def sb(name, shape, dt=F32):
            return ctx.enter_context(nc.sbuf_tensor(name, shape, dt))

        def sem(name):
            return ctx.enter_context(nc.semaphore(name))

        h = sb("h", [P, TT, D])
        hn = sb("hn", [P, TT, D])
        mixed = sb("mixed", [P, TT, D])
        xT = sb("xT", [P, KD, T])
        ring = sb("ring", [P, RING, 4096])
        proj = sb("proj", [P, 7168])
        arena = sb("arena", [P, 8, 1024])
        reset = sb("reset", [P, 1024])
        aTm = sb("aTm", [P, HH * TT, P])
        k2tok = sb("k2tok", [P, TT, HH * DK])
        state = sb("state", [P, 3, HH * GLA_DV])
        wX = sb("wX", [P, 4096])
        cst = sb("cst", [P, C_WIDTH])
        gcol = sb("gcol", [P, 96])
        cw = sb("cw", [P, 2, CW_ROWS])
        pe_col = sb("pe_col", [P, 2, CMP_LEN])
        w2 = sb("w2", [DH, 2, DH])
        walpha = sb("walpha", [16, 512])
        gaT = sb("gaT", [16, T])
        ss = sb("ss", [P, 2 * len(NORMS)])
        var = sb("var", [P, len(ROOTS), 32])
        std = sb("std", [P, len(ROOTS), 32])
        rstd = sb("rstd", [P, len(ROOTS), 32])
        lbw = sb("lbw", [P, 6, HH])
        dec = sb("dec", [P, 2, HH * NCH])
        hid = sb("hid", [DH, 4, NCMP])
        kvc = sb("kvc", [NCMP, 4, DH])
        kcd = sb("kcd", [NCMP, NG, 2, DH])
        kcT = sb("kcT", [P, NG, NCMP])
        cst8 = sb("cst8", [P, 3, TT * NH])
        nmx = sb("nmx", [P, TT * NH, 2])
        sums = sb("sums", [P, TT, 2, NH])
        coef = sb("coef", [P, TT, 3, NH])
        gates = sb("gates", [P, TT, 24])
        routes = sb("routes", [P, TT, PAIRS], U32)
        stage = sb("stage", [P, 2, TOPK], U32)
        dots = sb("dots", [P, TT, PAIRS])
        gatew = sb("gatew", [P, TT, PAIRS])
        ps = ctx.enter_context(nc.psum_tensor("ps", [P, 8, 512], F32))

        psf = ps[:].rearrange("p b n -> p (b n)")
        ident = cst[:, slice(*C_COLS["ident"])]

        def cview(name):
            return cst[:, slice(*C_COLS[name])]

        def block(i, n=1):
            return arena[:, i:i + n, :].rearrange("p a n -> p (a n)")

        def grid(ap, b, c):
            return ap.rearrange("p (b c) -> p b c", b=b, c=c)

        def tokens(lo, n, tt=None):
            v = proj[:].rearrange("p (t n) -> p t n", t=TT)
            return v[:, :, lo:lo + n] if tt is None else v[:, tt, lo:lo + n]

        def pair(turn):
            return psf[:, turn * 1024:(turn + 1) * 1024]

        gbc = block(7)
        vblock = state[0:NH * NCMP, 0, 512:1024].rearrange("p (h d) -> p h d", h=NH)
        pc = state[:, 1, 512:512 + TT * NH * NCMP].rearrange("p (t n) -> p t n", t=TT)
        pcT = state[0:NH * NCMP, 2, 512:512 + TT * P].rearrange("p (t n) -> p t n", t=TT)
        p_raw, pT = grid(proj[:, 6144:6656], TT, T), grid(proj[:, 6656:7168], 2, T)
        rows = mixed[:].rearrange("p a n -> p (a n)")
        g_rows, cw_rows, pe_rows = rows[:, 0:P], grid(rows[:, P:3 * P], 2, P), grid(rows[:, 3 * P:5 * P], 2, P)
        w1 = wX[:].rearrange("p (k l m) -> p k l m", k=2, l=CMP_LEN)
        keys_raw, keysT = grid(wX[:, 0:2048], 16, P), grid(wX[:, 2048:4096], 16, P)
        ple = grid(wX[:, 0:2048], TT, D)

        gain_in, consts_in, x_in, rows_blank, rows_in, w1_in, small_in, keys_in, p_in = map(sem, (
            "gain_in", "consts_in", "x_in", "rows_blank", "rows_in", "w1_in", "small_in", "keys_in", "p_in"))
        chunk_loaded = [sem(f"chunk_loaded{i}") for i in range(RING)]
        chunk_done = sem("chunk_done")
        pair_read = [sem("pair_read0"), sem("pair_read1")]
        cols_turned, cols_ready = sem("cols_turned"), sem("cols_ready")
        blank_ready = sem("blank_ready")
        h_ready, ss_ready, var_ready, std_ready = map(sem, ("h_ready", "ss_ready", "var_ready", "std_ready"))
        src_ready, turn_done, xT_ready = map(sem, ("src_ready", "turn_done", "xT_ready"))
        dve_chain, act_chain, pool_chain = map(sem, ("dve_chain", "act_chain", "pool_chain"))
        lb_in, lb_exp = sem("lb_in"), sem("lb_exp")
        sig_ready, copies_ready = sem("sig_ready"), sem("copies_ready")
        cl_forget, cl_log, cl_diff, cl_exp, cl_ready = map(sem, ("cl_forget", "cl_log", "cl_diff", "cl_exp", "cl_ready"))
        cl_a_done, cl_a_ready, cl_k2_turned, cl_k2_ready = map(sem, (
            "cl_a_done", "cl_a_ready", "cl_k2_turned", "cl_k2_ready"))
        cl_add_done, cl_state_ready, cl_o_done, cl_o_read = map(sem, (
            "cl_add_done", "cl_state_ready", "cl_o_done", "cl_o_read"))
        qk_ready, qk_turned, qk_read = map(sem, ("qk_ready", "qk_turned", "qk_read"))
        blk_ready, hid_done, hid_ready, kvc_done, kvc_ready = map(sem, (
            "blk_ready", "hid_done", "hid_ready", "kvc_done", "kvc_ready"))
        kcd_ready, kc_turned, kcT_ready, vb_done, vb_ready = map(sem, (
            "kcd_ready", "kc_turned", "kcT_ready", "vb_done", "vb_ready"))
        cs_done, cs_shift, cs_exp, pc_ready, pc_turned, pcT_ready, oc_done = map(sem, (
            "cs_done", "cs_shift", "cs_exp", "pc_ready", "pc_turned", "pcT_ready", "oc_done"))
        s_done, s_shift, s_exp, p_turned, pT_ready, pv_done, o_read = map(sem, (
            "s_done", "s_shift", "s_exp", "p_turned", "pT_ready", "pv_done", "o_read"))

        keys_turned, keysT_ready, sk_done, sk_read, ple_turned, pleT_ready = map(sem, (
            "keys_turned", "keysT_ready", "sk_done", "sk_read", "ple_turned", "pleT_ready"))
        best_shift, best_exp, idx_ready, dots_done, gelu_done, weights_ready = map(sem, (
            "best_shift", "best_exp", "idx_ready", "dots_done", "gelu_done", "weights_ready"))
        gathered = [sem(f"gathered{i}") for i in range(GATHER_SLOTS)]
        rows_used, slots_taken = sem("rows_used"), sem("slots_taken")
        sb_z, sb_l, sb_sp, sb_suf, sb_t, sb_w, sb_wm, sb_o, ret_s, ret_d, ret_o = map(sem, (
            "sb_z", "sb_l", "sb_sp", "sb_suf", "sb_t", "sb_w", "sb_wm", "sb_o", "ret_s", "ret_d", "ret_o"))
        conv_ready, conv_silu = map(sem, ("conv_ready", "conv_silu"))
        ple_sig, alpha_done, alpha_read, out_stored = map(sem, ("ple_sig", "alpha_done", "alpha_read", "out_stored"))

        weights = {}
        for name in ("w_in", "w_out", "peer_wq", "ple_gate_w", "even_w_in", "even_w_out", "odd_w_in", "odd_w_out"):
            src = a[name if name in a else name + "_2"]
            weights[name] = src[0].rearrange("(k p) n -> p k n", p=P)
        for layer in range(2):
            weights[f"up{layer}"] = a["ffn_w_up_2"][layer].rearrange("(k p) (u n) -> p k u n", p=P, u=2)
            weights[f"down{layer}"] = a["ffn_w_down_2"][layer].rearrange("(k p) n -> p k n", p=P)

        def chunk_width(name, c):
            return min(512, weights[name].shape[2] - 512 * c)

        def slot(i):
            return ring[:, i % RING, :]

        def product_slot(i):
            name, c = CHUNKS[i]
            n = chunk_width(name, c)
            return slot(i)[:, 0:KD * n].rearrange("p (k n) -> p k n", k=KD)

        def read_out(i, side=None):
            turn_, used = PLAN[i]
            if turn_ is None:
                turn_ = side
            return pair_read[turn_], used[turn_] + 1

        def after(name):
            return {"mix1": (x_in, 16), "peer": read_out(CHUNK_AT["w_out"] + 1), "ple": (h_ready, 1),
                    "mix2a": (h_ready, 2), "ffn2a": read_out(CHUNK_AT["even_w_out"] + 1),
                    "mix2b": read_out(CHUNK_AT["down0"] + FCH - 1, 1),
                    "ffn2b": read_out(CHUNK_AT["odd_w_out"] + 1),
                    "end": read_out(CHUNK_AT["down1"] + FCH - 1, 1)}[name]

        blockctx = ctx.enter_context(nc.Block())

        @blockctx.sync
        def _(sp):
            sp.dma_start(h[:], a["x"][0].rearrange("(t p) d -> p t d", p=P)).then_inc(x_in, 16)
            for i, (name, c) in enumerate(CHUNKS):
                if LEVEL[name] > UPTO:
                    break
                if i >= RING:
                    sp.wait_ge(chunk_done, i - RING + 1)
                if name == "ple_proj":
                    dst, src = slot(i)[:, 0:2048].rearrange("p (k n) -> p k n", k=2), a["ple_proj"][0].rearrange("(k p) n -> p k n", p=P)
                    sp.dma_start(dst, src).then_inc(chunk_loaded[i % RING], 16)
                elif name.startswith("up"):
                    dst = slot(i).rearrange("p (u k n) -> p u k n", u=2, k=KD)
                    if True:
                        sp.dma_start(dst, weights[name][:, :, :, 256 * c:256 * c + 256].rearrange("p k u n -> p u k n")).then_inc(chunk_loaded[i % RING], 16)
                elif name.startswith("down"):
                    dst = slot(i)[:, 0:2048].rearrange("p (k n) -> p k n", k=2)
                    sp.dma_start(dst, weights[name][:, 2 * c:2 * c + 2, :]).then_inc(chunk_loaded[i % RING], 16)
                else:
                    n = chunk_width(name, c)
                    sp.dma_start(product_slot(i), weights[name][:, :, 512 * c:512 * c + n]).then_inc(chunk_loaded[i % RING], 16)
            sp.wait_ge(*after(END))
            sp.dma_start(out[0].rearrange("(t p) d -> p t d", p=P), h[:]).then_inc(out_stored, 16)
            sp.wait_ge(out_stored, 16)

        @blockctx.tensor
        def _(pe):
            mm = nc.tensor.matmul

            def turn(name):
                n = TURNS.index(name)
                src = mixed if name.startswith("out") else hn
                pe.wait_ge(src_ready, n + 1)
                for b in range(4):
                    for k in (2 * b, 2 * b + 1):
                        for tt in range(TT):
                            last = nc.tensor.transpose(ps[:, 4 + b, (k % 2) * T + tt * P:(k % 2) * T + (tt + 1) * P],
                                                       src[:, tt, k * P:(k + 1) * P], ident)
                    last.then_inc(turn_done, 1)
                pe.wait_ge(xT_ready, 4 * (n + 1))

            def begin(i):
                turn_, used = PLAN[i]
                pe.wait_ge(chunk_loaded[i % RING], 16 * (i // RING + 1))
                for side in (0, 1):
                    if turn_ in (None, side) and used[side]:
                        pe.wait_ge(pair_read[side], used[side])

            def by_tokens(i, lo, n, col0):
                w = product_slot(i)
                for tt in range(TT):
                    o = psf[:, 1024 * PLAN[i][0] + 512 * tt + col0:][:, 0:n]
                    for k in range(KD):
                        last = mm(o, xT[:, k, tt * P:(tt + 1) * P], w[:, k, lo:lo + n], start=(k == 0), stop=(k == KD - 1))
                return last

            def by_features(i, tiles, m=P):
                w = product_slot(i)
                for j in range(tiles):
                    o = psf[0:m, 1024 * PLAN[i][0] + T * j:][:, 0:T]
                    for k in range(KD):
                        last = mm(o, w[:, k, j * P:j * P + m], xT[:, k, :], start=(k == 0), stop=(k == KD - 1))
                return last

            def chunked_linear(n, dv, q1, k1, q2, k2, value, add_banks, o_banks):
                pe.wait_ge(cl_ready, n + 1)
                for hd in range(HH):
                    for tt in range(TT):
                        for cc in range(2):
                            at = slice(tt * P + cc * CH, tt * P + cc * CH + CH)
                            last = mm(ps[CH * cc:CH * cc + CH, 4, (hd * TT + tt) * CH:(hd * TT + tt + 1) * CH],
                                      k1[:, hd, at], q1[:, hd, at], start=True, stop=True, skip_group_check=True)
                last.then_inc(cl_a_done, 1)
                for tt in range(TT):
                    for hd in range(HH):
                        last = nc.tensor.transpose(ps[:, 5 + tt, hd * P:(hd + 1) * P], k2[:, hd, tt * P:(tt + 1) * P], ident)
                    last.then_inc(cl_k2_turned, 1)
                pe.wait_ge(cl_a_ready, n + 1)
                for c in range(NCH - 1):
                    tt, cc = c // 2, c % 2
                    pe.wait_ge(cl_k2_ready, 2 * n + tt + 1)
                    if c == 2:
                        pe.wait_ge(cl_state_ready, 3 * n + 1)
                    if c == 1:
                        pe.wait_ge(cl_k2_ready, 2 * n + 2)
                    for hd in range(HH):
                        o = psf[:, 512 * add_banks[c][hd * dv // 512] + hd * dv % 512:][:, 0:dv]
                        last = mm(o, k2tok[CH * cc:CH * cc + CH, tt, hd * DK:(hd + 1) * DK],
                                  value(tt, hd)[CH * cc:CH * cc + CH, :], start=True, stop=True)
                    last.then_inc(cl_add_done, 1)
                for tt in range(TT):
                    for hd in range(HH):
                        o = psf[:, 512 * o_banks[tt][hd * dv // 512] + hd * dv % 512:][:, 0:dv]
                        last = mm(o, aTm[:, hd * TT + tt, :], value(tt, hd), start=True, stop=False, skip_group_check=True)
                        for cc in range(2):
                            c = 2 * tt + cc
                            if c:
                                pe.wait_ge(cl_state_ready, 3 * n + c)
                                last = mm(o[CH * cc:CH * cc + CH, :], q2[:, hd, c * CH:(c + 1) * CH],
                                          state[:, c - 1, hd * dv:(hd + 1) * dv], start=False, stop=True, skip_group_check=True)
                    last.then_inc(cl_o_done, 1)

            def head_turns(n, src, count, bank0):
                for j in range(count):
                    for tt in range(TT):
                        last = nc.tensor.transpose(ps[:, bank0 + j // 2, (j % 2) * T + tt * P:(j % 2) * T + (tt + 1) * P],
                                                   src(j, tt), ident)
                    if j % 2:
                        last.then_inc(qk_turned, 1)

            pe.wait_ge(consts_in, 16)
            pe.wait_ge(rows_in, 16 * N_ROW_DMAS)
            nc.tensor.transpose(ps[:, 0, 0:G_ROWS], g_rows[0:G_ROWS, :], ident[0:G_ROWS, 0:G_ROWS])
            for layer in range(2):
                nc.tensor.transpose(ps[:, 0, 128 + 128 * layer:128 + 128 * layer + CW_ROWS],
                                    cw_rows[0:CW_ROWS, layer, :], ident[0:CW_ROWS, 0:CW_ROWS])
            for kind in range(2):
                last = nc.tensor.transpose(ps[:, 1, CMP_LEN * kind:CMP_LEN * (kind + 1)],
                                           pe_rows[0:CMP_LEN, kind, :], ident[0:CMP_LEN, 0:CMP_LEN])
            last.then_inc(cols_turned, 1)
            pe.wait_ge(cols_ready, 1)

            turn("mix1")
            i0 = CHUNK_AT["w_in"]
            for c in range(7):
                begin(i0 + c)
                if c < 2:
                    last = by_features(i0 + c, HH)
                elif c == 5:
                    by_features(i0 + c, 2)
                    w = product_slot(i0 + c)
                    for tt in range(TT):
                        o = psf[:, 1024 * PLAN[i0 + c][0] + 512 + T * tt:][:, 0:T]
                        for k in range(KD):
                            last = mm(o, xT[:, k, tt * P:(tt + 1) * P], w[:, k, T:2 * T], start=(k == 0), stop=(k == KD - 1))
                else:
                    last = by_tokens(i0 + c, 0, chunk_width("w_in", c), 0)
                last.then_inc(chunk_done, 1)
            for side in (0, 1):
                pe.wait_ge(pair_read[side], PLAN[i0 + 7][1][side])

            if UPTO >= 2:
                chunked_linear(0, HG_DV, grid(block(6), HH, T), grid(block(7), HH, T), grid(block(3), HH, T), grid(block(1), HH, T),
                               lambda tt, hd: tokens(HI + hd * HG_DV, HG_DV, tt), [[7], [0], [1]], [[2], [3]])

            if UPTO >= 3:
                kd = block(0).rearrange("p (t a g d) -> p t a g d", t=TT, a=2, g=NG)
                pe.wait_ge(qk_ready, 1)
                pe.wait_ge(cl_state_ready, 3)
                head_turns(0, lambda j, tt: tokens(NQ + j * P, P, tt) if j < 4 else kd[:, tt, (j - 4) // 2, (j - 4) % 2, :], 8, 4)
                pe.wait_ge(blk_ready, 1)
                pe.wait_ge(w1_in, 64)
                blkT = block(7)[:, 0:2 * CMP_LEN * NCMP].rearrange("p (k l n) -> p k l n", k=2, l=CMP_LEN)
                for kind in range(2):
                    for l in range(CMP_LEN):
                        for g in range(NG):
                            last = mm(ps[0:DH, g, SIDE[g] + kind * NCMP:][:, 0:NCMP],
                                      w1[DH * g:DH * g + DH, kind, l, :], blkT[DH * g:DH * g + DH, kind, l, :],
                                      start=(l == 0), stop=(l == CMP_LEN - 1))
                last.then_inc(hid_done, 1)
                pe.wait_ge(hid_ready, 1)
                pe.wait_ge(small_in, 32)
                for kind in range(2):
                    for g in range(NG):
                        last = mm(ps[0:NCMP, 1, (kind * NG + g) * DH:(kind * NG + g + 1) * DH], hid[:, kind * NG + g, :], w2[:, kind, :],
                                  start=True, stop=True)
                last.then_inc(kvc_done, 1)
                pe.wait_ge(kvc_ready, 1)
                mm(ps[0:NH * NCMP, 1, T:T + P], cview("sel")[0:NCMP, :], kvc[:, 2:4, :], start=True, stop=True).then_inc(vb_done, 1)
                pe.wait_ge(kcd_ready, 1)
                for g in range(NG):
                    last = nc.tensor.transpose(ps[:, 0, 256 + g * NCMP:256 + (g + 1) * NCMP], kcd[:, g, :, :], ident[0:NCMP, 0:NCMP])
                last.then_inc(kc_turned, 1)
                pe.wait_ge(kcT_ready, 1)
                pe.wait_ge(qk_read, 4)
                qT, kT = grid(block(2), 4, T), block(6).rearrange("p (a g t) -> p a g t", a=2, g=NG)

                def half(hd):
                    return slice(DH * (hd % 2), DH * (hd % 2) + DH)

                for tt in range(TT):
                    for hd in range(NH):
                        last = mm(ps[:, hd % 2, SIDE[hd % 2] + (tt * NH + hd) // 2 * NCMP:][:, 0:NCMP], qT[half(hd), hd // 2, tt * P:(tt + 1) * P],
                                  kcT[half(hd), hd // (NH // NG), :], start=True, stop=True)
                last.then_inc(cs_done, 1)

                def scores(u):
                    tt, hd = u // NH, u % NH
                    nk = (tt + 1) * P
                    if u >= 2:
                        pe.wait_ge(s_shift, u - 1)
                    for kind in range(2):
                        last = mm(ps[:, 4 + u % 2, kind * T:kind * T + nk], qT[half(hd), hd // 2, tt * P:(tt + 1) * P],
                                  kT[half(hd), kind, hd // (NH // NG), 0:nk], start=True, stop=True)
                    last.then_inc(s_done, 1)

                def weighted(u):
                    tt, hd = u // NH, u % NH
                    pe.wait_ge(s_exp, u + 1)
                    if u >= 2:
                        pe.wait_ge(pT_ready, u - 1)
                    for kind in range(2):
                        for kt in range(tt + 1):
                            last = nc.tensor.transpose(ps[:, 6 + u % 2, (kind * 2 + kt) * P:(kind * 2 + kt + 1) * P],
                                                       block(0)[:, (u % 2) * 512 + kind * T + kt * P:][:, 0:P], ident)
                    last.then_inc(p_turned, 1)
                    pe.wait_ge(pT_ready, u + 1)
                    if u == NH:
                        pe.wait_ge(o_read, 1)
                    for kind in range(2):
                        for kt in range(tt + 1):
                            last = mm(ps[:, kind, hd * DH:(hd + 1) * DH], block(3)[:, (u % 2) * 512 + (kind * 2 + kt) * P:][:, 0:P],
                                      tokens((NVS, NVW)[kind] + (hd // (NH // NG)) * DH, DH, kt), start=(kt == 0), stop=(kt == tt))
                    if hd == NH - 1:
                        last.then_inc(pv_done, 1)

                scores(0)
                scores(1)
                pe.wait_ge(pc_ready, 1)
                for tt in range(TT):
                    last = nc.tensor.transpose(ps[0:NH * NCMP, 1, tt * P:(tt + 1) * P], pc[:, tt, :], ident)
                last.then_inc(pc_turned, 1)
                pe.wait_ge(pcT_ready, 1)
                pe.wait_ge(vb_ready, 1)
                pe.wait_ge(cl_o_read, 1)
                for tt in range(TT):
                    last = mm(ps[:, 2 + tt, :], pcT[:, tt, :], vblock.rearrange("p h d -> p (h d)"), start=True, stop=True)
                last.then_inc(oc_done, 1)
                for u in range(TT * NH):
                    if u >= 1 and u + 1 < TT * NH:
                        scores(u + 1)
                    weighted(u)

            def plain_product(name, n, evac_all=True):
                i1 = CHUNK_AT[name]
                for c in range(n):
                    begin(i1 + c)
                    by_tokens(i1 + c, 0, 512, 0).then_inc(chunk_done, 1)

            if UPTO >= 4:
                turn("out1")
                pe.wait_ge(o_read, 2)
                plain_product("w_out", 2)
            if UPTO >= 5:
                pe.wait_ge(keys_in, 16)
                for hc in range(2 * PH):
                    last = nc.tensor.transpose(psf[:, 2048 + hc * P:2048 + (hc + 1) * P], keys_raw[:, hc, :], ident)
                last.then_inc(keys_turned, 1)
                pe.wait_ge(keysT_ready, 1)
                turn("peer")
                i1 = CHUNK_AT["peer_wq"]
                for c in range(4):
                    begin(i1 + c)
                    by_features(i1 + c, 4).then_inc(chunk_done, 1)
                qT_ = grid(proj[:, 0:4096], 2 * PH, T)
                for side in (0, 1):
                    pe.wait_ge(pair_read[side], PLAN[i1 + 4][1][side])
                for tt in range(TT):
                    if tt:
                        pe.wait_ge(sk_read, tt)
                    for hc in range(2 * PH):
                        last = mm(psf[:, 2048 + hc * P:2048 + (hc + 1) * P], qT_[:, hc, tt * P:(tt + 1) * P], keysT[:, hc, :], start=True, stop=True)
                    last.then_inc(sk_done, 1)
                pe.wait_ge(p_in, 16)
                i1 = CHUNK_AT["ple_proj"]
                begin(i1)
                for tt in range(TT):
                    for k in range(2):
                        last = nc.tensor.transpose(ps[:, 0, k * T + tt * P:k * T + (tt + 1) * P], p_raw[:, tt, k * P:(k + 1) * P], ident)
                last.then_inc(ple_turned, 1)
                pe.wait_ge(pleT_ready, 1)
                w = slot(i1)[:, 0:2048].rearrange("p (k n) -> p k n", k=2)
                for tt in range(TT):
                    for half_ in range(2):
                        for k in range(2):
                            last = mm(ps[:, 2 * tt + half_, :], pT[:, k, tt * P:(tt + 1) * P], w[:, k, 512 * half_:512 * half_ + 512],
                                      start=(k == 0), stop=(k == 1))
                last.then_inc(chunk_done, 1)
            if UPTO >= 6:
                turn("ple")
                plain_product("ple_gate_w", 2)
            if UPTO >= 7:
                turn("mix2a")
                i1 = CHUNK_AT["even_w_in"]
                for c in range(7):
                    begin(i1 + c)
                    by_tokens(i1 + c, 0, 512, 0).then_inc(chunk_done, 1)
                pe.wait_ge(qk_ready, 2)
                head_turns(1, lambda j, tt: tokens(j * P, P, tt), 8, 4)
                pe.wait_ge(qk_ready, 3)
                for side in (0, 1):
                    pe.wait_ge(pair_read[side], PLAN[i1 + 7][1][side])
                rot = block(4, 2).rearrange("p (t n) -> p t n", t=TT)
                head_turns(2, lambda j, tt: rot[:, tt, j * P:(j + 1) * P], 8, 0)
                sqT, skT = grid(block(0), 4, T), grid(block(1), 4, T)
                rT = grid(block(2, 2), 8, T)

                def sticks(u):
                    at = slice(DH * (u % 2), DH * (u % 2) + DH)
                    mm(ps[:, 4 + u % 2, 0:T], skT[at, u // 2, 0:P], sqT[at, u // 2, :], start=True, stop=True)
                    mm(ps[:, 4 + u % 2, T:T + P], skT[at, u // 2, P:T], sqT[at, u // 2, P:T], start=True, stop=True).then_inc(sb_z, 1)

                pe.wait_ge(qk_read, 8)
                sticks(0)
                sticks(1)
                for i in range(NH + 2):
                    if i < NH:
                        pe.wait_ge(sb_sp, i + 1)
                        if i >= 2:
                            pe.wait_ge(sb_t, i - 1)
                        sp_ = block(6 + i % 2)[:, 0:T + P]
                        o = ps[:, 6 + i % 2, :]
                        mm(o[:, 0:P], cview("negstrict"), sp_[:, 0:P], start=True, stop=True)
                        mm(o[:, P:T], cview("negstrict"), sp_[:, P:T], start=True, stop=False)
                        mm(o[:, P:T], cview("negones"), sp_[:, T:T + P], start=False, stop=True)
                        mm(o[:, T:T + P], cview("negstrict"), sp_[:, T:T + P], start=True, stop=True).then_inc(sb_suf, 1)
                    if i + 2 < NH:
                        sticks(i + 2)
                    if i >= 2:
                        u = i - 2
                        pe.wait_ge(sb_wm, u + 1)
                        if u == 0:
                            pe.wait_ge(qk_read, 12)
                        w_ = block(6 + u % 2)[:, T + P:2 * (T + P)]
                        v_ = [tokens(1024 + u * DH, DH, tt) for tt in range(TT)]
                        mm(ps[:, 0, u * DH:(u + 1) * DH], w_[:, 0:P], v_[0], start=True, stop=True)
                        mm(ps[:, 1, u * DH:(u + 1) * DH], w_[:, P:T], v_[0], start=True, stop=False)
                        mm(ps[:, 1, u * DH:(u + 1) * DH], w_[:, T:T + P], v_[1], start=False, stop=True).then_inc(sb_o, 1)
                for i in range(HH + 1):
                    if i < HH:
                        if i >= 2:
                            pe.wait_ge(ret_d, i - 1)
                        mm(ps[:, 2 + i % 2, 0:T], rT[:, 4 + i, 0:P], rT[:, i, :], start=True, stop=True)
                        mm(ps[:, 2 + i % 2, T:T + P], rT[:, 4 + i, P:T], rT[:, i, P:T], start=True, stop=True).then_inc(ret_s, 1)
                    if i >= 1:
                        u = i - 1
                        pe.wait_ge(ret_d, u + 1)
                        d_ = block(u % 2)[:, 0:T + P]
                        v_ = [tokens(2560 + u * DK, DK, tt) for tt in range(TT)]
                        mm(ps[:, 4, u * DK:(u + 1) * DK], d_[:, 0:P], v_[0], start=True, stop=True)
                        mm(ps[:, 5, u * DK:(u + 1) * DK], d_[:, P:T], v_[0], start=True, stop=False)
                        mm(ps[:, 5, u * DK:(u + 1) * DK], d_[:, T:T + P], v_[1], start=False, stop=True).then_inc(ret_o, 1)
                turn("out2")
                plain_product("even_w_out", 2)

            def conv_ffn(layer):
                turn("ffn2" + "ab"[layer])
                i1 = CHUNK_AT[f"up{layer}"]
                for c in range(FCH):
                    begin(i1 + c)
                    w = slot(i1 + c).rearrange("p (u k n) -> p u k n", u=2, k=KD)
                    for u in range(2):
                        for f in range(2):
                            o = psf[:, 1024 * PLAN[i1 + c][0] + 512 * u + T * f:][:, 0:T]
                            for k in range(KD):
                                last = mm(o, w[:, u, k, f * P:(f + 1) * P], xT[:, k, :], start=(k == 0), stop=(k == KD - 1))
                    last.then_inc(chunk_done, 1)
                i1 = CHUNK_AT[f"down{layer}"]
                gT = grid(proj[:, 0:FT * T], FT, T)
                for c in range(FCH):
                    begin(i1 + c)
                    pe.wait_ge(*read_out(CHUNK_AT[f"up{layer}"] + c))
                    w = slot(i1 + c)[:, 0:2048].rearrange("p (k n) -> p k n", k=2)
                    for tt in range(TT):
                        for half_ in range(2):
                            for k in range(2):
                                last = mm(ps[:, 2 * tt + half_, :], gT[:, 2 * c + k, tt * P:(tt + 1) * P], w[:, k, 512 * half_:512 * half_ + 512],
                                          start=(c == 0 and k == 0), stop=(c == FCH - 1 and k == 1), skip_group_check=True)
                    last.then_inc(chunk_done, 1)

            if UPTO >= 8:
                conv_ffn(0)
            if UPTO >= 9:
                turn("mix2b")
                i1 = CHUNK_AT["odd_w_in"]
                for c in range(7):
                    begin(i1 + c)
                    if c < 2:
                        last = by_features(i1 + c, HH)
                    elif c == 6:
                        last = by_features(i1 + c, 1, 16)
                    else:
                        last = by_tokens(i1 + c, 0, 512, 0)
                    last.then_inc(chunk_done, 1)
                for side in (0, 1):
                    pe.wait_ge(pair_read[side], PLAN[i1 + 7][1][side])
                pe.wait_ge(small_in, 32)
                for hd in range(HH):
                    last = mm(psf[:, 4 * 512 + T * hd:][:, 0:T], walpha[:, hd * DK:(hd + 1) * DK], gaT[:], start=True, stop=True)
                last.then_inc(alpha_done, 1)
                pe.wait_ge(alpha_read, 1)
                chunked_linear(1, GLA_DV, grid(block(3), HH, T), grid(block(7), HH, T), grid(block(3), HH, T), grid(block(1), HH, T),
                               lambda tt, hd: tokens(1024 + hd * GLA_DV, GLA_DV, tt),
                               [[4, 7], [5, 6], [4, 7]], [[0, 1], [2, 3]])
                turn("out3")
                pe.wait_ge(cl_o_read, 2)
                plain_product("odd_w_out", 2)
            if UPTO >= 10:
                conv_ffn(1)

        @blockctx.scalar
        def _(act):
            do = nc.scalar.activation

            def squares(name):
                n = NORMS.index(name)
                act.wait_ge(*after(name))
                for tt in range(TT):
                    last = do(hn[:, tt, :], h[:, tt, :], ACT.Square, accum_out=ss[:, 2 * n + tt:2 * n + tt + 1])
                last.then_inc(ss_ready, 1)

            def root(name, w, p=P):
                k = ROOTS.index(name)
                act.wait_ge(var_ready, k + 1)
                do(std[0:p, k, 0:w], var[0:p, k, 0:w], ACT.Sqrt).then_inc(std_ready, 1)

            def turn(name):
                n, g = TURNS.index(name), TURN_GAIN[name]
                for b in (2, 3):
                    act.wait_ge(turn_done, 4 * n + b + 1)
                    for k in (2 * b, 2 * b + 1):
                        col = G_ONE if g is None else g + k
                        last = do(xT[:, k, :], ps[:, 4 + b, (k % 2) * T:(k % 2 + 1) * T], ACT.Copy, scale=gcol[:, col:col + 1])
                    last.then_inc(xT_ready, 1)

            def chunk(i):
                act.wait_ge(chunk_done, i + 1)
                return pair(PLAN[i][0]).rearrange("p (t n) -> p t n", t=TT)

            def copy_tokens(i, col, n=512):
                src = chunk(i)
                do(tokens(col, n), src[:, :, 0:n], ACT.Copy).then_inc(pair_read[PLAN[i][0]], 1)

            def decays(n):
                act.wait_ge(cl_diff, 2 * n + 1)
                if n == 0:
                    do(block(6), block(5), ACT.Exp)
                    do(block(7), block(5), ACT.Exp, scale=-1.0)
                else:
                    do(block(7), block(4), ACT.Exp, scale=-1.0)
                do(block(3), block(4), ACT.Exp)
                do(dec[:, n, :], grid(block(4), HH * NCH, CH)[:, :, CH - 1], ACT.Exp).then_inc(cl_exp, 1)

            def last_decay(n):
                act.wait_ge(cl_diff, 2 * n + 2)
                do(block(1), block(5), ACT.Exp).then_inc(cl_exp, 1)

            def keys_to_tokens(n):
                for tt in range(TT):
                    act.wait_ge(cl_k2_turned, 2 * n + tt + 1)
                    do(k2tok[:, tt, :], ps[:, 5 + tt, :], ACT.Copy).then_inc(cl_k2_ready, 1)

            squares("mix1")
            root("mix1", TT)
            turn("mix1")
            act.wait_ge(lb_in, 1)
            do(lbw[:, 1:3, :], lbw[:, 1:3, :], ACT.Exp).then_inc(lb_exp, 1)
            i0 = CHUNK_AT["w_in"]
            act.wait_ge(chunk_done, i0 + 1)
            do(block(0), pair(PLAN[i0][0]), ACT.Sigmoid).then_inc(sig_ready, 1)
            act.wait_ge(chunk_done, i0 + 2)
            do(block(1), pair(PLAN[i0 + 1][0]), ACT.Sigmoid).then_inc(sig_ready, 1)
            copy_tokens(i0 + 2, HI)
            act.wait_ge(cl_forget, 1)
            do(block(3), block(1), ACT.Ln).then_inc(cl_log, 1)
            decays(0)
            last_decay(0)
            src = chunk(i0 + 3)
            do(tokens(HGT, 512), src, ACT.Sigmoid).then_inc(sig_ready, 1)
            copy_tokens(i0 + 4, NQ)
            src = chunk(i0 + 5)
            do(hn[:, 0, 0:512], src[:, 0, :], ACT.Copy)
            do(tokens(NKS, T), src[:, 1, :].rearrange("p (t n) -> p t n", t=TT), ACT.Copy).then_inc(pair_read[PLAN[i0 + 5][0]], 1)
            src = chunk(i0 + 6)
            do(gates[:], src[:, :, T:T + 24], ACT.Sigmoid)
            do(tokens(NKW, T), src[:, :, 0:T], ACT.Copy).then_inc(pair_read[PLAN[i0 + 6][0]], 1)

            if UPTO >= 2:
                keys_to_tokens(0)
            if UPTO >= 3:
                root("nsa_qk", 24)
                root("hg", TT * HH)
                for b, g in enumerate((G_NQ, G_NQ, G_KS, G_KW)):
                    act.wait_ge(qk_turned, b + 1)
                    dst = block(2)[:, 512 * b:512 * b + 512] if b < 2 else block(6)[:, 512 * (b - 2):512 * (b - 1)]
                    do(dst, ps[:, 4 + b, :], ACT.Copy, scale=gcol[:, g:g + 1]).then_inc(qk_read, 1)
                act.wait_ge(hid_done, 1)
                for g in range(NG):
                    last = do(hid[:, g:4:NG, :], grid(ps[0:DH, g, SIDE[g]:SIDE[g] + 2 * NCMP], 2, NCMP), ACT.Gelu_apprx_tanh)
                last.then_inc(hid_ready, 1)
                root("kc", NG, NCMP)
                act.wait_ge(cs_shift, 1)
                do(pc, pc, ACT.Exp).then_inc(cs_exp, 1)

                def exps(u):
                    tt, hd = u // NH, u % NH
                    nk = (tt + 1) * P
                    act.wait_ge(s_shift, u + 1)
                    for kind in range(2):
                        e = block(0)[:, (u % 2) * 512 + kind * T:][:, 0:nk]
                        last = do(e, e, ACT.Exp, bias=nmx[:, u, kind:kind + 1], accum_out=sums[:, tt, kind, hd:hd + 1])
                    last.then_inc(s_exp, 1)

                exps(0)
                for u in range(TT * NH):
                    if u + 1 < TT * NH:
                        exps(u + 1)
                    nk = (u // NH + 1) * P
                    act.wait_ge(p_turned, u + 1)
                    do(block(3)[:, (u % 2) * 512:][:, 0:512].rearrange("p (a n) -> p a n", a=2)[:, :, 0:nk],
                       ps[:, 6 + u % 2, :].rearrange("p (a n) -> p a n", a=2)[:, :, 0:nk], ACT.Copy).then_inc(pT_ready, 1)
                root("nsa_o", TT * NH)
            if UPTO >= 4:
                turn("out1")
            if UPTO >= 5:
                act.wait_ge(keys_turned, 1)
                do(wX[:, 2048:4096], psf[:, 2048:4096], ACT.Copy).then_inc(keysT_ready, 1)
                squares("peer")
                root("peer", TT)
                turn("peer")
                i1 = CHUNK_AT["peer_wq"]
                for c in range(4):
                    act.wait_ge(chunk_done, i1 + c + 1)
                    do(proj[:, c * 1024:(c + 1) * 1024], pair(PLAN[i1 + c][0]), ACT.Copy).then_inc(pair_read[PLAN[i1 + c][0]], 1)
                for tt in range(TT):
                    act.wait_ge(best_shift, tt + 1)
                    do(gatew[:, tt, :], gatew[:, tt, :], ACT.Exp).then_inc(best_exp, 1)
                act.wait_ge(ple_turned, 1)
                do(pT.rearrange("p k t -> p (k t)"), ps[:, 0, :], ACT.Copy).then_inc(pleT_ready, 1)
                act.wait_ge(chunk_done, CHUNK_AT["ple_proj"] + 1)
                for side in (0, 1):
                    do(ple[:, side, :], pair(side), ACT.Copy).then_inc(pair_read[side], 1)
                for tt in range(TT):
                    act.wait_ge(rows_used, GATHER_SLOTS + PAIRS * (tt + 1))
                    do(dots[:, tt, :], dots[:, tt, :], ACT.Gelu_apprx_tanh).then_inc(gelu_done, 1)
            if UPTO >= 6:
                squares("ple")
                root("ple", TT)
                turn("ple")
                i1 = CHUNK_AT["ple_gate_w"]
                for c in range(2):
                    act.wait_ge(chunk_done, i1 + c + 1)
                    do(proj[:, c * 1024:(c + 1) * 1024], pair(PLAN[i1 + c][0]), ACT.Sigmoid).then_inc(pair_read[PLAN[i1 + c][0]], 1)
            if UPTO >= 7:
                squares("mix2a")
                root("mix2a", TT)
                turn("mix2a")
                i1 = CHUNK_AT["even_w_in"]
                for c in range(6):
                    copy_tokens(i1 + c, 512 * c)
                src = chunk(i1 + 6)
                do(tokens(3072, 512), src, ACT.Sigmoid).then_inc(sig_ready, 1)
                root("sbqk", 32)
                for b, g in enumerate((G_SBQ, G_SBQ, G_SBK, G_SBK)):
                    act.wait_ge(qk_turned, 4 + b + 1)
                    do(block(b // 2)[:, 512 * (b % 2):512 * (b % 2) + 512], ps[:, 4 + b, :], ACT.Copy,
                       scale=gcol[:, g:g + 1]).then_inc(qk_read, 1)
                for b in range(4):
                    act.wait_ge(qk_turned, 8 + b + 1)
                    do(block(2, 2)[:, 512 * b:512 * b + 512], ps[:, b, :], ACT.Copy).then_inc(qk_read, 1)
                W = T + P
                chain = 0
                for i in range(NH + 1):
                    if i < NH:
                        e = block(4 + i % 2)[:, 0:W]
                        act.wait_ge(sb_z, i + 1)
                        if i >= 2:
                            act.wait_ge(sb_sp, i - 1)
                        if i < 2:
                            act.wait_ge(qk_turned, 12)
                        do(e, ps[:, 4 + i % 2, 0:W], ACT.Abs).then_inc(act_chain, 1)
                        chain += 1
                        act.wait_ge(act_chain, chain)
                        do(e, e, ACT.Exp, scale=-1.0).then_inc(act_chain, 1)
                        chain += 1
                        act.wait_ge(act_chain, chain)
                        do(e, e, ACT.Ln, bias=1.0).then_inc(sb_l, 1)
                    if i >= 1:
                        u = i - 1
                        act.wait_ge(sb_t, u + 1)
                        if u >= 2:
                            act.wait_ge(sb_o, u - 1)
                        do(block(6 + u % 2)[:, W:2 * W], block(4 + u % 2)[:, W:2 * W], ACT.Exp).then_inc(sb_w, 1)
                root("ret", TT * HH)
                turn("out2")

            def conv_ffn(layer):
                name = "ffn2" + "ab"[layer]
                squares(name)
                root(name, TT)
                turn(name)
                for c in range(FCH):
                    act.wait_ge(conv_ready, layer * FCH + c + 1)
                    e = block(c % 2)[:, 0:512]
                    do(e, e, ACT.Silu).then_inc(conv_silu, 1)

            if UPTO >= 8:
                conv_ffn(0)
            if UPTO >= 9:
                squares("mix2b")
                root("mix2b", TT)
                turn("mix2b")
                i1 = CHUNK_AT["odd_w_in"]
                act.wait_ge(chunk_done, i1 + 1)
                do(block(0), pair(PLAN[i1][0]), ACT.Copy, scale=DK ** -0.5).then_inc(pair_read[PLAN[i1][0]], 1)
                act.wait_ge(chunk_done, i1 + 2)
                do(block(2), pair(PLAN[i1 + 1][0]), ACT.Copy).then_inc(pair_read[PLAN[i1 + 1][0]], 1)
                copy_tokens(i1 + 2, 1024)
                copy_tokens(i1 + 3, 1536)
                for c in (4, 5):
                    src = chunk(i1 + c)
                    do(tokens(512 * c, 512), src, ACT.Sigmoid).then_inc(sig_ready, 1)
                act.wait_ge(chunk_done, i1 + 7)
                do(gaT[:], pair(PLAN[i1 + 6][0])[0:16, 0:T], ACT.Copy).then_inc(pair_read[PLAN[i1 + 6][0]], 1)
                chain = 2 * NH
                act.wait_ge(cl_forget, 2)
                do(block(5), block(1), ACT.Abs).then_inc(act_chain, 1)
                chain += 1
                act.wait_ge(act_chain, chain)
                do(block(5), block(5), ACT.Exp, scale=-1.0).then_inc(act_chain, 1)
                chain += 1
                act.wait_ge(act_chain, chain)
                do(block(5), block(5), ACT.Ln, bias=1.0).then_inc(cl_log, 1)
                decays(1)
                last_decay(1)
                keys_to_tokens(1)
                root("gla", TT * HH)
                turn("out3")
            if UPTO >= 10:
                conv_ffn(1)

        @blockctx.vector
        def _(dve):
            v = nc.vector
            links = [0]

            def link(ins):
                links[0] += 1
                ins.then_inc(dve_chain, 1)
                dve.wait_ge(dve_chain, links[0])

            def rsqrt(name, src, w, p=P, width=None):
                k = ROOTS.index(name)
                v.tensor_scalar(var[0:p, k, 0:w], src, 1.0 / width, EPS, ALU.mult, ALU.add).then_inc(var_ready, 1)
                dve.wait_ge(std_ready, k + 1)
                link(v.reciprocal(rstd[0:p, k, 0:w], std[0:p, k, 0:w]))
                return rstd[0:p, k, 0:w]

            def norm(name, gain=None):
                n = NORMS.index(name)
                dve.wait_ge(ss_ready, n + 1)
                r = rsqrt(name, ss[:, 2 * n:2 * n + 2], TT, width=D)
                for tt in range(TT):
                    ins = v.tensor_scalar(hn[:, tt, :], h[:, tt, :], r[:, tt:tt + 1], None, ALU.mult)
                    if tt and gain is None:
                        ins.then_inc(src_ready, 1)
                    elif tt:
                        link(ins)
                if gain is not None:
                    dve.wait_ge(gain_in, 16)
                    v.tensor_tensor(hn[:], hn[:], gain.unsqueeze(1).broadcast_to((P, TT, D)), ALU.mult).then_inc(src_ready, 1)

            def turn(name):
                n, g = TURNS.index(name), TURN_GAIN[name]
                for b in (0, 1):
                    dve.wait_ge(turn_done, 4 * n + b + 1)
                    for k in (2 * b, 2 * b + 1):
                        col = G_ONE if g is None else g + k
                        ins = v.tensor_scalar(xT[:, k, :], ps[:, 4 + b, (k % 2) * T:(k % 2 + 1) * T], gcol[:, col:col + 1], None, ALU.mult)
                    ins.then_inc(xT_ready, 1)

            def residual(name, n=2):
                i1 = CHUNK_AT[name]
                for c in range(n):
                    dve.wait_ge(chunk_done, i1 + c + 1)
                    o = h[:, :, 512 * c:512 * (c + 1)]
                    v.tensor_tensor(o, o, pair(PLAN[i1 + c][0]).rearrange("p (t n) -> p t n", t=TT), ALU.add)\
                        .then_inc(pair_read[PLAN[i1 + c][0]], 1)

            def over(ap, shape):
                return ap.unsqueeze(len(shape) - 1).broadcast_to(shape)

            def chunk_decays(n):
                dve.wait_ge(cl_log, n + 1)
                if n == 0:
                    link(v.tensor_tensor_scan(block(4), reset[:], block(3), 0.0, ALU.mult, ALU.add))
                    cum = grid(block(4), HH * NCH, CH)
                    mid = cum[:, :, CH // 2 - 1:CH // 2].broadcast_to((P, HH * NCH, CH))
                    v.tensor_tensor(grid(block(5), HH * NCH, CH), cum, mid, ALU.subtract).then_inc(cl_diff, 1)
                else:
                    v.tensor_tensor_scan(block(4), reset[:], block(3), 0.0, ALU.mult, ALU.add).then_inc(cl_diff, 1)
                    cum = grid(block(4), HH * NCH, CH)
                dve.wait_ge(cl_exp, 2 * n + 1)
                end = cum[:, :, CH - 1:CH].broadcast_to((P, HH * NCH, CH))
                v.tensor_tensor(grid(block(5), HH * NCH, CH), end, cum, ALU.subtract).then_inc(cl_diff, 1)
                if n == 0:
                    v.tensor_tensor(block(6), block(6), block(0), ALU.mult)
                v.tensor_tensor(block(7), block(7), block(2), ALU.mult)
                v.tensor_tensor(block(3), block(3), block(0), ALU.mult)
                dve.wait_ge(cl_exp, 2 * n + 2)
                v.tensor_tensor(block(1), block(1), block(2), ALU.mult).then_inc(cl_ready, 1)

            def chunk_states(n, dv, add_banks):
                dve.wait_ge(cl_a_done, n + 1)
                for cc in range(2):
                    part = slice(CH * cc, CH * cc + CH)
                    mask = cview("causal").bitcast(I32)[part].unsqueeze(1).broadcast_to((CH, HH * TT, CH))
                    ins = v.copy_predicated(aTm[part, :, part], mask, grid(ps[part, 4, :], HH * TT, CH))
                ins.then_inc(cl_a_ready, 1)
                for c in range(NCH - 1):
                    dve.wait_ge(cl_add_done, 3 * n + c + 1)
                    for hd in range(HH):
                        new = psf[:, 512 * add_banks[c][hd * dv // 512] + hd * dv % 512:][:, 0:dv]
                        o = state[:, c, hd * dv:(hd + 1) * dv]
                        if c == 0:
                            ins = v.tensor_copy(o, new)
                        else:
                            ins = v.scalar_tensor_tensor(o, state[:, c - 1, hd * dv:(hd + 1) * dv], dec[:, n, hd * NCH + c:hd * NCH + c + 1],
                                                         new, ALU.mult, ALU.add)
                    ins.then_inc(cl_state_ready, 1)
                    dve.wait_ge(cl_state_ready, 3 * n + c + 1)

            def heads_rms(name, x, sq, n, w):
                link(v.tensor_tensor(sq, x, x, ALU.mult))
                k = ROOTS.index(name)
                link(v.tensor_reduce(std[:, k, 0:n], grid(sq, n, w), X, ALU.add))
                return rsqrt(name, std[:, k, 0:n], n, width=w)

            v.memset(aTm[:], 0.0)
            link(v.memset(reset[:], 1.0))
            v.memset(grid(reset[:], HH * NCH, CH)[:, :, 0], 0.0)
            dve.wait_ge(cols_turned, 1)
            link(v.tensor_copy(gcol[:, 0:G_ROWS], ps[:, 0, 0:G_ROWS]))
            for col in (G_SBQ, G_NQ):
                v.tensor_scalar(gcol[:, col:col + 1], gcol[:, col:col + 1], DH ** -0.5, None, ALU.mult)
            v.tensor_copy(cw[:], grid(ps[:, 0, 128:384], 2, 128)[:, :, 0:CW_ROWS])
            v.tensor_copy(pe_col[:], grid(ps[:, 1, 0:2 * CMP_LEN], 2, CMP_LEN)).then_inc(cols_ready, 1)
            dve.wait_ge(cols_ready, 1)

            norm("mix1")
            l0, l1 = gcol[:, G_LB:G_LB + HH], gcol[:, G_LB + HH:G_LB + 2 * HH]
            link(v.tensor_tensor(lbw[:, 0, :], l0, l1, ALU.max))
            v.tensor_tensor(lbw[:, 1, :], l0, lbw[:, 0, :], ALU.subtract)
            v.tensor_tensor(lbw[:, 2, :], l1, lbw[:, 0, :], ALU.subtract).then_inc(lb_in, 1)
            turn("mix1")
            dve.wait_ge(lb_exp, 1)
            link(v.tensor_tensor(lbw[:, 3, :], lbw[:, 1, :], lbw[:, 2, :], ALU.add))
            link(v.reciprocal(lbw[:, 4, :], lbw[:, 3, :]))
            link(v.tensor_tensor(lbw[:, 0, :], lbw[:, 1, :], lbw[:, 4, :], ALU.mult))
            link(v.tensor_scalar(lbw[:, 5, :], lbw[:, 0, :], -1.0, 1.0, ALU.mult, ALU.add))

            i0 = CHUNK_AT["w_in"]
            dve.wait_ge(sig_ready, 1)
            v.scalar_tensor_tensor(block(0), pair(PLAN[i0][0]), DK ** -0.5, block(0), ALU.mult, ALU.mult).then_inc(pair_read[PLAN[i0][0]], 1)
            dve.wait_ge(sig_ready, 2)
            for hd in range(HH):
                f = grid(block(1), HH, T)[:, hd, :]
                ins = v.tensor_scalar(f, f, lbw[:, 5, hd:hd + 1], lbw[:, 0, hd:hd + 1], ALU.mult, ALU.add)
                if hd == 0:
                    ins.then_inc(pair_read[PLAN[i0 + 1][0]], 1)
            ins.then_inc(cl_forget, 1)
            dve.wait_ge(cl_forget, 1)
            v.tensor_scalar(block(2), block(1), -1.0, 1.0, ALU.mult, ALU.add)
            chunk_decays(0)
            dve.wait_ge(sig_ready, 3)
            gate = tokens(HGT, 512)
            src = pair(PLAN[i0 + 3][0]).rearrange("p (t n) -> p t n", t=TT)
            v.tensor_tensor(gate, src, gate, ALU.mult).then_inc(pair_read[PLAN[i0 + 3][0]], 1)

            if UPTO >= 2:
                chunk_states(0, HG_DV, [[7], [0], [1]])
            if UPTO >= 3:
                dve.wait_ge(*read_out(i0 + 6))
                dve.wait_ge(*read_out(i0 + 5))
                dve.wait_ge(*read_out(i0 + 4))
                k = ROOTS.index("nsa_qk")
                sq = block(4, 2)[:, 0:TT * 768].rearrange("p (t n) -> p t n", t=TT)
                for lo, n, at in ((NQ, 512, 0), (NKS, 128, 512), (NKW, 128, 640)):
                    ins = v.tensor_tensor(sq[:, :, at:at + n], tokens(lo, n), tokens(lo, n), ALU.mult)
                link(ins)
                link(v.tensor_reduce(std[:, k, 0:24], grid(block(4, 2)[:, 0:TT * 768], 24, DH), X, ALU.add))
                r = grid(rsqrt("nsa_qk", std[:, k, 0:24], 24, width=DH), TT, 12)
                for tt in range(TT):
                    q = grid(tokens(NQ, 512, tt), NH, DH)
                    v.tensor_tensor(q, q, over(r[:, tt, 0:8], (P, NH, DH)), ALU.mult)
                kd = block(0).rearrange("p (t a g e d) -> p t a g e d", t=TT, a=2, g=NG, e=2)
                for tt in range(TT):
                    for kind, lo in ((0, NKS), (1, NKW)):
                        for e in range(2):
                            ins = v.tensor_tensor(kd[:, tt, kind, :, e, :], grid(tokens(lo, 128, tt), NG, DH),
                                                  over(r[:, tt, 8 + 2 * kind:10 + 2 * kind], (P, NG, DH)), ALU.mult)
                ins.then_inc(qk_ready, 1)
                blkT = block(7)[:, 0:2 * CMP_LEN * NCMP].rearrange("p (k l n) -> p k l n", k=2, l=CMP_LEN)
                for kind in range(2):
                    xv = hn[:, 0, kind * T:(kind + 1) * T].rearrange("p (n l) -> p l n", l=CMP_STRIDE)
                    for half_ in range(2):
                        ls = slice(half_ * CMP_STRIDE, (half_ + 1) * CMP_STRIDE)
                        ins = v.tensor_tensor(blkT[:, kind, ls, :], xv[:, :, half_:half_ + NCMP],
                                              over(pe_col[:, kind, ls], (P, CMP_STRIDE, NCMP)), ALU.add)
                ins.then_inc(blk_ready, 1)
                dve.wait_ge(cl_o_done, 2)
                link(v.tensor_copy(block(4), psf[:, 1024:2048]))
                r = heads_rms("hg", block(4), block(5), TT * HH, HG_DV)
                o = grid(block(4), TT * HH, HG_DV)
                ins = v.tensor_tensor(o, o, over(r, (P, TT * HH, HG_DV)), ALU.mult)
                ins.then_inc(cl_o_read, 1)
                dve.wait_ge(cl_o_read, 1)
                v.tensor_tensor(mixed[:, :, 0:512], grid(block(4), TT, 512), tokens(HGT, 512), ALU.mult)
                dve.wait_ge(kvc_done, 1)
                v.tensor_copy(kvc[:].rearrange("n a d -> n (a d)"), ps[0:NCMP, 1, 0:4 * DH]).then_inc(kvc_ready, 1)
                dve.wait_ge(kvc_ready, 1)
                k = ROOTS.index("kc")
                link(v.tensor_tensor(kcd[:, :, 0, :], kvc[:, 0:2, :], kvc[:, 0:2, :], ALU.mult))
                link(v.tensor_reduce(std[0:NCMP, k, 0:NG], kcd[:, :, 0, :], X, ALU.add))
                r = rsqrt("kc", std[0:NCMP, k, 0:NG], NG, NCMP, DH)
                for e in range(2):
                    ins = v.tensor_tensor(kcd[:, :, e, :], kvc[:, 0:2, :], over(r, (NCMP, NG, DH)), ALU.mult)
                ins.then_inc(kcd_ready, 1)
                dve.wait_ge(vb_done, 1)
                for g in range(NG):
                    hs = slice(g * NH // NG, (g + 1) * NH // NG)
                    val = ps[0:NH * NCMP, 1, T + g * DH:T + (g + 1) * DH].unsqueeze(1).broadcast_to((NH * NCMP, NH // NG, DH))
                    ins = v.tensor_tensor(vblock[:, hs, :], val, over(cview("blk")[0:NH * NCMP, hs], (NH * NCMP, NH // NG, DH)), ALU.mult)
                ins.then_inc(vb_ready, 1)
                dve.wait_ge(kc_turned, 1)
                v.tensor_scalar(kcT[:].rearrange("p g n -> p (g n)"), ps[:, 0, 256:256 + NG * NCMP], gcol[:, G_KC:G_KC + 1], None, ALU.mult)\
                    .then_inc(kcT_ready, 1)
                dve.wait_ge(cs_done, 1)
                pcf = pc.rearrange("p t n -> p (t n)")
                pc3 = grid(pcf, TT * NH, NCMP)
                for side in range(2):
                    n = TT * NH * NCMP // 2
                    ins = v.tensor_tensor(pc3[:, side::2, :], grid(ps[:, side, SIDE[side]:SIDE[side] + n], TT * NH // 2, NCMP),
                                          grid(cview("cbias"), TT * NH, NCMP)[:, side::2, :], ALU.add)
                link(ins)
                link(v.tensor_reduce(cst8[:, 0, :], pc3, X, ALU.max))
                v.tensor_tensor(pc3, pc3, over(cst8[:, 0, :], (P, TT * NH, NCMP)), ALU.subtract).then_inc(cs_shift, 1)
                dve.wait_ge(cs_exp, 1)
                for tt in range(TT):
                    m = grid(cview("cmask"), TT, NCMP)[:, tt, :].unsqueeze(1).broadcast_to((P, NH, NCMP))
                    ins = v.tensor_tensor(grid(pc[:, tt, :], NH, NCMP), grid(pc[:, tt, :], NH, NCMP), m, ALU.mult)
                link(ins)
                link(v.tensor_reduce(cst8[:, 1, :], pc3, X, ALU.add))
                link(v.tensor_scalar(cst8[:, 1, :], cst8[:, 1, :], 1e-30, None, ALU.max))
                link(v.reciprocal(cst8[:, 2, :], cst8[:, 1, :]))
                v.tensor_tensor(pc3, pc3, over(cst8[:, 2, :], (P, TT * NH, NCMP)), ALU.mult).then_inc(pc_ready, 1)
                dve.wait_ge(pc_turned, 1)
                v.tensor_copy(pcT.rearrange("p t n -> p (t n)"), ps[0:NH * NCMP, 1, 0:T]).then_inc(pcT_ready, 1)

                def shift(u):
                    tt, hd = u // NH, u % NH
                    nk = (tt + 1) * P
                    dve.wait_ge(s_done, u + 1)
                    s_ = grid(block(0)[:, (u % 2) * 512:(u % 2 + 1) * 512], 2, T)[:, :, 0:nk]
                    d_ = grid(cview("dist"), TT, T)[:, tt, 0:nk].unsqueeze(1).broadcast_to((P, 2, nk))
                    link(v.scalar_tensor_tensor(s_, d_, -SLOPES[hd], grid(ps[:, 4 + u % 2, :], 2, T)[:, :, 0:nk], ALU.mult, ALU.add))
                    v.tensor_reduce(nmx[:, u, :], s_, X, ALU.max, negate=True).then_inc(s_shift, 1)

                def combine(tt):
                    dve.wait_ge(pv_done, tt + 1)
                    dve.wait_ge(oc_done, 1)
                    dve.wait_ge(s_exp, (tt + 1) * NH)
                    g3 = gates[:, tt, :].rearrange("p (h c) -> p c h", c=3)
                    link(v.tensor_scalar(sums[:, tt], sums[:, tt], 1e-30, None, ALU.max))
                    link(v.reciprocal(coef[:, tt, 0:2, :], sums[:, tt]))
                    link(v.tensor_tensor(coef[:, tt, 0:2, :], coef[:, tt, 0:2, :], g3[:, 1:3, :], ALU.mult))
                    o = grid(block(4)[:, 512 * tt:512 * tt + 512], NH, DH)
                    b = [grid(block(5)[:, 512 * kind:512 * kind + 512], NH, DH) for kind in range(2)]
                    shape = (P, NH, DH)
                    v.tensor_tensor(o, grid(ps[:, 2 + tt, :], NH, DH), over(g3[:, 0, :], shape), ALU.mult)
                    for kind in range(2):
                        ins = v.tensor_tensor(b[kind], grid(ps[:, kind, :], NH, DH), over(coef[:, tt, kind, :], shape), ALU.mult)
                    ins.then_inc(o_read, 1)
                    dve.wait_ge(o_read, tt + 1)
                    link(v.tensor_tensor(o, o, b[0], ALU.add))
                    link(v.tensor_tensor(o, o, b[1], ALU.add))

                for u in range(TT * NH):
                    shift(u)
                    if u % NH == 0 and u:
                        combine(u // NH - 1)
                combine(TT - 1)
                r = heads_rms("nsa_o", block(4), block(5), TT * NH, DH)
                for tt in range(TT):
                    ins = v.tensor_tensor(grid(mixed[:, tt, 512:1024], NH, DH), grid(block(4)[:, 512 * tt:512 * tt + 512], NH, DH),
                                          over(r[:, tt * NH:(tt + 1) * NH], (P, NH, DH)), ALU.mult)
                ins.then_inc(src_ready, 1)
            if UPTO >= 4:
                turn("out1")
                residual("w_out")
            if UPTO >= 5:
                norm("peer", gbc)
                turn("peer")
                small = k2tok[:].rearrange("p t n -> p (t n)")
                top_v, top_i, top_f = (grid(small[:, 256 * j:256 * j + 256], 2 * PH, TOPK) for j in range(3))
                best_v, best_i = (grid(small[:, 768 + 128 * j:896 + 128 * j], PH, TOPK) for j in range(2))
                st = state[:].rearrange("p c n -> p (c n)")
                onehot = st[:, 0:2048].rearrange("p (h k j) -> p h k j", h=PH, k=TOPK)
                ci = [st[:, 2048 + 128 * j:2176 + 128 * j] for j in range(6)]
                s_all = grid(proj[:, 4096:6144], 2 * PH, NK)
                rest = mixed[:].rearrange("p t n -> p (t n)")
                cand = xT[:].rearrange("p k t -> p (k t)")

                def best16(src, left, vals, idx, n, free=False):
                    for j in range(n):
                        ins = v.max(vals[:, j, 0:8], src[:, j, :])
                        if free and j < GATHER_SLOTS:
                            ins.then_inc(rows_used, 1)
                    link(ins)
                    for j in range(n):
                        v.max_index(idx[:, j, 0:8], vals[:, j, 0:8], src[:, j, :])
                        ins = v.match_replace(left[:, j, :], vals[:, j, 0:8], src[:, j, :], -3e38)
                    link(ins)
                    for j in range(n):
                        ins = v.max(vals[:, j, 8:16], left[:, j, :])
                    link(ins)
                    for j in range(n):
                        ins = v.max_index(idx[:, j, 8:16], vals[:, j, 8:16], left[:, j, :])
                    link(ins)

                def route(tt):
                    dve.wait_ge(sk_done, tt + 1)
                    v.tensor_copy(proj[:, 4096:6144], psf[:, 2048:4096]).then_inc(sk_read, 1)
                    dve.wait_ge(sk_read, tt + 1)
                    best16(s_all, grid(rest, 2 * PH, NK), top_v, top_i.bitcast(U32), 2 * PH, free=(tt == 0))
                    v.tensor_copy(top_f, top_i.bitcast(U32))
                    tv = top_v.rearrange("p (h c) k -> p h c k", c=2)
                    for hd in range(PH):
                        ins = v.tensor_tensor(grid(cand[:, 256 * hd:256 * (hd + 1)], TOPK, TOPK), over(tv[:, hd, 0, :], (P, TOPK, TOPK)),
                                              tv[:, hd, 1, :].unsqueeze(1).broadcast_to((P, TOPK, TOPK)), ALU.add)
                    link(ins)
                    best16(grid(cand, PH, 256), grid(rest, PH, 256), best_v, best_i.bitcast(U32), PH)
                    bi = small[:, 896:1024].bitcast(U32)
                    v.tensor_scalar(ci[0].bitcast(U32), bi, 4, None, ALU.logical_shift_right)
                    link(v.tensor_scalar(ci[1].bitcast(U32), bi, 15, None, ALU.bitwise_and))
                    v.tensor_copy(ci[2], ci[0].bitcast(U32))
                    link(v.tensor_copy(ci[3], ci[1].bitcast(U32)))
                    tf = top_f.rearrange("p (h c) k -> p h c k", c=2)
                    for side in range(2):
                        for hd in range(PH):
                            place = over(ci[2 + side][:, hd * TOPK:(hd + 1) * TOPK], (P, TOPK, TOPK))
                            ins = v.tensor_tensor(onehot[:, hd], cview("iota").unsqueeze(1).broadcast_to((P, TOPK, TOPK)), place, ALU.is_equal)
                        link(ins)
                        for hd in range(PH):
                            ins = v.tensor_tensor(onehot[:, hd], onehot[:, hd], tf[:, hd, side, :].unsqueeze(1).broadcast_to((P, TOPK, TOPK)), ALU.mult)
                        link(ins)
                        link(v.tensor_reduce(ci[4 + side], grid(st[:, 0:2048], PAIRS, TOPK), X, ALU.add))
                    link(v.scalar_tensor_tensor(ci[0], ci[4], float(NK), ci[5], ALU.mult, ALU.add))
                    v.tensor_copy(routes[:, tt, :], ci[0]).then_inc(idx_ready, 1)
                    v.tensor_tensor(grid(gatew[:, tt, :], PH, TOPK), best_v, best_v[:, :, 0:1].broadcast_to((P, PH, TOPK)), ALU.subtract)\
                        .then_inc(best_shift, 1)

                for tt in range(TT):
                    route(tt)
                dve.wait_ge(idx_ready, TT)
                for tt in range(TT):
                    dve.wait_ge(best_exp, tt + 1)
                    w_ = grid(gatew[:, tt, :], PH, TOPK)
                    link(v.tensor_reduce(ci[0][:, 0:PH], w_, X, ALU.add))
                    link(v.reciprocal(ci[1][:, 0:PH], ci[0][:, 0:PH]))
                    link(v.tensor_tensor(w_, w_, over(ci[1][:, 0:PH], (P, PH, TOPK)), ALU.mult))

                for side, tt in ((0, 0), (0, 1), (1, 0), (1, 1)):
                    base = PAIRS * (2 * side + tt)
                    acc = mixed[:, tt, :]
                    if side:
                        dve.wait_ge(gelu_done, tt + 1)
                        v.tensor_tensor(gatew[:, tt, :], gatew[:, tt, :], dots[:, tt, :], ALU.mult)
                        link(v.memset(acc, 0.0))
                    with dve.Fori(0, PAIRS // GBODY) as i:
                        for b in range(GBODY):
                            s_ = b % GATHER_SLOTS
                            row = arena[:, s_, :]
                            pair_ = bass.ds(i * GBODY + b, 1)
                            dve.wait_ge(gathered[s_], i * (16 * GBODY // GATHER_SLOTS) + 16 * (base // GATHER_SLOTS + b // GATHER_SLOTS + 1))
                            if side == 0:
                                v.scalar_tensor_tensor(row, row, 1.0, hn[:, tt, :], ALU.mult, ALU.mult, accum_out=dots[:, tt, pair_]).then_inc(rows_used, 1)
                            else:
                                dve.wait_ge(rows_used, i * GBODY + (GATHER_SLOTS + base + b))
                                v.scalar_tensor_tensor(acc, row, gatew[:, tt, pair_], acc, ALU.mult, ALU.add).then_inc(rows_used, 1)
                dve.wait_ge(rows_used, GATHER_SLOTS + 4 * PAIRS)
                v.tensor_tensor(h[:], h[:], mixed[:], ALU.add).then_inc(h_ready, 1)
            if UPTO >= 6:
                norm("ple")
                turn("ple")
                i1 = CHUNK_AT["ple_gate_w"]
                for c in range(2):
                    dve.wait_ge(*read_out(i1 + c))
                    g_ = grid(proj[:, c * 1024:(c + 1) * 1024], TT, 512)
                    link(v.tensor_tensor(g_, g_, ple[:, :, 512 * c:512 * (c + 1)], ALU.mult))
                    ins = v.tensor_tensor(h[:, :, 512 * c:512 * (c + 1)], h[:, :, 512 * c:512 * (c + 1)], g_, ALU.add)
                ins.then_inc(h_ready, 1)
            if UPTO >= 7:
                norm("mix2a")
                turn("mix2a")
                i1 = CHUNK_AT["even_w_in"]
                dve.wait_ge(*read_out(i1))
                dve.wait_ge(*read_out(i1 + 1))
                k = ROOTS.index("sbqk")
                for tt in range(TT):
                    ins = v.tensor_tensor(block(4 + tt), tokens(0, 1024, tt), tokens(0, 1024, tt), ALU.mult)
                link(ins)
                link(v.tensor_reduce(std[:, k, 0:32], grid(block(4, 2), 32, DH), X, ALU.add))
                r = rsqrt("sbqk", std[:, k, 0:32], 32, width=DH)
                for tt in range(TT):
                    q = grid(tokens(0, 1024, tt), 2 * NH, DH)
                    ins = v.tensor_tensor(q, q, over(r[:, tt * 16:(tt + 1) * 16], (P, 2 * NH, DH)), ALU.mult)
                ins.then_inc(qk_ready, 1)
                dve.wait_ge(*read_out(i1 + 3))
                dve.wait_ge(*read_out(i1 + 4))
                shape = (P, 2 * HH, 64)
                for tt in range(TT):
                    x_ = tokens(1536, 1024, tt).rearrange("p (h e d) -> p h e d", h=2 * HH, e=2)
                    o = block(4 + tt).rearrange("p (h e d) -> p h e d", h=2 * HH, e=2)
                    cos, sin = (grid(cview(n_), TT, 64)[:, tt, :].unsqueeze(1).broadcast_to(shape) for n_ in ("cos", "sin"))
                    t_ = block(6 + tt).rearrange("p (h e d) -> p h e d", h=2 * HH, e=2)
                    v.tensor_tensor(t_[:, :, 0, :], x_[:, :, 1, :], sin, ALU.mult)
                    v.tensor_tensor(t_[:, :, 1, :], x_[:, :, 0, :], sin, ALU.mult)
                    v.tensor_tensor(o[:, :, 0, :], x_[:, :, 0, :], cos, ALU.mult)
                    link(v.tensor_tensor(o[:, :, 1, :], x_[:, :, 1, :], cos, ALU.mult))
                    v.tensor_tensor(o[:, :, 0, :], o[:, :, 0, :], t_[:, :, 0, :], ALU.subtract)
                    ins = v.tensor_tensor(o[:, :, 1, :], o[:, :, 1, :], t_[:, :, 1, :], ALU.add)
                ins.then_inc(qk_ready, 1)
                dve.wait_ge(sig_ready, 4)
                gate = tokens(3072, 512)
                src = pair(PLAN[i1 + 6][0]).rearrange("p (t n) -> p t n", t=TT)
                v.tensor_tensor(gate, src, gate, ALU.mult).then_inc(pair_read[PLAN[i1 + 6][0]], 1)
                W = T + P

                def diagonal(ap):
                    return grid(ap, 3, P)[:, 0:3:2, :]

                strict = cview("sbmask").unsqueeze(1).broadcast_to((P, 2, P))
                for i in range(NH + 2):
                    if i < NH:
                        dve.wait_ge(sb_l, i + 1)
                        if i >= 2:
                            dve.wait_ge(sb_w, i - 1)
                        z, l = ps[:, 4 + i % 2, 0:W], block(4 + i % 2)[:, 0:W]
                        lb, sp_ = block(4 + i % 2)[:, W:2 * W], block(6 + i % 2)[:, 0:W]
                        v.scalar_tensor_tensor(lb, z, 0.0, l, ALU.min, ALU.subtract)
                        link(v.scalar_tensor_tensor(sp_, z, 0.0, l, ALU.max, ALU.add))
                        v.tensor_tensor(diagonal(sp_), diagonal(sp_), strict, ALU.mult).then_inc(sb_sp, 1)
                    if 1 <= i <= NH:
                        u = i - 1
                        dve.wait_ge(sb_suf, u + 1)
                        lb = block(4 + u % 2)[:, W:2 * W]
                        v.tensor_tensor(lb, lb, ps[:, 6 + u % 2, 0:W], ALU.add).then_inc(sb_t, 1)
                    if i >= 2:
                        u = i - 2
                        dve.wait_ge(sb_w, u + 1)
                        w_ = diagonal(block(6 + u % 2)[:, W:2 * W])
                        v.tensor_tensor(w_, w_, strict, ALU.mult).then_inc(sb_wm, 1)
                for i in range(HH):
                    dve.wait_ge(ret_s, i + 1)
                    if i >= 2:
                        dve.wait_ge(ret_o, i - 1)
                    if i < 2:
                        dve.wait_ge(sb_o, NH)
                    dc = grid(cview("decay"), HH, T)[:, i, :]
                    v.tensor_tensor(block(i % 2)[:, 0:T], ps[:, 2 + i % 2, 0:T], dc, ALU.mult)
                    v.tensor_tensor(block(i % 2)[:, T:W], ps[:, 2 + i % 2, T:W], dc[:, 0:P], ALU.mult).then_inc(ret_d, 1)
                v.tensor_copy(mixed[:, :, 0:512], grid(psf[:, 0:1024], TT, 512))
                dve.wait_ge(ret_o, HH)
                link(v.tensor_copy(block(4), psf[:, 2048:3072]))
                r = heads_rms("ret", block(4), block(5), TT * HH, DK)
                o = grid(block(4), TT * HH, DK)
                link(v.tensor_tensor(o, o, over(r, (P, TT * HH, DK)), ALU.mult))
                v.tensor_tensor(mixed[:, :, 512:1024], grid(block(4), TT, 512), gate, ALU.mult).then_inc(src_ready, 1)
                turn("out2")
                residual("even_w_out")

            def conv_ffn(layer):
                name = "ffn2" + "ab"[layer]
                norm(name)
                turn(name)
                i1 = CHUNK_AT[f"up{layer}"]
                gT = grid(proj[:, 0:FT * T], FT, T)
                for c in range(FCH):
                    dve.wait_ge(chunk_done, i1 + c + 1)
                    u_, v_ = (grid(pair(PLAN[i1 + c][0])[:, 512 * j:512 * j + 512], 2, T) for j in range(2))
                    e = grid(block(c % 2)[:, 0:512], 2, T)

                    def tap(j, f):
                        return cw[:, layer, j * FT + 2 * c + f:j * FT + 2 * c + f + 1]

                    for f in range(2):
                        ins = v.tensor_scalar(e[:, f, :], u_[:, f, :], tap(2, f), tap(3, f), ALU.mult, ALU.add)
                    link(ins)
                    for back in (1, 2):
                        for f in range(2):
                            ins = v.scalar_tensor_tensor(e[:, f, back:T], u_[:, f, 0:T - back], tap(2 - back, f), e[:, f, back:T], ALU.mult, ALU.add)
                        if back == 1:
                            link(ins)
                    ins.then_inc(conv_ready, 1)
                    dve.wait_ge(conv_silu, layer * FCH + c + 1)
                    v.tensor_tensor(gT[:, 2 * c:2 * c + 2, :], e, v_, ALU.mult).then_inc(pair_read[PLAN[i1 + c][0]], 1)
                i1 = CHUNK_AT[f"down{layer}"]
                dve.wait_ge(chunk_done, i1 + FCH)
                for tt in range(TT):
                    v.tensor_tensor(h[:, tt, :], h[:, tt, :], pair(tt), ALU.add).then_inc(pair_read[tt], 1)

            if UPTO >= 8:
                conv_ffn(0)
            if UPTO >= 9:
                norm("mix2b")
                turn("mix2b")
                i1 = CHUNK_AT["odd_w_in"]
                for c in (4, 5):
                    dve.wait_ge(sig_ready, 5 + c - 4)
                    g_ = tokens(512 * c, 512)
                    src = pair(PLAN[i1 + c][0]).rearrange("p (t n) -> p t n", t=TT)
                    v.tensor_tensor(g_, src, g_, ALU.mult).then_inc(pair_read[PLAN[i1 + c][0]], 1)
                dve.wait_ge(alpha_done, 1)
                for hd in range(HH):
                    ins = v.tensor_scalar(block(1)[:, hd * T:(hd + 1) * T], psf[:, 2048 + T * hd:2048 + T * (hd + 1)],
                                          gcol[:, G_BAL + hd:G_BAL + hd + 1], None, ALU.add)
                ins.then_inc(cl_forget, 1)
                dve.wait_ge(cl_forget, 2)
                v.tensor_scalar(block(6), block(1), 0.0, 1.0 / 16.0, ALU.min, ALU.mult).then_inc(alpha_read, 1)
                dve.wait_ge(alpha_read, 1)
                dve.wait_ge(cl_log, 2)
                link(v.scalar_tensor_tensor(block(3), block(5), -1.0 / 16.0, block(6), ALU.mult, ALU.add))
                chunk_decays(1)
                chunk_states(1, GLA_DV, [[4, 7], [5, 6], [4, 7]])
                dve.wait_ge(cl_o_done, 4)
                link(v.tensor_copy(block(4, 2), psf[:, 0:2048]))
                r = heads_rms("gla", block(4, 2), block(6, 2), TT * HH, GLA_DV)
                o = grid(block(4, 2), TT * HH, GLA_DV)
                v.tensor_tensor(o, o, over(r, (P, TT * HH, GLA_DV)), ALU.mult).then_inc(cl_o_read, 1)
                dve.wait_ge(cl_o_read, 2)
                v.tensor_tensor(mixed[:], grid(block(4, 2), TT, 1024), tokens(2048, 1024), ALU.mult).then_inc(src_ready, 1)
                turn("out3")
                residual("odd_w_out")
            if UPTO >= 10:
                conv_ffn(1)

        @blockctx.gpsimd
        def _(pool):
            pool.dma_start(cst[:], consts).then_inc(consts_in, 16)
            pool.memset(rows[:, 0:5 * P], 1.0).then_inc(rows_blank, 1)
            pool.wait_ge(rows_blank, 1)

            def to_rows(dst, src):
                pool.dma_start(dst, src).then_inc(rows_in, 16)

            n_rows = 0
            lines = [(G_MIX, 8, a["mix_norm"][0]), (G_OUT1, 4, a["hg_out_norm"][0]), (G_OUT1 + 4, 4, a["nsa_out_norm"][0]),
                     (G_PLE, 8, a["ple_gate_norm"][0]), (G_MIX2[0], 8, a["mix_norm_g_2"][0]), (G_MIX2[1], 8, a["mix_norm_g_2"][1]),
                     (G_FFN2[0], 8, a["ffn_norm_g_2"][0]), (G_FFN2[1], 8, a["ffn_norm_g_2"][1]),
                     (G_LB, 4, a["hg_lb_logits"][0]), (G_LB + 4, 4, a["hg_lb_logits"][1]), (G_BAL, 4, a["gla_b_alpha_2"][0])]
            lines += [(G_OUT2 + 4 + j, 1, a["ret_out_gain_2"][0]) for j in range(HH)]
            lines += [(G_OUT3 + 2 * j, 2, a["gla_out_gain_2"][0]) for j in range(HH)]
            for row, n, src in lines:
                to_rows(g_rows[row:row + n, :], src.rearrange("(r c) -> r c", c=P))
                n_rows += 1
            for row, src in ((G_SBQ, a["sb_q_gain_2"][0]), (G_SBK, a["sb_k_gain_2"][0]), (G_NQ, a["nsa_q_norm"][0]),
                             (G_KC, a["nsa_k_norm"][0, 0]), (G_KS, a["nsa_k_norm"][0, 1]), (G_KW, a["nsa_k_norm"][0, 2])):
                for half_ in range(2):
                    to_rows(g_rows[row:row + 1, DH * half_:DH * half_ + DH], src.rearrange("(r c) -> r c", r=1))
                    n_rows += 1
            for layer in range(2):
                to_rows(cw_rows[0:3 * FT, layer, :], a["ffn_conv_w_2"][layer].rearrange("j (f c) -> (j f) c", c=P))
                to_rows(cw_rows[3 * FT:4 * FT, layer, :], a["ffn_conv_b_2"][layer].rearrange("(f c) -> f c", c=P))
                n_rows += 2
            for kind in range(2):
                for half_ in range(2):
                    to_rows(pe_rows[0:CMP_LEN, kind, DH * half_:DH * half_ + DH], a["cmp_pe"][0, kind])
                    n_rows += 1
            assert n_rows == N_ROW_DMAS
            for half_ in range(2):
                for kind in range(2):
                    pool.dma_start(w1[DH * half_:DH * half_ + DH, kind], a["cmp_w1"][0, kind].rearrange("(l d) m -> d l m", d=DH)).then_inc(w1_in, 16)
            pool.dma_start(w2[:], a["cmp_w2"][0].rearrange("k d m -> d k m")).then_inc(small_in, 16)
            pool.dma_start(walpha[:], a["gla_w_alpha_2"][0]).then_inc(small_in, 16)
            if UPTO >= 5:
                pool.wait_ge(hid_done, 1)
                pool.dma_start(keys_raw, a["peer_keys"][0].rearrange("h c k d -> k (h c) d")).then_inc(keys_in, 16)
                pool.dma_start(gbc, a["ffn_norm"][0].partition_broadcast(P)).then_inc(gain_in, 16)
                pool.wait_ge(src_ready, 2)
                pool.dma_start(p_raw, a["p"][0, 0].rearrange("(t p) d -> p t d", p=P)).then_inc(p_in, 16)
                for side, tt in ((0, 0), (0, 1), (1, 0), (1, 1)):
                    table = a["peer_u" if side == 0 else "peer_v"][0]
                    base = PAIRS * (2 * side + tt)
                    if side == 0:
                        pool.wait_ge(idx_ready, tt + 1)
                    with pool.Fori(0, PAIRS // GBODY) as i:
                        for half_ in range(GBODY // TOPK):
                            pool.tensor_copy(stage[:, half_, :], routes[:, tt, bass.ds(i * GBODY + half_ * TOPK, TOPK)]).then_inc(pool_chain, 1)
                            pool.wait_ge(pool_chain, i * 2 + (2 * (PAIRS // GBODY) * (2 * side + tt) + half_ + 1))
                            for k in range(TOPK):
                                b = half_ * TOPK + k
                                pool.wait_ge(rows_used, i * GBODY + (base + b + 1))
                                pool.sem_inc(slots_taken, 1)
                                pool.indirect_dma_start(arena[:, b % GATHER_SLOTS, :], None, table,
                                                        bass.IndirectOffsetOnAxis(ap=stage[:, half_, k:k + 1], axis=0))\
                                    .then_inc(gathered[b % GATHER_SLOTS], 16)


def kernel(**inputs):
    import concourse.bacc as bacc
    from concourse.bass_utils import run_bass_kernel_spmd

    nc = bacc.Bacc("TRN2", target_bir_lowering=False, num_devices=1)
    arrays, aps = {}, {}
    for name, value in inputs.items():
        value = np.ascontiguousarray(value)
        arrays["in_" + name] = value
        aps[name] = nc.dram_tensor("in_" + name, value.shape, mybir.dt.from_np(value.dtype), kind="ExternalInput").ap()
    arrays["shape_constants"] = shape_constants()
    consts = nc.dram_tensor("shape_constants", (P, C_WIDTH), F32, kind="ExternalInput").ap()
    out = nc.dram_tensor("out", (1, T, D), F32, kind="ExternalOutput").ap()
    two_blocks(nc, aps, consts, out)
    r = run_bass_kernel_spmd(nc, [arrays], core_ids=[0])
    return r.results[0]["out"]
```

```python
from contextlib import ExitStack

import numpy as np

import concourse.bass as bass
from concourse import mybir

F32 = mybir.dt.float32
U32 = mybir.dt.uint32
F32R = mybir.dt.float32r
I32 = mybir.dt.int32
ALU = mybir.AluOpType
ACT = mybir.ActivationFunctionType
X = mybir.AxisListType.X

P = 128
T, D = 256, 1024
TT, KD = T // P, D // P
EPS = 1e-6
BIG = 1e30

CH = 64
NCH = T // CH
HH, DK = 4, 128
HG_DV, GLA_DV = 128, 256
NH, NG, DH = 8, 2, 64
CMP_LEN, CMP_STRIDE = 32, 16
NCMP = (T - CMP_LEN) // CMP_STRIDE + 1
PH, NK, TOPK = 8, 128, 16
PAIRS = PH * TOPK
HPAIR = 2
UNITS = PH // HPAIR * TT
UROWS = HPAIR * TOPK
GATHER_SLOTS = 8


def rows_before(side, u):
    if side == 0:
        return UROWS * max(2 * u - 1, 0)
    return UROWS * min(2 * u + 2, 2 * UNITS - 1)


DFF = 2816
FT = DFF // P
FCH = FT // 2
FHALF = 2048
FUNITS = 3 * FCH
HQ, HF, HI, HGT, NQ, NKC, NVC, NKS, NVS, NKW, NVW, NGATE, D_IN1 = (
    0, 512, 1024, 1536, 2048, 2560, 2688, 2816, 2944, 3072, 3200, 3328, 3352)
RING = 3

G_MIX, G_LB, FIRST_ROWS = 0, 8, 16
G_OUT1, G_PLE, G_MIX2, G_FFN2, G_OUT2, G_OUT3 = 16, 24, (32, 40), (48, 56), 64, 72
G_SBQ, G_SBK, G_NQ, G_KC, G_KS, G_KW, G_BAL, G_COLS = 80, 81, 82, 83, 84, 85, 86, 90
G_ROWS, G_ONE = G_COLS - FIRST_ROWS, G_OUT2
CW_ROWS = 4 * FT

C_COLS = {}
_at = 0
for _name, _n in (("ident", P), ("dist", TT * T), ("cbias", TT * NH * NCMP), ("cmask", TT * NCMP),
                  ("cos", TT * 64), ("sin", TT * 64), ("decay", HH * T), ("negstrict", P), ("negones", P),
                  ("sbmask", P), ("causal", CH), ("sel", NH * NCMP), ("blk", NH), ("iota", TOPK)):
    C_COLS[_name] = (_at, _at + _n)
    _at += _n
C_WIDTH = _at

SIDE = (0, 384)
SLOPES = [2.0 ** (-8.0 * (i + 1) / NH) for i in range(NH)]


def shape_constants():
    c = np.zeros((P, C_WIDTH), np.float32)

    def put(name, a):
        lo, hi = C_COLS[name]
        c[:a.shape[0], lo:hi] = a.reshape(a.shape[0], -1)

    p = np.arange(P)
    t = p[:, None] + P * np.arange(TT)[None, :]
    put("ident", np.eye(P))
    dist = (t[:, :, None] - np.arange(T)).astype(np.float64)
    put("dist", np.where(dist >= 0, dist, BIG))
    cend = np.arange(NCMP) * CMP_STRIDE + CMP_LEN - 1
    dc = (t[:, :, None] - cend).astype(np.float64)
    sl = np.asarray(SLOPES)[None, None, :, None]
    put("cbias", np.where(dc[:, :, None] >= 0, -sl * dc[:, :, None], -BIG * sl))
    put("cmask", (dc >= 0).astype(np.float32))
    inv = np.float32(10000.0) ** (-np.arange(64, dtype=np.float32) / np.float32(64))
    ang = (t[:, :, None].astype(np.float32) * inv).astype(np.float32)
    put("cos", np.cos(ang))
    put("sin", np.sin(ang))
    lg = np.log(1.0 - np.exp2(-5.0 - np.arange(HH)))
    d = np.arange(T)[None, :] - p[:, None]
    put("decay", np.where(d[:, None] >= 0, np.exp(lg[None, :, None] * np.maximum(d, 0)[:, None]), 0.0) * DK ** -0.5)
    put("negstrict", -(p[:, None] > p[None, :]).astype(np.float32))
    put("negones", -np.ones((P, P)))
    put("sbmask", (p[:, None] < p[None, :]).astype(np.float32))
    put("causal", ((p % CH)[:, None] <= np.arange(CH)[None, :]).astype(np.float32))
    hn = np.arange(NH * NCMP)
    put("sel", (np.arange(NCMP)[:, None] == (hn % NCMP)[None, :]).astype(np.float32))
    put("blk", ((hn // NCMP)[:, None] == np.arange(NH)[None, :]).astype(np.float32))
    put("iota", np.tile(np.arange(TOPK, dtype=np.float32), (P, 1)))
    return c


def weight_chunks():
    out = [("w_in", c) for c in range(7)] + [("w_out", c) for c in range(2)]
    out += [("peer_wq", c) for c in range(4)] + [("ple_proj", 0)] + [("ple_gate_w", c) for c in range(2)]
    out += [("even_w_in", c) for c in range(7)] + [("even_w_out", c) for c in range(2)]
    out += [("up0", c) for c in range(FCH)] + [("down0", c) for c in range(FCH)]
    out += [("odd_w_in", c) for c in (6, 0, 1, 2, 3, 4, 5)] + [("odd_w_out", c) for c in range(2)]
    out += [("up1", c) for c in range(FCH)] + [("down1", c) for c in range(FCH)]
    return out


CHUNKS = weight_chunks()
CHUNK_AT = {}
for _i, (_n, _c) in enumerate(CHUNKS):
    CHUNK_AT.setdefault(_n, _i)


def bank_plan():
    used, plan, turn = [0, 0], [], 0
    for name, c in CHUNKS:
        if name.startswith("down") or name == "ple_proj":
            plan.append((None, tuple(used)))
            if c == FCH - 1 or name == "ple_proj":
                used = [used[0] + 1, used[1] + 1]
        else:
            plan.append((turn, tuple(used)))
            used[turn] += 1
            turn = 1 - turn
    return plan


PLAN = bank_plan()

ROOTS = ["mix1", "nsa_qk", "hg", "kc", "nsa_o", "peer", "ple", "mix2a", "sbqk", "ret", "ffn2a", "mix2b", "gla", "ffn2b"]
TURNS = ["mix1", "out1", "peer", "ple", "mix2a", "out2", "ffn2a", "mix2b", "out3", "ffn2b"]
TURN_GAIN = {"mix1": G_MIX, "out1": G_OUT1, "peer": None, "ple": G_PLE, "mix2a": G_MIX2[0], "out2": G_OUT2,
             "ffn2a": G_FFN2[0], "mix2b": G_MIX2[1], "out3": G_OUT3, "ffn2b": G_FFN2[1]}
NORMS = ["mix1", "peer", "ple", "mix2a", "ffn2a", "mix2b", "ffn2b"]
N_ROW_DMAS = 24


def two_blocks(nc, a, consts, out):
    with ExitStack() as ctx:
        def sb(name, shape, dt=F32):
            return ctx.enter_context(nc.sbuf_tensor(name, shape, dt))

        def sem(name):
            return ctx.enter_context(nc.semaphore(name))

        h = sb("h", [P, TT, D])
        hn = sb("hn", [P, TT, D])
        xT = sb("xT", [P, KD, T])
        with ExitStack() as outside_ffn:
            mixed, proj, arena, k2tok, state, wX = (outside_ffn.enter_context(nc.sbuf_tensor(*t, F32)) for t in (
                ("mixed", [P, TT, D]),
                ("proj", [P, 7168]),
                ("arena", [P, 8, 1024]),
                ("k2tok", [P, TT, HH * DK]),
                ("state", [P, 3, HH * GLA_DV]),
                ("wX", [P, 4096])))
        w_hi = [sb(f"w_hi{j}", [P, FHALF], F32R) for j in range(2)]
        w_lo = [sb(f"w_lo{j}", [P, FHALF], F32R) for j in range(2)]
        x_hi, x_lo = (sb(n_, [P, KD, T], F32R) for n_ in ("x_hi", "x_lo"))
        g_hi, g_lo = (sb(n_, [P, FT, T], F32R) for n_ in ("g_hi", "g_lo"))
        conv = sb("conv", [P, 2, 2, T])
        sb("end_of_mixers", [P, 1024])
        ring = sb("ring", [P, RING, 4096])
        reset = sb("reset", [P, 1024])
        aTm = sb("aTm", [P, HH * TT, P])
        cst = sb("cst", [P, C_WIDTH])
        gcol = sb("gcol", [P, 96])
        cw = sb("cw", [P, 2, CW_ROWS])
        pe_col = sb("pe_col", [P, 2, CMP_LEN])
        w2 = sb("w2", [DH, 2, DH])
        walpha = sb("walpha", [16, 512])
        gaT = sb("gaT", [16, T])
        ss = sb("ss", [P, 2 * len(NORMS)])
        var = sb("var", [P, len(ROOTS), 32])
        std = sb("std", [P, len(ROOTS), 32])
        rstd = sb("rstd", [P, len(ROOTS), 32])
        lbw = sb("lbw", [P, 6, HH])
        dec = sb("dec", [P, 2, HH * NCH])
        hid = sb("hid", [DH, 4, NCMP])
        kvc = sb("kvc", [NCMP, 4, DH])
        kcd = sb("kcd", [NCMP, NG, 2, DH])
        kcT = sb("kcT", [P, NG, NCMP])
        cst8 = sb("cst8", [P, 3, TT * NH])
        nmx = sb("nmx", [P, TT * NH, 2])
        sums = sb("sums", [P, TT, 2, NH])
        coef = sb("coef", [P, TT, 3, NH])
        gates = sb("gates", [P, TT, 24])
        routes = sb("routes", [P, UNITS * UROWS], U32)
        stage = sb("stage", [P, 2, TOPK], U32)
        dots = sb("dots", [P, UNITS * UROWS])
        gatew = sb("gatew", [P, UNITS * UROWS])
        ps = ctx.enter_context(nc.psum_tensor("ps", [P, 8, 512], F32))

        psf = ps[:].rearrange("p b n -> p (b n)")
        ident = cst[:, slice(*C_COLS["ident"])]

        def cview(name):
            return cst[:, slice(*C_COLS[name])]

        def block(i, n=1):
            return arena[:, i:i + n, :].rearrange("p a n -> p (a n)")

        def grid(ap, b, c):
            return ap.rearrange("p (b c) -> p b c", b=b, c=c)

        def tokens(lo, n, tt=None):
            v = proj[:].rearrange("p (t n) -> p t n", t=TT)
            return v[:, :, lo:lo + n] if tt is None else v[:, tt, lo:lo + n]

        def pair(turn):
            return psf[:, turn * 1024:(turn + 1) * 1024]

        gbc = block(7)
        vblock = state[0:NH * NCMP, 0, 512:1024].rearrange("p (h d) -> p h d", h=NH)
        pc = state[:, 1, 512:512 + TT * NH * NCMP].rearrange("p (t n) -> p t n", t=TT)
        pcT = state[0:NH * NCMP, 2, 512:512 + TT * P].rearrange("p (t n) -> p t n", t=TT)
        p_raw, pT = grid(proj[:, 6144:6656], TT, T), grid(proj[:, 6656:7168], 2, T)
        rows = mixed[:].rearrange("p a n -> p (a n)")
        g_rows, cw_rows, pe_rows = rows[:, 0:P], grid(rows[:, P:3 * P], 2, P), grid(rows[:, 3 * P:5 * P], 2, P)
        first_rows = rows[0:FIRST_ROWS, 5 * P:6 * P]
        w1 = wX[:].rearrange("p (k l m) -> p k l m", k=2, l=CMP_LEN)
        keys_raw, keysT = grid(wX[:, 0:2048], 16, P), grid(wX[:, 2048:4096], 16, P)
        ple = grid(wX[:, 0:2048], TT, D)

        gain_in, ident_in, consts_in, first_in, rows_blank, rows_in, w1_in, small_in, keys_in, p_in = map(sem, (
            "gain_in", "ident_in", "consts_in", "first_in", "rows_blank", "rows_in", "w1_in", "small_in", "keys_in", "p_in"))
        x_in = [sem(f"x_in{tt}") for tt in range(TT)]
        chunk_loaded = [sem(f"chunk_loaded{i}") for i in range(RING)]
        chunk_done = sem("chunk_done")
        pair_read = [sem("pair_read0"), sem("pair_read1")]
        cols_turned, cols_ready = sem("cols_turned"), sem("cols_ready")
        h_ready, ss_ready, var_ready, std_ready = map(sem, ("h_ready", "ss_ready", "var_ready", "std_ready"))
        src_ready, turn_done, xT_ready = map(sem, ("src_ready", "turn_done", "xT_ready"))
        dve_chain, act_chain, pool_chain = map(sem, ("dve_chain", "act_chain", "pool_chain"))
        lb_in, lb_exp = sem("lb_in"), sem("lb_exp")
        sig_ready = sem("sig_ready")
        cl_forget, cl_log, cl_diff, cl_exp, cl_ready = map(sem, ("cl_forget", "cl_log", "cl_diff", "cl_exp", "cl_ready"))
        cl_a_done, cl_a_ready, cl_k2_turned, cl_k2_ready = map(sem, (
            "cl_a_done", "cl_a_ready", "cl_k2_turned", "cl_k2_ready"))
        cl_add_done, cl_state_ready, cl_o_done, cl_o_read = map(sem, (
            "cl_add_done", "cl_state_ready", "cl_o_done", "cl_o_read"))
        qk_ready, qk_turned, qk_read = map(sem, ("qk_ready", "qk_turned", "qk_read"))
        blk_ready, hid_done, hid_ready, kvc_done, kvc_ready = map(sem, (
            "blk_ready", "hid_done", "hid_ready", "kvc_done", "kvc_ready"))
        kcd_ready, kc_turned, kcT_ready, vb_done, vb_ready = map(sem, (
            "kcd_ready", "kc_turned", "kcT_ready", "vb_done", "vb_ready"))
        cs_done, cs_shift, cs_exp, pc_ready, pc_turned, pcT_ready, oc_done = map(sem, (
            "cs_done", "cs_shift", "cs_exp", "pc_ready", "pc_turned", "pcT_ready", "oc_done"))
        s_done, s_shift, s_exp, p_turned, pT_ready, pv_done, o_read = map(sem, (
            "s_done", "s_shift", "s_exp", "p_turned", "pT_ready", "pv_done", "o_read"))

        keys_turned, keysT_ready, sk_done, sk_read, ple_turned, pleT_ready = map(sem, (
            "keys_turned", "keysT_ready", "sk_done", "sk_read", "ple_turned", "pleT_ready"))
        best_exp, idx_ready, dots_done, gelu_done, weights_ready = map(sem, (
            "best_exp", "idx_ready", "dots_done", "gelu_done", "weights_ready"))
        gathered = [sem(f"gathered{i}") for i in range(GATHER_SLOTS)]
        rows_used, slots_taken, units_taken = sem("rows_used"), sem("slots_taken"), sem("units_taken")
        sb_z, sb_l, sb_sp, sb_suf, sb_t, sb_w, sb_wm, sb_o, ret_s, ret_d, ret_o = map(sem, (
            "sb_z", "sb_l", "sb_sp", "sb_suf", "sb_t", "sb_w", "sb_wm", "sb_o", "ret_s", "ret_d", "ret_o"))
        conv_ready, conv_silu, hidden_ready, x_lo_ready = map(sem, ("conv_ready", "conv_silu", "hidden_ready", "x_lo_ready"))
        hi_ready, lo_ready, lo2_ready, unit_done = map(sem, ("hi_ready", "lo_ready", "lo2_ready", "unit_done"))
        ple_sig, alpha_done, alpha_read, out_stored = map(sem, ("ple_sig", "alpha_done", "alpha_read", "out_stored"))

        weights = {}
        for name in ("w_in", "w_out", "peer_wq", "ple_gate_w", "even_w_in", "even_w_out", "odd_w_in", "odd_w_out"):
            src = a[name if name in a else name + "_2"]
            weights[name] = src[0].rearrange("(k p) n -> p k n", p=P)
        for layer in range(2):
            weights[f"up{layer}"] = a["ffn_w_up_2"][layer].rearrange("(k p) (u n) -> p k u n", p=P, u=2)
            weights[f"down{layer}"] = a["ffn_w_down_2"][layer].rearrange("(k p) n -> p k n", p=P)

        def unit_scores(u):
            return proj[:, 2048 + 512 * u:2048 + 512 * (u + 1)]

        def chunk_width(name, c):
            return min(512, weights[name].shape[2] - 512 * c)

        def slot(i):
            return ring[:, i % RING, :]

        def product_slot(i):
            name, c = CHUNKS[i]
            n = chunk_width(name, c)
            return slot(i)[:, 0:KD * n].rearrange("p (k n) -> p k n", k=KD)

        def unit_weights(j):
            layer, k = j // FUNITS, j % FUNITS
            if k < 2 * FCH:
                i, lo = CHUNK_AT[f"up{layer}"] + k // 2, FHALF * (k % 2)
            else:
                i, lo = CHUNK_AT[f"down{layer}"] + k - 2 * FCH, 0
            return i, slot(i)[:, lo:lo + FHALF]

        def read_out(i, side=None):
            turn_, used = PLAN[i]
            if turn_ is None:
                turn_ = side
            return pair_read[turn_], used[turn_] + 1

        def after(name):
            return {"peer": read_out(CHUNK_AT["w_out"] + 1), "ple": (h_ready, 1),
                    "mix2a": (h_ready, 2), "ffn2a": read_out(CHUNK_AT["even_w_out"] + 1),
                    "mix2b": read_out(CHUNK_AT["down0"] + FCH - 1, 1),
                    "ffn2b": read_out(CHUNK_AT["odd_w_out"] + 1),
                    "end": read_out(CHUNK_AT["down1"] + FCH - 1, 1)}[name]

        blockctx = ctx.enter_context(nc.Block())

        @blockctx.sync
        def _(sp):
            for tt in range(TT):
                sp.dma_start(h[:, tt, :], a["x"][0, tt * P:(tt + 1) * P, :]).then_inc(x_in[tt], 16)
            for i, (name, c) in enumerate(CHUNKS):
                if i >= RING:
                    sp.wait_ge(chunk_done, i - RING + 1)
                if name == "ple_proj":
                    dst, src = slot(i)[:, 0:2048].rearrange("p (k n) -> p k n", k=2), a["ple_proj"][0].rearrange("(k p) n -> p k n", p=P)
                    sp.dma_start(dst, src).then_inc(chunk_loaded[i % RING], 16)
                elif name.startswith("up"):
                    dst = slot(i).rearrange("p (u k n) -> p u k n", u=2, k=KD)
                    sp.dma_start(dst, weights[name][:, :, :, 256 * c:256 * c + 256].rearrange("p k u n -> p u k n")).then_inc(chunk_loaded[i % RING], 16)
                elif name.startswith("down"):
                    dst = slot(i)[:, 0:2048].rearrange("p (k n) -> p k n", k=2)
                    sp.dma_start(dst, weights[name][:, 2 * c:2 * c + 2, :]).then_inc(chunk_loaded[i % RING], 16)
                else:
                    n = chunk_width(name, c)
                    sp.dma_start(product_slot(i), weights[name][:, :, 512 * c:512 * c + n]).then_inc(chunk_loaded[i % RING], 16)
            sp.wait_ge(*after("end"))
            sp.dma_start(out[0].rearrange("(t p) d -> p t d", p=P), h[:]).then_inc(out_stored, 16)
            sp.wait_ge(out_stored, 16)

        @blockctx.tensor
        def _(pe):
            mm = nc.tensor.matmul

            def turn(name):
                n = TURNS.index(name)
                src = mixed if name.startswith("out") else hn
                pe.wait_ge(src_ready, n + 1)
                for b in range(4):
                    for k in (2 * b, 2 * b + 1):
                        for tt in range(TT):
                            last = nc.tensor.transpose(ps[:, 4 + b, (k % 2) * T + tt * P:(k % 2) * T + (tt + 1) * P],
                                                       src[:, tt, k * P:(k + 1) * P], ident)
                    last.then_inc(turn_done, 1)
                pe.wait_ge(xT_ready, 4 * (n + 1))

            def begin(i):
                turn_, used = PLAN[i]
                pe.wait_ge(chunk_loaded[i % RING], 16 * (i // RING + 1))
                for side in (0, 1):
                    if turn_ in (None, side) and used[side]:
                        pe.wait_ge(pair_read[side], used[side])

            def by_tokens(i, lo, n, col0):
                w = product_slot(i)
                for tt in range(TT):
                    o = psf[:, 1024 * PLAN[i][0] + 512 * tt + col0:][:, 0:n]
                    for k in range(KD):
                        last = mm(o, xT[:, k, tt * P:(tt + 1) * P], w[:, k, lo:lo + n], start=(k == 0), stop=(k == KD - 1))
                return last

            def by_features(i, tiles, m=P):
                w = product_slot(i)
                for j in range(tiles):
                    o = psf[0:m, 1024 * PLAN[i][0] + T * j:][:, 0:T]
                    for k in range(KD):
                        last = mm(o, w[:, k, j * P:j * P + m], xT[:, k, :], start=(k == 0), stop=(k == KD - 1))
                return last

            def chunked_linear(n, dv, q1, k1, q2, k2, value, add_banks, o_banks):
                pe.wait_ge(cl_ready, n + 1)
                for hd in range(HH):
                    for tt in range(TT):
                        for cc in range(2):
                            at = slice(tt * P + cc * CH, tt * P + cc * CH + CH)
                            last = mm(ps[CH * cc:CH * cc + CH, 4, (hd * TT + tt) * CH:(hd * TT + tt + 1) * CH],
                                      k1[:, hd, at], q1[:, hd, at], start=True, stop=True, skip_group_check=True)
                last.then_inc(cl_a_done, 1)
                for tt in range(TT):
                    for hd in range(HH):
                        last = nc.tensor.transpose(ps[:, 5 + tt, hd * P:(hd + 1) * P], k2[:, hd, tt * P:(tt + 1) * P], ident)
                    last.then_inc(cl_k2_turned, 1)
                pe.wait_ge(cl_a_ready, n + 1)
                for c in range(NCH - 1):
                    tt, cc = c // 2, c % 2
                    pe.wait_ge(cl_k2_ready, 2 * n + tt + 1)
                    if c == 2:
                        pe.wait_ge(cl_state_ready, 3 * n + 1)
                    if c == 1:
                        pe.wait_ge(cl_k2_ready, 2 * n + 2)
                    for hd in range(HH):
                        o = psf[:, 512 * add_banks[c][hd * dv // 512] + hd * dv % 512:][:, 0:dv]
                        last = mm(o, k2tok[CH * cc:CH * cc + CH, tt, hd * DK:(hd + 1) * DK],
                                  value(tt, hd)[CH * cc:CH * cc + CH, :], start=True, stop=True)
                    last.then_inc(cl_add_done, 1)
                for tt in range(TT):
                    for hd in range(HH):
                        o = psf[:, 512 * o_banks[tt][hd * dv // 512] + hd * dv % 512:][:, 0:dv]
                        last = mm(o, aTm[:, hd * TT + tt, :], value(tt, hd), start=True, stop=False, skip_group_check=True)
                        for cc in range(2):
                            c = 2 * tt + cc
                            if c:
                                pe.wait_ge(cl_state_ready, 3 * n + c)
                                last = mm(o[CH * cc:CH * cc + CH, :], q2[:, hd, c * CH:(c + 1) * CH],
                                          state[:, c - 1, hd * dv:(hd + 1) * dv], start=False, stop=True, skip_group_check=True)
                    last.then_inc(cl_o_done, 1)

            def head_turns(n, src, count, bank0):
                for j in range(count):
                    for tt in range(TT):
                        last = nc.tensor.transpose(ps[:, bank0 + j // 2, (j % 2) * T + tt * P:(j % 2) * T + (tt + 1) * P],
                                                   src(j, tt), ident)
                    if j % 2:
                        last.then_inc(qk_turned, 1)

            pe.wait_ge(ident_in, 16)
            pe.wait_ge(first_in, 32)
            nc.tensor.transpose(ps[:, 0, 0:FIRST_ROWS], first_rows, ident[0:FIRST_ROWS, 0:FIRST_ROWS]).then_inc(cols_turned, 1)
            pe.wait_ge(cols_ready, 1)

            turn("mix1")
            i0 = CHUNK_AT["w_in"]
            for c in range(7):
                begin(i0 + c)
                if c < 2:
                    last = by_features(i0 + c, HH)
                elif c == 5:
                    by_features(i0 + c, 2)
                    w = product_slot(i0 + c)
                    for tt in range(TT):
                        o = psf[:, 1024 * PLAN[i0 + c][0] + 512 + T * tt:][:, 0:T]
                        for k in range(KD):
                            last = mm(o, xT[:, k, tt * P:(tt + 1) * P], w[:, k, T:2 * T], start=(k == 0), stop=(k == KD - 1))
                else:
                    last = by_tokens(i0 + c, 0, chunk_width("w_in", c), 0)
                last.then_inc(chunk_done, 1)
                if c == 2:
                    pe.wait_ge(rows_in, 16 * N_ROW_DMAS)
                    nc.tensor.transpose(ps[:, 4, 0:G_ROWS], g_rows[0:G_ROWS, :], ident[0:G_ROWS, 0:G_ROWS])
                    for layer in range(2):
                        nc.tensor.transpose(ps[:, 4, 128 + 128 * layer:128 + 128 * layer + CW_ROWS],
                                            cw_rows[0:CW_ROWS, layer, :], ident[0:CW_ROWS, 0:CW_ROWS])
                    for kind in range(2):
                        last = nc.tensor.transpose(ps[:, 5, CMP_LEN * kind:CMP_LEN * (kind + 1)],
                                                   pe_rows[0:CMP_LEN, kind, :], ident[0:CMP_LEN, 0:CMP_LEN])
                    last.then_inc(cols_turned, 1)
            pe.wait_ge(cols_ready, 2)
            for side in (0, 1):
                pe.wait_ge(pair_read[side], PLAN[i0 + 7][1][side])

            chunked_linear(0, HG_DV, grid(block(6), HH, T), grid(block(7), HH, T), grid(block(3), HH, T), grid(block(1), HH, T),
                           lambda tt, hd: tokens(HI + hd * HG_DV, HG_DV, tt), [[7], [0], [1]], [[2], [3]])

            kd = block(0).rearrange("p (t a g d) -> p t a g d", t=TT, a=2, g=NG)
            pe.wait_ge(qk_ready, 1)
            pe.wait_ge(cl_state_ready, 3)
            head_turns(0, lambda j, tt: tokens(NQ + j * P, P, tt) if j < 4 else kd[:, tt, (j - 4) // 2, (j - 4) % 2, :], 8, 4)
            pe.wait_ge(blk_ready, 1)
            pe.wait_ge(w1_in, 64)
            blkT = block(7)[:, 0:2 * CMP_LEN * NCMP].rearrange("p (k l n) -> p k l n", k=2, l=CMP_LEN)
            for kind in range(2):
                for l in range(CMP_LEN):
                    for g in range(NG):
                        last = mm(ps[0:DH, g, SIDE[g] + kind * NCMP:][:, 0:NCMP],
                                  w1[DH * g:DH * g + DH, kind, l, :], blkT[DH * g:DH * g + DH, kind, l, :],
                                  start=(l == 0), stop=(l == CMP_LEN - 1))
            last.then_inc(hid_done, 1)
            pe.wait_ge(hid_ready, 1)
            pe.wait_ge(small_in, 32)
            for kind in range(2):
                for g in range(NG):
                    last = mm(ps[0:NCMP, 1, (kind * NG + g) * DH:(kind * NG + g + 1) * DH], hid[:, kind * NG + g, :], w2[:, kind, :],
                              start=True, stop=True)
            last.then_inc(kvc_done, 1)
            pe.wait_ge(kvc_ready, 1)
            mm(ps[0:NH * NCMP, 1, T:T + P], cview("sel")[0:NCMP, :], kvc[:, 2:4, :], start=True, stop=True).then_inc(vb_done, 1)
            pe.wait_ge(kcd_ready, 1)
            for g in range(NG):
                last = nc.tensor.transpose(ps[:, 0, 256 + g * NCMP:256 + (g + 1) * NCMP], kcd[:, g, :, :], ident[0:NCMP, 0:NCMP])
            last.then_inc(kc_turned, 1)
            pe.wait_ge(kcT_ready, 1)
            pe.wait_ge(qk_read, 4)
            qT, kT = grid(block(2), 4, T), block(6).rearrange("p (a g t) -> p a g t", a=2, g=NG)

            def half(hd):
                return slice(DH * (hd % 2), DH * (hd % 2) + DH)

            for tt in range(TT):
                for hd in range(NH):
                    last = mm(ps[:, hd % 2, SIDE[hd % 2] + (tt * NH + hd) // 2 * NCMP:][:, 0:NCMP], qT[half(hd), hd // 2, tt * P:(tt + 1) * P],
                              kcT[half(hd), hd // (NH // NG), :], start=True, stop=True)
            last.then_inc(cs_done, 1)

            def scores(u):
                tt, hd = u // NH, u % NH
                nk = (tt + 1) * P
                if u >= 2:
                    pe.wait_ge(s_shift, u - 1)
                for kind in range(2):
                    last = mm(ps[:, 4 + u % 2, kind * T:kind * T + nk], qT[half(hd), hd // 2, tt * P:(tt + 1) * P],
                              kT[half(hd), kind, hd // (NH // NG), 0:nk], start=True, stop=True)
                last.then_inc(s_done, 1)

            def weights_turned(u):
                pe.wait_ge(s_exp, u + 1)
                if u >= 2:
                    pe.wait_ge(pT_ready, u - 1)
                for kind in range(2):
                    for kt in range(u // NH + 1):
                        last = nc.tensor.transpose(ps[:, 6 + u % 2, (kind * 2 + kt) * P:(kind * 2 + kt + 1) * P],
                                                   block(0, 2)[:, (u % 4) * 512 + kind * T + kt * P:][:, 0:P], ident)
                last.then_inc(p_turned, 1)

            def weighted(u):
                tt, hd = u // NH, u % NH
                pe.wait_ge(pT_ready, u + 1)
                if u == NH:
                    pe.wait_ge(o_read, 1)
                for kind in range(2):
                    for kt in range(tt + 1):
                        last = mm(ps[:, kind, hd * DH:(hd + 1) * DH], block(3)[:, (u % 2) * 512 + (kind * 2 + kt) * P:][:, 0:P],
                                  tokens((NVS, NVW)[kind] + (hd // (NH // NG)) * DH, DH, kt), start=(kt == 0), stop=(kt == tt))
                if hd == NH - 1:
                    last.then_inc(pv_done, 1)

            scores(0)
            scores(1)
            pe.wait_ge(pc_ready, 1)
            for tt in range(TT):
                last = nc.tensor.transpose(ps[0:NH * NCMP, 1, tt * P:(tt + 1) * P], pc[:, tt, :], ident)
            last.then_inc(pc_turned, 1)
            pe.wait_ge(pcT_ready, 1)
            pe.wait_ge(vb_ready, 1)
            pe.wait_ge(cl_o_read, 1)
            for tt in range(TT):
                last = mm(ps[:, 2 + tt, :], pcT[:, tt, :], vblock.rearrange("p h d -> p (h d)"), start=True, stop=True)
            last.then_inc(oc_done, 1)
            for i in range(2, TT * NH + 3):
                if i < TT * NH:
                    scores(i)
                if i - 2 < TT * NH:
                    weights_turned(i - 2)
                if i >= 3:
                    weighted(i - 3)

            def plain_product(name, n):
                i1 = CHUNK_AT[name]
                for c in range(n):
                    begin(i1 + c)
                    by_tokens(i1 + c, 0, 512, 0).then_inc(chunk_done, 1)

            turn("out1")
            pe.wait_ge(o_read, 2)
            plain_product("w_out", 2)
            pe.wait_ge(keys_in, 16)
            for hc in range(2 * PH):
                last = nc.tensor.transpose(psf[:, 2048 + hc * P:2048 + (hc + 1) * P], keys_raw[:, hc, :], ident)
            last.then_inc(keys_turned, 1)
            pe.wait_ge(keysT_ready, 1)
            turn("peer")
            i1 = CHUNK_AT["peer_wq"]
            for c in range(PH // HPAIR):
                begin(i1 + c)
                by_features(i1 + c, 2 * HPAIR).then_inc(chunk_done, 1)
                pe.wait_ge(*read_out(i1 + c))
                q_ = grid(proj[:, (c % 2) * 1024:(c % 2 + 1) * 1024], 2 * HPAIR, T)
                for tt in range(TT):
                    u = TT * c + tt
                    if u >= 4:
                        pe.wait_ge(sk_read, u - 3)
                    for hc in range(2 * HPAIR):
                        last = mm(ps[:, 4 + u % 4, hc * P:(hc + 1) * P], q_[:, hc, tt * P:(tt + 1) * P], keysT[:, 2 * HPAIR * c + hc, :],
                                  start=True, stop=True)
                    last.then_inc(sk_done, 1)
            for side in (0, 1):
                pe.wait_ge(pair_read[side], PLAN[i1 + 4][1][side])
            pe.wait_ge(p_in, 16)
            i1 = CHUNK_AT["ple_proj"]
            begin(i1)
            for tt in range(TT):
                for k in range(2):
                    last = nc.tensor.transpose(ps[:, 0, k * T + tt * P:k * T + (tt + 1) * P], p_raw[:, tt, k * P:(k + 1) * P], ident)
            last.then_inc(ple_turned, 1)
            pe.wait_ge(pleT_ready, 1)
            w = slot(i1)[:, 0:2048].rearrange("p (k n) -> p k n", k=2)
            for tt in range(TT):
                for half_ in range(2):
                    for k in range(2):
                        last = mm(ps[:, 2 * tt + half_, :], pT[:, k, tt * P:(tt + 1) * P], w[:, k, 512 * half_:512 * half_ + 512],
                                  start=(k == 0), stop=(k == 1))
            last.then_inc(chunk_done, 1)
            turn("ple")
            plain_product("ple_gate_w", 2)
            turn("mix2a")
            i1 = CHUNK_AT["even_w_in"]
            for c in range(7):
                begin(i1 + c)
                by_tokens(i1 + c, 0, 512, 0).then_inc(chunk_done, 1)
            pe.wait_ge(qk_ready, 2)
            head_turns(1, lambda j, tt: tokens(j * P, P, tt), 8, 4)
            pe.wait_ge(qk_ready, 3)
            for side in (0, 1):
                pe.wait_ge(pair_read[side], PLAN[i1 + 7][1][side])
            rot = block(4, 2).rearrange("p (t n) -> p t n", t=TT)
            head_turns(2, lambda j, tt: rot[:, tt, j * P:(j + 1) * P], 8, 0)
            sqT, skT = grid(block(0), 4, T), grid(block(1), 4, T)
            rT = grid(block(2, 2), 8, T)

            def sticks(u):
                at = slice(DH * (u % 2), DH * (u % 2) + DH)
                mm(ps[:, 4 + u % 2, 0:T], skT[at, u // 2, 0:P], sqT[at, u // 2, :], start=True, stop=True)
                mm(ps[:, 4 + u % 2, T:T + P], skT[at, u // 2, P:T], sqT[at, u // 2, P:T], start=True, stop=True).then_inc(sb_z, 1)

            pe.wait_ge(qk_read, 8)
            sticks(0)
            sticks(1)
            for i in range(NH + 2):
                if i < NH:
                    pe.wait_ge(sb_sp, i + 1)
                    if i >= 2:
                        pe.wait_ge(sb_t, i - 1)
                    sp_ = block(6 + i % 2)[:, 0:T + P]
                    o = ps[:, 6 + i % 2, :]
                    mm(o[:, 0:P], cview("negstrict"), sp_[:, 0:P], start=True, stop=True)
                    mm(o[:, P:T], cview("negstrict"), sp_[:, P:T], start=True, stop=False)
                    mm(o[:, P:T], cview("negones"), sp_[:, T:T + P], start=False, stop=True)
                    mm(o[:, T:T + P], cview("negstrict"), sp_[:, T:T + P], start=True, stop=True).then_inc(sb_suf, 1)
                if i + 2 < NH:
                    sticks(i + 2)
                if i >= 2:
                    u = i - 2
                    pe.wait_ge(sb_wm, u + 1)
                    if u == 0:
                        pe.wait_ge(qk_read, 12)
                    w_ = block(6 + u % 2)[:, T + P:2 * (T + P)]
                    v_ = [tokens(1024 + u * DH, DH, tt) for tt in range(TT)]
                    mm(ps[:, 0, u * DH:(u + 1) * DH], w_[:, 0:P], v_[0], start=True, stop=True)
                    mm(ps[:, 1, u * DH:(u + 1) * DH], w_[:, P:T], v_[0], start=True, stop=False)
                    mm(ps[:, 1, u * DH:(u + 1) * DH], w_[:, T:T + P], v_[1], start=False, stop=True).then_inc(sb_o, 1)
            for i in range(HH + 1):
                if i < HH:
                    if i >= 2:
                        pe.wait_ge(ret_d, i - 1)
                    mm(ps[:, 2 + i % 2, 0:T], rT[:, 4 + i, 0:P], rT[:, i, :], start=True, stop=True)
                    mm(ps[:, 2 + i % 2, T:T + P], rT[:, 4 + i, P:T], rT[:, i, P:T], start=True, stop=True).then_inc(ret_s, 1)
                if i >= 1:
                    u = i - 1
                    pe.wait_ge(ret_d, u + 1)
                    d_ = block(u % 2)[:, 0:T + P]
                    v_ = [tokens(2560 + u * DK, DK, tt) for tt in range(TT)]
                    mm(ps[:, 4, u * DK:(u + 1) * DK], d_[:, 0:P], v_[0], start=True, stop=True)
                    mm(ps[:, 5, u * DK:(u + 1) * DK], d_[:, P:T], v_[0], start=True, stop=False)
                    mm(ps[:, 5, u * DK:(u + 1) * DK], d_[:, T:T + P], v_[1], start=False, stop=True).then_inc(ret_o, 1)
            turn("out2")
            plain_product("even_w_out", 2)

            def unit_split(j):
                pe.wait_ge(lo_ready, j + 1)
                pe.wait_ge(lo2_ready, j + 1)
                return w_hi[j % 2], w_lo[j % 2]

            def conv_ffn(layer):
                turn("ffn2" + "ab"[layer])
                i1 = CHUNK_AT[f"up{layer}"]
                for c in range(FCH):
                    begin(i1 + c)
                    for u in range(2):
                        j = FUNITS * layer + 2 * c + u
                        hi, lo = (w[:].rearrange("p (k n) -> p k n", k=KD) for w in unit_split(j))
                        for f in range(2):
                            o = psf[:, 1024 * PLAN[i1 + c][0] + 512 * u + T * f:][:, 0:T]
                            for step, (w, x_) in enumerate(((hi, x_hi), (lo, x_hi), (hi, x_lo))):
                                if c == u == f == 0 and step == 2:
                                    pe.wait_ge(x_lo_ready, layer + 1)
                                for k in range(KD):
                                    last = mm(o, w[:, k, f * P:(f + 1) * P], x_[:, k, :], start=(step == k == 0), stop=(step == 2 and k == KD - 1))
                        last.then_inc(unit_done if u == 0 else chunk_done, 1)
                i1 = CHUNK_AT[f"down{layer}"]
                for c in range(FCH):
                    begin(i1 + c)
                    pe.wait_ge(hidden_ready, layer * FCH + c + 1)
                    hi, lo = (w[:].rearrange("p (k n) -> p k n", k=2) for w in unit_split(FUNITS * layer + 2 * FCH + c))
                    for tt in range(TT):
                        for half_ in range(2):
                            for step, (w, g_) in enumerate(((hi, g_hi), (lo, g_hi), (hi, g_lo))):
                                for k in range(2):
                                    last = mm(ps[:, 2 * tt + half_, :], g_[:, 2 * c + k, tt * P:(tt + 1) * P], w[:, k, 512 * half_:512 * half_ + 512],
                                              start=(c == step == k == 0), stop=(c == FCH - 1 and step == 2 and k == 1), skip_group_check=True)
                    last.then_inc(chunk_done, 1)

            conv_ffn(0)
            turn("mix2b")
            i1 = CHUNK_AT["odd_w_in"]
            for n in range(7):
                begin(i1 + n)
                if n == 0:
                    last = by_features(i1, 1, 16)
                elif n < 3:
                    last = by_features(i1 + n, HH)
                else:
                    last = by_tokens(i1 + n, 0, 512, 0)
                last.then_inc(chunk_done, 1)
                if n == 1:
                    pe.wait_ge(small_in, 32)
                    pe.wait_ge(*read_out(i1))
                    for hd in range(HH):
                        last = mm(psf[:, 4 * 512 + T * hd:][:, 0:T], walpha[:, hd * DK:(hd + 1) * DK], gaT[:], start=True, stop=True)
                    last.then_inc(alpha_done, 1)
            for side in (0, 1):
                pe.wait_ge(pair_read[side], PLAN[i1 + 7][1][side])
            pe.wait_ge(alpha_read, 1)
            chunked_linear(1, GLA_DV, grid(block(3), HH, T), grid(block(7), HH, T), grid(block(3), HH, T), grid(block(1), HH, T),
                           lambda tt, hd: tokens(1024 + hd * GLA_DV, GLA_DV, tt),
                           [[4, 7], [5, 6], [4, 7]], [[0, 1], [2, 3]])
            turn("out3")
            pe.wait_ge(cl_o_read, 2)
            plain_product("odd_w_out", 2)
            conv_ffn(1)

        @blockctx.scalar
        def _(act):
            do = nc.scalar.activation

            def squares(name):
                n = NORMS.index(name)
                if name != "mix1":
                    act.wait_ge(*after(name))
                for tt in range(TT):
                    if name == "mix1":
                        act.wait_ge(x_in[tt], 16)
                    last = do(hn[:, tt, :], h[:, tt, :], ACT.Square, accum_out=ss[:, 2 * n + tt:2 * n + tt + 1])
                last.then_inc(ss_ready, 1)

            def root(name, w, p=P):
                k = ROOTS.index(name)
                act.wait_ge(var_ready, k + 1)
                do(std[0:p, k, 0:w], var[0:p, k, 0:w], ACT.Sqrt).then_inc(std_ready, 1)

            def turn(name):
                n, g = TURNS.index(name), TURN_GAIN[name]
                for b in (2, 3):
                    act.wait_ge(turn_done, 4 * n + b + 1)
                    for k in (2 * b, 2 * b + 1):
                        col = G_ONE if g is None else g + k
                        last = do((x_hi if name.startswith("ffn") else xT)[:, k, :], ps[:, 4 + b, (k % 2) * T:(k % 2 + 1) * T], ACT.Copy,
                                  scale=gcol[:, col:col + 1])
                    last.then_inc(xT_ready, 1)

            def chunk(i):
                act.wait_ge(chunk_done, i + 1)
                return pair(PLAN[i][0]).rearrange("p (t n) -> p t n", t=TT)

            def copy_tokens(i, col, n=512):
                src = chunk(i)
                do(tokens(col, n), src[:, :, 0:n], ACT.Copy).then_inc(pair_read[PLAN[i][0]], 1)

            def decays(n):
                act.wait_ge(cl_diff, 2 * n + 1)
                if n == 0:
                    do(block(6), block(5), ACT.Exp)
                    do(block(7), block(5), ACT.Exp, scale=-1.0)
                else:
                    do(block(7), block(4), ACT.Exp, scale=-1.0)
                do(block(3), block(4), ACT.Exp)
                do(dec[:, n, :], grid(block(4), HH * NCH, CH)[:, :, CH - 1], ACT.Exp).then_inc(cl_exp, 1)

            def last_decay(n):
                act.wait_ge(cl_diff, 2 * n + 2)
                do(block(1), block(5), ACT.Exp).then_inc(cl_exp, 1)

            def keys_to_tokens(n):
                for tt in range(TT):
                    act.wait_ge(cl_k2_turned, 2 * n + tt + 1)
                    do(k2tok[:, tt, :], ps[:, 5 + tt, :], ACT.Copy).then_inc(cl_k2_ready, 1)

            lo, hi = C_COLS["ident"]
            act.dma_start(cst[:, lo:hi], consts[:, lo:hi]).then_inc(ident_in, 16)
            act.dma_start(first_rows[G_MIX:G_MIX + KD, :], a["mix_norm"][0].rearrange("(r c) -> r c", c=P)).then_inc(first_in, 16)
            act.dma_start(first_rows[G_LB:G_LB + 2 * HH, :], a["hg_lb_logits"].rearrange("l (r c) -> (l r) c", c=P)).then_inc(first_in, 16)
            act.dma_start(cst[:, hi:C_WIDTH], consts[:, hi:C_WIDTH]).then_inc(consts_in, 16)

            squares("mix1")
            root("mix1", TT)
            turn("mix1")
            act.wait_ge(lb_in, 1)
            do(lbw[:, 1:3, :], lbw[:, 1:3, :], ACT.Exp).then_inc(lb_exp, 1)
            i0 = CHUNK_AT["w_in"]
            act.wait_ge(chunk_done, i0 + 1)
            do(block(0), pair(PLAN[i0][0]), ACT.Sigmoid).then_inc(sig_ready, 1)
            act.wait_ge(chunk_done, i0 + 2)
            do(block(1), pair(PLAN[i0 + 1][0]), ACT.Sigmoid).then_inc(sig_ready, 1)
            copy_tokens(i0 + 2, HI)
            act.wait_ge(cl_forget, 1)
            do(block(3), block(1), ACT.Ln).then_inc(cl_log, 1)
            decays(0)
            last_decay(0)
            src = chunk(i0 + 3)
            do(tokens(HGT, 512), src, ACT.Sigmoid).then_inc(sig_ready, 1)
            copy_tokens(i0 + 4, NQ)
            src = chunk(i0 + 5)
            do(hn[:, 0, 0:512], src[:, 0, :], ACT.Copy)
            do(tokens(NKS, T), src[:, 1, :].rearrange("p (t n) -> p t n", t=TT), ACT.Copy).then_inc(pair_read[PLAN[i0 + 5][0]], 1)
            src = chunk(i0 + 6)
            do(gates[:], src[:, :, T:T + 24], ACT.Sigmoid)
            do(tokens(NKW, T), src[:, :, 0:T], ACT.Copy).then_inc(pair_read[PLAN[i0 + 6][0]], 1)

            keys_to_tokens(0)
            root("nsa_qk", 24)
            root("hg", TT * HH)
            for b, g in enumerate((G_NQ, G_NQ, G_KS, G_KW)):
                act.wait_ge(qk_turned, b + 1)
                dst = block(2)[:, 512 * b:512 * b + 512] if b < 2 else block(6)[:, 512 * (b - 2):512 * (b - 1)]
                do(dst, ps[:, 4 + b, :], ACT.Copy, scale=gcol[:, g:g + 1]).then_inc(qk_read, 1)
            act.wait_ge(hid_done, 1)
            for g in range(NG):
                last = do(hid[:, g:4:NG, :], grid(ps[0:DH, g, SIDE[g]:SIDE[g] + 2 * NCMP], 2, NCMP), ACT.Gelu_apprx_tanh)
            last.then_inc(hid_ready, 1)
            root("kc", NG, NCMP)
            act.wait_ge(cs_shift, 1)
            do(pc, pc, ACT.Exp).then_inc(cs_exp, 1)

            def exps(u):
                tt, hd = u // NH, u % NH
                nk = (tt + 1) * P
                act.wait_ge(s_shift, u + 1)
                for kind in range(2):
                    e = block(0, 2)[:, (u % 4) * 512 + kind * T:][:, 0:nk]
                    last = do(e, e, ACT.Exp, bias=nmx[:, u, kind:kind + 1], accum_out=sums[:, tt, kind, hd:hd + 1])
                last.then_inc(s_exp, 1)

            for i in range(TT * NH + 2):
                if i >= 2:
                    u = i - 2
                    nk = (u // NH + 1) * P
                    act.wait_ge(p_turned, u + 1)
                    do(block(3)[:, (u % 2) * 512:][:, 0:512].rearrange("p (a n) -> p a n", a=2)[:, :, 0:nk],
                       ps[:, 6 + u % 2, :].rearrange("p (a n) -> p a n", a=2)[:, :, 0:nk], ACT.Copy).then_inc(pT_ready, 1)
                if i < TT * NH:
                    exps(i)
            root("nsa_o", TT * NH)
            turn("out1")
            act.wait_ge(keys_turned, 1)
            do(wX[:, 2048:4096], psf[:, 2048:4096], ACT.Copy).then_inc(keysT_ready, 1)
            squares("peer")
            root("peer", TT)
            turn("peer")
            i1 = CHUNK_AT["peer_wq"]
            for c in range(PH // HPAIR):
                act.wait_ge(chunk_done, i1 + c + 1)
                do(proj[:, (c % 2) * 1024:(c % 2 + 1) * 1024], pair(PLAN[i1 + c][0]), ACT.Copy).then_inc(pair_read[PLAN[i1 + c][0]], 1)
                for u in range(TT * c, TT * (c + 1)):
                    act.wait_ge(sk_done, u + 1)
                    do(unit_scores(u), ps[:, 4 + u % 4, :], ACT.Copy).then_inc(sk_read, 1)
            act.wait_ge(ple_turned, 1)
            do(pT.rearrange("p k t -> p (k t)"), ps[:, 0, :], ACT.Copy).then_inc(pleT_ready, 1)
            act.wait_ge(chunk_done, CHUNK_AT["ple_proj"] + 1)
            for side in (0, 1):
                do(ple[:, side, :], pair(side), ACT.Copy).then_inc(pair_read[side], 1)
            for u in range(UNITS):
                part = slice(u * UROWS, (u + 1) * UROWS)
                act.wait_ge(idx_ready, u + 1)
                do(gatew[:, part], gatew[:, part], ACT.Exp).then_inc(best_exp, 1)
                act.wait_ge(rows_used, GATHER_SLOTS + rows_before(0, u) + UROWS)
                do(dots[:, part], dots[:, part], ACT.Gelu_apprx_tanh).then_inc(gelu_done, 1)
            squares("ple")
            root("ple", TT)
            turn("ple")
            i1 = CHUNK_AT["ple_gate_w"]
            for c in range(2):
                act.wait_ge(chunk_done, i1 + c + 1)
                do(proj[:, c * 1024:(c + 1) * 1024], pair(PLAN[i1 + c][0]), ACT.Sigmoid).then_inc(pair_read[PLAN[i1 + c][0]], 1)
            squares("mix2a")
            root("mix2a", TT)
            turn("mix2a")
            i1 = CHUNK_AT["even_w_in"]
            for c in range(6):
                copy_tokens(i1 + c, 512 * c)
                if c == 2:
                    root("sbqk", 32)
            src = chunk(i1 + 6)
            do(tokens(3072, 512), src, ACT.Sigmoid).then_inc(sig_ready, 1)
            for b, g in enumerate((G_SBQ, G_SBQ, G_SBK, G_SBK)):
                act.wait_ge(qk_turned, 4 + b + 1)
                do(block(b // 2)[:, 512 * (b % 2):512 * (b % 2) + 512], ps[:, 4 + b, :], ACT.Copy,
                   scale=gcol[:, g:g + 1]).then_inc(qk_read, 1)
            for b in range(4):
                act.wait_ge(qk_turned, 8 + b + 1)
                do(block(2, 2)[:, 512 * b:512 * b + 512], ps[:, b, :], ACT.Copy).then_inc(qk_read, 1)
            W = T + P
            chain = 0
            for i in range(NH + 1):
                if i < NH:
                    e = block(4 + i % 2)[:, 0:W]
                    act.wait_ge(sb_z, i + 1)
                    if i >= 2:
                        act.wait_ge(sb_sp, i - 1)
                    if i < 2:
                        act.wait_ge(qk_turned, 12)
                    do(e, ps[:, 4 + i % 2, 0:W], ACT.Abs).then_inc(act_chain, 1)
                    chain += 1
                    act.wait_ge(act_chain, chain)
                    do(e, e, ACT.Exp, scale=-1.0).then_inc(act_chain, 1)
                    chain += 1
                    act.wait_ge(act_chain, chain)
                    do(e, e, ACT.Ln, bias=1.0).then_inc(sb_l, 1)
                if i >= 1:
                    u = i - 1
                    act.wait_ge(sb_t, u + 1)
                    if u >= 2:
                        act.wait_ge(sb_o, u - 1)
                    do(block(6 + u % 2)[:, W:2 * W], block(4 + u % 2)[:, W:2 * W], ACT.Exp).then_inc(sb_w, 1)
            root("ret", TT * HH)
            turn("out2")

            def conv_ffn(layer):
                name = "ffn2" + "ab"[layer]
                squares(name)
                root(name, TT)
                turn(name)
                for c in range(FCH):
                    act.wait_ge(conv_ready, layer * FCH + c + 1)
                    e = conv[:, c % 2]
                    do(e, e, ACT.Silu).then_inc(conv_silu, 1)

            conv_ffn(0)
            squares("mix2b")
            root("mix2b", TT)
            turn("mix2b")
            i1 = CHUNK_AT["odd_w_in"]
            act.wait_ge(chunk_done, i1 + 1)
            do(gaT[:], pair(PLAN[i1][0])[0:16, 0:T], ACT.Copy).then_inc(pair_read[PLAN[i1][0]], 1)
            act.wait_ge(chunk_done, i1 + 2)
            do(block(0), pair(PLAN[i1 + 1][0]), ACT.Copy, scale=DK ** -0.5).then_inc(pair_read[PLAN[i1 + 1][0]], 1)
            chain = 2 * NH
            act.wait_ge(cl_forget, 2)
            do(block(5), block(1), ACT.Abs).then_inc(act_chain, 1)
            chain += 1
            act.wait_ge(act_chain, chain)
            do(block(5), block(5), ACT.Exp, scale=-1.0).then_inc(act_chain, 1)
            chain += 1
            act.wait_ge(act_chain, chain)
            do(block(5), block(5), ACT.Ln, bias=1.0).then_inc(cl_log, 1)
            act.wait_ge(chunk_done, i1 + 3)
            do(block(2), pair(PLAN[i1 + 2][0]), ACT.Copy).then_inc(pair_read[PLAN[i1 + 2][0]], 1)
            decays(1)
            last_decay(1)
            copy_tokens(i1 + 3, 1024)
            copy_tokens(i1 + 4, 1536)
            for c in (4, 5):
                src = chunk(i1 + c + 1)
                do(tokens(512 * c, 512), src, ACT.Sigmoid).then_inc(sig_ready, 1)
            keys_to_tokens(1)
            root("gla", TT * HH)
            turn("out3")
            conv_ffn(1)

        @blockctx.vector
        def _(dve):
            v = nc.vector
            links = [0]

            def link(ins):
                links[0] += 1
                ins.then_inc(dve_chain, 1)
                dve.wait_ge(dve_chain, links[0])

            def rsqrt(name, src, w, p=P, width=None):
                k = ROOTS.index(name)
                v.tensor_scalar(var[0:p, k, 0:w], src, 1.0 / width, EPS, ALU.mult, ALU.add).then_inc(var_ready, 1)
                dve.wait_ge(std_ready, k + 1)
                link(v.reciprocal(rstd[0:p, k, 0:w], std[0:p, k, 0:w]))
                return rstd[0:p, k, 0:w]

            def norm(name, gain=None):
                n = NORMS.index(name)
                dve.wait_ge(ss_ready, n + 1)
                r = rsqrt(name, ss[:, 2 * n:2 * n + 2], TT, width=D)
                for tt in range(TT):
                    ins = v.tensor_scalar(hn[:, tt, :], h[:, tt, :], r[:, tt:tt + 1], None, ALU.mult)
                    if tt and gain is None:
                        ins.then_inc(src_ready, 1)
                    elif tt:
                        link(ins)
                if gain is not None:
                    dve.wait_ge(gain_in, 16)
                    v.tensor_tensor(hn[:], hn[:], gain.unsqueeze(1).broadcast_to((P, TT, D)), ALU.mult).then_inc(src_ready, 1)

            def turn(name):
                n, g = TURNS.index(name), TURN_GAIN[name]
                for b in (0, 1):
                    dve.wait_ge(turn_done, 4 * n + b + 1)
                    for k in (2 * b, 2 * b + 1):
                        col = G_ONE if g is None else g + k
                        ins = v.tensor_scalar((x_hi if name.startswith("ffn") else xT)[:, k, :], ps[:, 4 + b, (k % 2) * T:(k % 2 + 1) * T],
                                              gcol[:, col:col + 1], None, ALU.mult)
                    ins.then_inc(xT_ready, 1)

            def residual(name, n=2):
                i1 = CHUNK_AT[name]
                for c in range(n):
                    dve.wait_ge(chunk_done, i1 + c + 1)
                    o = h[:, :, 512 * c:512 * (c + 1)]
                    v.tensor_tensor(o, o, pair(PLAN[i1 + c][0]).rearrange("p (t n) -> p t n", t=TT), ALU.add)\
                        .then_inc(pair_read[PLAN[i1 + c][0]], 1)

            def over(ap, shape):
                return ap.unsqueeze(len(shape) - 1).broadcast_to(shape)

            def chunk_decays(n):
                dve.wait_ge(cl_log, n + 1)
                if n == 0:
                    link(v.tensor_tensor_scan(block(4), reset[:], block(3), 0.0, ALU.mult, ALU.add))
                    cum = grid(block(4), HH * NCH, CH)
                    mid = cum[:, :, CH // 2 - 1:CH // 2].broadcast_to((P, HH * NCH, CH))
                    v.tensor_tensor(grid(block(5), HH * NCH, CH), cum, mid, ALU.subtract).then_inc(cl_diff, 1)
                else:
                    v.tensor_tensor_scan(block(4), reset[:], block(3), 0.0, ALU.mult, ALU.add).then_inc(cl_diff, 1)
                    cum = grid(block(4), HH * NCH, CH)
                dve.wait_ge(cl_exp, 2 * n + 1)
                end = cum[:, :, CH - 1:CH].broadcast_to((P, HH * NCH, CH))
                v.tensor_tensor(grid(block(5), HH * NCH, CH), end, cum, ALU.subtract).then_inc(cl_diff, 1)
                if n == 0:
                    v.tensor_tensor(block(6), block(6), block(0), ALU.mult)
                v.tensor_tensor(block(7), block(7), block(2), ALU.mult)
                v.tensor_tensor(block(3), block(3), block(0), ALU.mult)
                dve.wait_ge(cl_exp, 2 * n + 2)
                v.tensor_tensor(block(1), block(1), block(2), ALU.mult).then_inc(cl_ready, 1)

            def chunk_states(n, dv, add_banks):
                dve.wait_ge(cl_a_done, n + 1)
                for cc in range(2):
                    part = slice(CH * cc, CH * cc + CH)
                    mask = cview("causal").bitcast(I32)[part].unsqueeze(1).broadcast_to((CH, HH * TT, CH))
                    ins = v.copy_predicated(aTm[part, :, part], mask, grid(ps[part, 4, :], HH * TT, CH))
                ins.then_inc(cl_a_ready, 1)
                for c in range(NCH - 1):
                    dve.wait_ge(cl_add_done, 3 * n + c + 1)
                    for hd in range(HH):
                        new = psf[:, 512 * add_banks[c][hd * dv // 512] + hd * dv % 512:][:, 0:dv]
                        o = state[:, c, hd * dv:(hd + 1) * dv]
                        if c == 0:
                            ins = v.tensor_copy(o, new)
                        else:
                            ins = v.scalar_tensor_tensor(o, state[:, c - 1, hd * dv:(hd + 1) * dv], dec[:, n, hd * NCH + c:hd * NCH + c + 1],
                                                         new, ALU.mult, ALU.add)
                    ins.then_inc(cl_state_ready, 1)
                    dve.wait_ge(cl_state_ready, 3 * n + c + 1)

            def heads_rms(name, x, sq, n, w):
                link(v.tensor_tensor(sq, x, x, ALU.mult))
                k = ROOTS.index(name)
                link(v.tensor_reduce(std[:, k, 0:n], grid(sq, n, w), X, ALU.add))
                return rsqrt(name, std[:, k, 0:n], n, width=w)

            v.memset(aTm[:], 0.0)
            link(v.memset(reset[:], 1.0))
            v.memset(grid(reset[:], HH * NCH, CH)[:, :, 0], 0.0)
            dve.wait_ge(cols_turned, 1)
            v.tensor_copy(gcol[:, 0:FIRST_ROWS], ps[:, 0, 0:FIRST_ROWS]).then_inc(cols_ready, 1)
            dve.wait_ge(cols_ready, 1)

            norm("mix1")
            l0, l1 = gcol[:, G_LB:G_LB + HH], gcol[:, G_LB + HH:G_LB + 2 * HH]
            link(v.tensor_tensor(lbw[:, 0, :], l0, l1, ALU.max))
            v.tensor_tensor(lbw[:, 1, :], l0, lbw[:, 0, :], ALU.subtract)
            v.tensor_tensor(lbw[:, 2, :], l1, lbw[:, 0, :], ALU.subtract).then_inc(lb_in, 1)
            turn("mix1")
            dve.wait_ge(lb_exp, 1)
            link(v.tensor_tensor(lbw[:, 3, :], lbw[:, 1, :], lbw[:, 2, :], ALU.add))
            link(v.reciprocal(lbw[:, 4, :], lbw[:, 3, :]))
            link(v.tensor_tensor(lbw[:, 0, :], lbw[:, 1, :], lbw[:, 4, :], ALU.mult))
            link(v.tensor_scalar(lbw[:, 5, :], lbw[:, 0, :], -1.0, 1.0, ALU.mult, ALU.add))

            i0 = CHUNK_AT["w_in"]
            dve.wait_ge(sig_ready, 1)
            v.scalar_tensor_tensor(block(0), pair(PLAN[i0][0]), DK ** -0.5, block(0), ALU.mult, ALU.mult).then_inc(pair_read[PLAN[i0][0]], 1)
            dve.wait_ge(sig_ready, 2)
            for hd in range(HH):
                f = grid(block(1), HH, T)[:, hd, :]
                ins = v.tensor_scalar(f, f, lbw[:, 5, hd:hd + 1], lbw[:, 0, hd:hd + 1], ALU.mult, ALU.add)
                if hd == 0:
                    ins.then_inc(pair_read[PLAN[i0 + 1][0]], 1)
            ins.then_inc(cl_forget, 1)
            dve.wait_ge(cl_forget, 1)
            v.tensor_scalar(block(2), block(1), -1.0, 1.0, ALU.mult, ALU.add)
            chunk_decays(0)
            dve.wait_ge(sig_ready, 3)
            gate = tokens(HGT, 512)
            src = pair(PLAN[i0 + 3][0]).rearrange("p (t n) -> p t n", t=TT)
            v.tensor_tensor(gate, src, gate, ALU.mult).then_inc(pair_read[PLAN[i0 + 3][0]], 1)
            dve.wait_ge(consts_in, 16)
            dve.wait_ge(cols_turned, 2)
            link(v.tensor_copy(gcol[:, FIRST_ROWS:G_COLS], ps[:, 4, 0:G_ROWS]))
            for col in (G_SBQ, G_NQ):
                v.tensor_scalar(gcol[:, col:col + 1], gcol[:, col:col + 1], DH ** -0.5, None, ALU.mult)
            v.tensor_copy(cw[:], grid(ps[:, 4, 128:384], 2, 128)[:, :, 0:CW_ROWS])
            v.tensor_copy(pe_col[:], grid(ps[:, 5, 0:2 * CMP_LEN], 2, CMP_LEN)).then_inc(cols_ready, 1)
            dve.wait_ge(cols_ready, 2)

            chunk_states(0, HG_DV, [[7], [0], [1]])
            dve.wait_ge(*read_out(i0 + 6))
            dve.wait_ge(*read_out(i0 + 5))
            dve.wait_ge(*read_out(i0 + 4))
            k = ROOTS.index("nsa_qk")
            sq = block(4, 2)[:, 0:TT * 768].rearrange("p (t n) -> p t n", t=TT)
            for lo, n, at in ((NQ, 512, 0), (NKS, 128, 512), (NKW, 128, 640)):
                ins = v.tensor_tensor(sq[:, :, at:at + n], tokens(lo, n), tokens(lo, n), ALU.mult)
            link(ins)
            link(v.tensor_reduce(std[:, k, 0:24], grid(block(4, 2)[:, 0:TT * 768], 24, DH), X, ALU.add))
            r = grid(rsqrt("nsa_qk", std[:, k, 0:24], 24, width=DH), TT, 12)
            for tt in range(TT):
                q = grid(tokens(NQ, 512, tt), NH, DH)
                v.tensor_tensor(q, q, over(r[:, tt, 0:8], (P, NH, DH)), ALU.mult)
            kd = block(0).rearrange("p (t a g e d) -> p t a g e d", t=TT, a=2, g=NG, e=2)
            for tt in range(TT):
                for kind, lo in ((0, NKS), (1, NKW)):
                    for e in range(2):
                        ins = v.tensor_tensor(kd[:, tt, kind, :, e, :], grid(tokens(lo, 128, tt), NG, DH),
                                              over(r[:, tt, 8 + 2 * kind:10 + 2 * kind], (P, NG, DH)), ALU.mult)
            ins.then_inc(qk_ready, 1)
            blkT = block(7)[:, 0:2 * CMP_LEN * NCMP].rearrange("p (k l n) -> p k l n", k=2, l=CMP_LEN)
            for kind in range(2):
                xv = hn[:, 0, kind * T:(kind + 1) * T].rearrange("p (n l) -> p l n", l=CMP_STRIDE)
                for half_ in range(2):
                    ls = slice(half_ * CMP_STRIDE, (half_ + 1) * CMP_STRIDE)
                    ins = v.tensor_tensor(blkT[:, kind, ls, :], xv[:, :, half_:half_ + NCMP],
                                          over(pe_col[:, kind, ls], (P, CMP_STRIDE, NCMP)), ALU.add)
            ins.then_inc(blk_ready, 1)
            dve.wait_ge(cl_o_done, 2)
            link(v.tensor_copy(block(4), psf[:, 1024:2048]))
            r = heads_rms("hg", block(4), block(5), TT * HH, HG_DV)
            o = grid(block(4), TT * HH, HG_DV)
            ins = v.tensor_tensor(o, o, over(r, (P, TT * HH, HG_DV)), ALU.mult)
            ins.then_inc(cl_o_read, 1)
            dve.wait_ge(cl_o_read, 1)
            v.tensor_tensor(mixed[:, :, 0:512], grid(block(4), TT, 512), tokens(HGT, 512), ALU.mult)
            dve.wait_ge(kvc_done, 1)
            v.tensor_copy(kvc[:].rearrange("n a d -> n (a d)"), ps[0:NCMP, 1, 0:4 * DH]).then_inc(kvc_ready, 1)
            dve.wait_ge(kvc_ready, 1)
            k = ROOTS.index("kc")
            link(v.tensor_tensor(kcd[:, :, 0, :], kvc[:, 0:2, :], kvc[:, 0:2, :], ALU.mult))
            link(v.tensor_reduce(std[0:NCMP, k, 0:NG], kcd[:, :, 0, :], X, ALU.add))
            r = rsqrt("kc", std[0:NCMP, k, 0:NG], NG, NCMP, DH)
            for e in range(2):
                ins = v.tensor_tensor(kcd[:, :, e, :], kvc[:, 0:2, :], over(r, (NCMP, NG, DH)), ALU.mult)
            ins.then_inc(kcd_ready, 1)
            dve.wait_ge(vb_done, 1)
            for g in range(NG):
                hs = slice(g * NH // NG, (g + 1) * NH // NG)
                val = ps[0:NH * NCMP, 1, T + g * DH:T + (g + 1) * DH].unsqueeze(1).broadcast_to((NH * NCMP, NH // NG, DH))
                ins = v.tensor_tensor(vblock[:, hs, :], val, over(cview("blk")[0:NH * NCMP, hs], (NH * NCMP, NH // NG, DH)), ALU.mult)
            ins.then_inc(vb_ready, 1)
            dve.wait_ge(kc_turned, 1)
            v.tensor_scalar(kcT[:].rearrange("p g n -> p (g n)"), ps[:, 0, 256:256 + NG * NCMP], gcol[:, G_KC:G_KC + 1], None, ALU.mult)\
                .then_inc(kcT_ready, 1)
            dve.wait_ge(cs_done, 1)
            pcf = pc.rearrange("p t n -> p (t n)")
            pc3 = grid(pcf, TT * NH, NCMP)
            for side in range(2):
                n = TT * NH * NCMP // 2
                ins = v.tensor_tensor(pc3[:, side::2, :], grid(ps[:, side, SIDE[side]:SIDE[side] + n], TT * NH // 2, NCMP),
                                      grid(cview("cbias"), TT * NH, NCMP)[:, side::2, :], ALU.add)
            link(ins)
            link(v.tensor_reduce(cst8[:, 0, :], pc3, X, ALU.max))
            v.tensor_tensor(pc3, pc3, over(cst8[:, 0, :], (P, TT * NH, NCMP)), ALU.subtract).then_inc(cs_shift, 1)
            dve.wait_ge(cs_exp, 1)
            for tt in range(TT):
                m = grid(cview("cmask"), TT, NCMP)[:, tt, :].unsqueeze(1).broadcast_to((P, NH, NCMP))
                ins = v.tensor_tensor(grid(pc[:, tt, :], NH, NCMP), grid(pc[:, tt, :], NH, NCMP), m, ALU.mult)
            link(ins)
            link(v.tensor_reduce(cst8[:, 1, :], pc3, X, ALU.add))
            link(v.tensor_scalar(cst8[:, 1, :], cst8[:, 1, :], 1e-30, None, ALU.max))
            link(v.reciprocal(cst8[:, 2, :], cst8[:, 1, :]))
            v.tensor_tensor(pc3, pc3, over(cst8[:, 2, :], (P, TT * NH, NCMP)), ALU.mult).then_inc(pc_ready, 1)
            dve.wait_ge(pc_turned, 1)
            v.tensor_copy(pcT.rearrange("p t n -> p (t n)"), ps[0:NH * NCMP, 1, 0:T]).then_inc(pcT_ready, 1)

            def shift(u):
                tt, hd = u // NH, u % NH
                nk = (tt + 1) * P
                dve.wait_ge(s_done, u + 1)
                s_ = grid(block(0, 2)[:, (u % 4) * 512:(u % 4 + 1) * 512], 2, T)[:, :, 0:nk]
                d_ = grid(cview("dist"), TT, T)[:, tt, 0:nk].unsqueeze(1).broadcast_to((P, 2, nk))
                link(v.scalar_tensor_tensor(s_, d_, -SLOPES[hd], grid(ps[:, 4 + u % 2, :], 2, T)[:, :, 0:nk], ALU.mult, ALU.add))
                v.tensor_reduce(nmx[:, u, :], s_, X, ALU.max, negate=True).then_inc(s_shift, 1)

            def combine(tt):
                dve.wait_ge(pv_done, tt + 1)
                dve.wait_ge(oc_done, 1)
                dve.wait_ge(s_exp, (tt + 1) * NH)
                g3 = gates[:, tt, :].rearrange("p (h c) -> p c h", c=3)
                link(v.tensor_scalar(sums[:, tt], sums[:, tt], 1e-30, None, ALU.max))
                link(v.reciprocal(coef[:, tt, 0:2, :], sums[:, tt]))
                link(v.tensor_tensor(coef[:, tt, 0:2, :], coef[:, tt, 0:2, :], g3[:, 1:3, :], ALU.mult))
                o = grid(block(4)[:, 512 * tt:512 * tt + 512], NH, DH)
                b = [grid(block(5)[:, 512 * kind:512 * kind + 512], NH, DH) for kind in range(2)]
                shape = (P, NH, DH)
                v.tensor_tensor(o, grid(ps[:, 2 + tt, :], NH, DH), over(g3[:, 0, :], shape), ALU.mult)
                for kind in range(2):
                    ins = v.tensor_tensor(b[kind], grid(ps[:, kind, :], NH, DH), over(coef[:, tt, kind, :], shape), ALU.mult)
                ins.then_inc(o_read, 1)
                dve.wait_ge(o_read, tt + 1)
                link(v.tensor_tensor(o, o, b[0], ALU.add))
                link(v.tensor_tensor(o, o, b[1], ALU.add))

            for u in range(TT * NH):
                shift(u)
                if u == NH + 2:
                    combine(0)
            combine(TT - 1)
            r = heads_rms("nsa_o", block(4), block(5), TT * NH, DH)
            for tt in range(TT):
                ins = v.tensor_tensor(grid(mixed[:, tt, 512:1024], NH, DH), grid(block(4)[:, 512 * tt:512 * tt + 512], NH, DH),
                                      over(r[:, tt * NH:(tt + 1) * NH], (P, NH, DH)), ALU.mult)
            ins.then_inc(src_ready, 1)
            turn("out1")
            residual("w_out")
            norm("peer", gbc)
            turn("peer")
            small = k2tok[:].rearrange("p t n -> p (t n)")
            top_v, top_i, top_f = (grid(small[:, 64 * j:64 * j + 64], 2 * HPAIR, TOPK) for j in range(3))
            best_v, best_i = (grid(small[:, 192 + UROWS * j:192 + UROWS * (j + 1)], HPAIR, TOPK) for j in range(2))
            place, pick = (small[:, 256 + 64 * j:320 + 64 * j] for j in range(2))
            halves = [small[:, 384 + UROWS * j:384 + UROWS * (j + 1)] for j in range(3)]
            st = state[:].rearrange("p c n -> p (c n)")
            cand, rest, onehot = st[:, 0:512], st[:, 512:1024], st[:, 1024:2048]

            def best16(src, left, vals, idx, n):
                for j in range(n):
                    ins = v.max(vals[:, j, 0:8], src[:, j, :])
                link(ins)
                for j in range(n):
                    v.max_index(idx[:, j, 0:8], vals[:, j, 0:8], src[:, j, :])
                    ins = v.match_replace(left[:, j, :], vals[:, j, 0:8], src[:, j, :], -3e38)
                link(ins)
                for j in range(n):
                    ins = v.max(vals[:, j, 8:16], left[:, j, :])
                link(ins)
                for j in range(n):
                    ins = v.max_index(idx[:, j, 8:16], vals[:, j, 8:16], left[:, j, :])
                link(ins)

            def best_keys(u, hd):
                dve.wait_ge(sk_read, u + 1)
                two = slice(2 * hd, 2 * hd + 2)
                best16(grid(unit_scores(u), 2 * HPAIR, NK)[:, two], grid(rest, 2 * HPAIR, NK)[:, two], top_v[:, two], top_i.bitcast(U32)[:, two], 2)
                v.tensor_copy(top_f[:, two], top_i.bitcast(U32)[:, two])
                link(v.tensor_tensor(grid(grid(cand, HPAIR, TOPK * TOPK)[:, hd, :], TOPK, TOPK), over(top_v[:, 2 * hd, :], (P, TOPK, TOPK)),
                                     top_v[:, 2 * hd + 1, :].unsqueeze(1).broadcast_to((P, TOPK, TOPK)), ALU.add))

            def best_sums(hd):
                one = slice(hd, hd + 1)
                best16(grid(cand, HPAIR, TOPK * TOPK)[:, one], grid(rest, HPAIR, TOPK * TOPK)[:, one],
                       best_v[:, one], best_i.bitcast(U32)[:, one], 1)

            def places(u):
                bi = small[:, 192 + UROWS:192 + 2 * UROWS].bitcast(U32)
                v.tensor_scalar(halves[0].bitcast(U32), bi, 4, None, ALU.logical_shift_right)
                v.tensor_scalar(halves[1].bitcast(U32), bi, 15, None, ALU.bitwise_and)
                logits = grid(gatew[:, u * UROWS:(u + 1) * UROWS], HPAIR, TOPK)
                link(v.tensor_tensor(logits, best_v, best_v[:, :, 0:1].broadcast_to((P, HPAIR, TOPK)), ALU.subtract))
                place4 = place.rearrange("p (h c k) -> p h c k", h=HPAIR, c=2)
                for side in range(2):
                    ins = v.tensor_copy(place4[:, :, side, :], grid(halves[side].bitcast(U32), HPAIR, TOPK))
                link(ins)
                link(v.tensor_tensor(grid(onehot, 2 * UROWS, TOPK), cview("iota").unsqueeze(1).broadcast_to((P, 2 * UROWS, TOPK)),
                                     over(place, (P, 2 * UROWS, TOPK)), ALU.is_equal))

            def route(u):
                hot = onehot.rearrange("p (h k j) -> p h k j", h=2 * HPAIR, k=TOPK)
                link(v.tensor_tensor(hot, hot, top_f.unsqueeze(2).broadcast_to((P, 2 * HPAIR, TOPK, TOPK)), ALU.mult))
                link(v.tensor_reduce(pick, grid(onehot, 2 * UROWS, TOPK), X, ALU.add))
                pick4 = pick.rearrange("p (h c k) -> p h c k", h=HPAIR, c=2)
                link(v.scalar_tensor_tensor(grid(halves[2], HPAIR, TOPK), pick4[:, :, 0, :], float(NK), pick4[:, :, 1, :], ALU.mult, ALU.add))
                v.tensor_copy(routes[:, u * UROWS:(u + 1) * UROWS], halves[2]).then_inc(idx_ready, 1)

            def products(u, lo, n):
                first = rows_before(0, u) + lo
                with dve.Fori(0, n // GATHER_SLOTS) as i:
                    for s_ in range(GATHER_SLOTS):
                        row = arena[:, s_, :]
                        dve.wait_ge(gathered[s_], i * 16 + 16 * (first // GATHER_SLOTS + 1))
                        v.scalar_tensor_tensor(row, row, 1.0, hn[:, u % TT, :], ALU.mult, ALU.mult,
                                               accum_out=dots[:, bass.ds(i * GATHER_SLOTS + (u * UROWS + lo + s_), 1)]).then_inc(rows_used, 1)

            def expert_weights(u):
                w_ = gatew[:, u * UROWS:(u + 1) * UROWS]
                w3 = grid(w_, HPAIR, TOPK)
                total, share = (small[:, 480 + HPAIR * j:480 + HPAIR * (j + 1)] for j in range(2))
                dve.wait_ge(best_exp, u + 1)
                link(v.tensor_reduce(total, w3, X, ALU.add))
                link(v.reciprocal(share, total))
                link(v.tensor_tensor(w3, w3, over(share, (P, HPAIR, TOPK)), ALU.mult))
                dve.wait_ge(gelu_done, u + 1)
                link(v.tensor_tensor(w_, w_, dots[:, u * UROWS:(u + 1) * UROWS], ALU.mult))

            def weighted_rows(u, lo, n):
                first = rows_before(1, u) + lo
                accs = sums2[0][:, u % TT, :], sums2[1][:, u % TT, :]
                with dve.Fori(0, n // GATHER_SLOTS) as i:
                    for s_ in range(GATHER_SLOTS):
                        dve.wait_ge(gathered[s_], i * 16 + 16 * (first // GATHER_SLOTS + 1))
                        dve.wait_ge(rows_used, i * GATHER_SLOTS + (GATHER_SLOTS + first + s_ - 1))
                        v.scalar_tensor_tensor(accs[s_ % 2], arena[:, s_, :], gatew[:, bass.ds(i * GATHER_SLOTS + (u * UROWS + lo + s_), 1)],
                                               accs[s_ % 2], ALU.mult, ALU.add).then_inc(rows_used, 1)

            sums2 = mixed, xT[:].rearrange("p (t a) n -> p t (a n)", t=TT)
            v.memset(sums2[0][:], 0.0).then_inc(rows_used, GATHER_SLOTS)
            for u in range(2):
                for hd in range(HPAIR):
                    best_keys(u, hd)
                for hd in range(HPAIR):
                    best_sums(hd)
                places(u)
                route(u)
            products(0, 0, UROWS)
            dve.wait_ge(chunk_done, CHUNK_AT["peer_wq"] + PH // HPAIR)
            v.memset(sums2[1], 0.0)
            for u in range(UNITS - 2):
                best_keys(u + 2, 0)
                products(u + 1, 0, 16)
                best_keys(u + 2, 1)
                products(u + 1, 16, 16)
                expert_weights(u)
                best_sums(0)
                weighted_rows(u, 0, 8)
                best_sums(1)
                weighted_rows(u, 8, 8)
                places(u + 2)
                weighted_rows(u, 16, 8)
                route(u + 2)
                weighted_rows(u, 24, 8)
            products(UNITS - 1, 0, UROWS)
            for u in range(UNITS - 2, UNITS):
                expert_weights(u)
                weighted_rows(u, 0, UROWS)
            dve.wait_ge(rows_used, GATHER_SLOTS + 2 * UNITS * UROWS)
            link(v.tensor_tensor(h[:], h[:], sums2[0][:], ALU.add))
            v.tensor_tensor(h[:], h[:], sums2[1], ALU.add).then_inc(h_ready, 1)
            norm("ple")
            turn("ple")
            i1 = CHUNK_AT["ple_gate_w"]
            for c in range(2):
                dve.wait_ge(*read_out(i1 + c))
                g_ = grid(proj[:, c * 1024:(c + 1) * 1024], TT, 512)
                link(v.tensor_tensor(g_, g_, ple[:, :, 512 * c:512 * (c + 1)], ALU.mult))
                ins = v.tensor_tensor(h[:, :, 512 * c:512 * (c + 1)], h[:, :, 512 * c:512 * (c + 1)], g_, ALU.add)
            ins.then_inc(h_ready, 1)
            norm("mix2a")
            turn("mix2a")
            i1 = CHUNK_AT["even_w_in"]
            dve.wait_ge(*read_out(i1))
            dve.wait_ge(*read_out(i1 + 1))
            k = ROOTS.index("sbqk")
            for tt in range(TT):
                ins = v.tensor_tensor(block(4 + tt), tokens(0, 1024, tt), tokens(0, 1024, tt), ALU.mult)
            link(ins)
            link(v.tensor_reduce(std[:, k, 0:32], grid(block(4, 2), 32, DH), X, ALU.add))
            r = rsqrt("sbqk", std[:, k, 0:32], 32, width=DH)
            for tt in range(TT):
                q = grid(tokens(0, 1024, tt), 2 * NH, DH)
                ins = v.tensor_tensor(q, q, over(r[:, tt * 16:(tt + 1) * 16], (P, 2 * NH, DH)), ALU.mult)
            ins.then_inc(qk_ready, 1)
            dve.wait_ge(*read_out(i1 + 3))
            dve.wait_ge(*read_out(i1 + 4))
            shape = (P, 2 * HH, 64)
            for tt in range(TT):
                x_ = tokens(1536, 1024, tt).rearrange("p (h e d) -> p h e d", h=2 * HH, e=2)
                o = block(4 + tt).rearrange("p (h e d) -> p h e d", h=2 * HH, e=2)
                cos, sin = (grid(cview(n_), TT, 64)[:, tt, :].unsqueeze(1).broadcast_to(shape) for n_ in ("cos", "sin"))
                t_ = block(6 + tt).rearrange("p (h e d) -> p h e d", h=2 * HH, e=2)
                v.tensor_tensor(t_[:, :, 0, :], x_[:, :, 1, :], sin, ALU.mult)
                v.tensor_tensor(t_[:, :, 1, :], x_[:, :, 0, :], sin, ALU.mult)
                v.tensor_tensor(o[:, :, 0, :], x_[:, :, 0, :], cos, ALU.mult)
                link(v.tensor_tensor(o[:, :, 1, :], x_[:, :, 1, :], cos, ALU.mult))
                v.tensor_tensor(o[:, :, 0, :], o[:, :, 0, :], t_[:, :, 0, :], ALU.subtract)
                ins = v.tensor_tensor(o[:, :, 1, :], o[:, :, 1, :], t_[:, :, 1, :], ALU.add)
            ins.then_inc(qk_ready, 1)
            dve.wait_ge(sig_ready, 4)
            gate = tokens(3072, 512)
            src = pair(PLAN[i1 + 6][0]).rearrange("p (t n) -> p t n", t=TT)
            v.tensor_tensor(gate, src, gate, ALU.mult).then_inc(pair_read[PLAN[i1 + 6][0]], 1)
            W = T + P

            def diagonal(ap):
                return grid(ap, 3, P)[:, 0:3:2, :]

            strict = cview("sbmask").unsqueeze(1).broadcast_to((P, 2, P))
            for i in range(NH + 2):
                if i < NH:
                    dve.wait_ge(sb_l, i + 1)
                    if i >= 2:
                        dve.wait_ge(sb_w, i - 1)
                    z, l = ps[:, 4 + i % 2, 0:W], block(4 + i % 2)[:, 0:W]
                    lb, sp_ = block(4 + i % 2)[:, W:2 * W], block(6 + i % 2)[:, 0:W]
                    v.scalar_tensor_tensor(lb, z, 0.0, l, ALU.min, ALU.subtract)
                    link(v.scalar_tensor_tensor(sp_, z, 0.0, l, ALU.max, ALU.add))
                    v.tensor_tensor(diagonal(sp_), diagonal(sp_), strict, ALU.mult).then_inc(sb_sp, 1)
                if 1 <= i <= NH:
                    u = i - 1
                    dve.wait_ge(sb_suf, u + 1)
                    lb = block(4 + u % 2)[:, W:2 * W]
                    v.tensor_tensor(lb, lb, ps[:, 6 + u % 2, 0:W], ALU.add).then_inc(sb_t, 1)
                if i >= 2:
                    u = i - 2
                    dve.wait_ge(sb_w, u + 1)
                    w_ = diagonal(block(6 + u % 2)[:, W:2 * W])
                    v.tensor_tensor(w_, w_, strict, ALU.mult).then_inc(sb_wm, 1)
            for i in range(HH):
                dve.wait_ge(ret_s, i + 1)
                if i >= 2:
                    dve.wait_ge(ret_o, i - 1)
                if i < 2:
                    dve.wait_ge(sb_o, NH)
                dc = grid(cview("decay"), HH, T)[:, i, :]
                v.tensor_tensor(block(i % 2)[:, 0:T], ps[:, 2 + i % 2, 0:T], dc, ALU.mult)
                v.tensor_tensor(block(i % 2)[:, T:W], ps[:, 2 + i % 2, T:W], dc[:, 0:P], ALU.mult).then_inc(ret_d, 1)
            v.tensor_copy(mixed[:, :, 0:512], grid(psf[:, 0:1024], TT, 512))
            dve.wait_ge(ret_o, HH)
            link(v.tensor_copy(block(4), psf[:, 2048:3072]))
            r = heads_rms("ret", block(4), block(5), TT * HH, DK)
            o = grid(block(4), TT * HH, DK)
            link(v.tensor_tensor(o, o, over(r, (P, TT * HH, DK)), ALU.mult))
            v.tensor_tensor(mixed[:, :, 512:1024], grid(block(4), TT, 512), gate, ALU.mult).then_inc(src_ready, 1)
            turn("out2")
            residual("even_w_out")

            def split(j):
                i, w = unit_weights(j)
                dve.wait_ge(chunk_loaded[i % RING], 16 * (i // RING + 1))
                if j >= 2:
                    before, k = unit_weights(j - 2)[0], (j - 2) % FUNITS
                    if k < 2 * FCH and k % 2 == 0:
                        dve.wait_ge(unit_done, (j - 2) // FUNITS * FCH + k // 2 + 1)
                    else:
                        dve.wait_ge(chunk_done, before + 1)
                v.tensor_copy(w_hi[j % 2][:], w).then_inc(hi_ready, 1)
                dve.wait_ge(hi_ready, j + 1)
                part = slice(0, FHALF // 2)
                v.tensor_tensor(w_lo[j % 2][:, part], w[:, part], w_hi[j % 2][:, part].bitcast(F32), ALU.subtract).then_inc(lo_ready, 1)

            def conv_ffn(layer):
                name, j = "ffn2" + "ab"[layer], FUNITS * layer
                split(j)
                norm(name)
                split(j + 1)
                turn(name)
                n, g = TURNS.index(name), TURN_GAIN[name]
                dve.wait_ge(xT_ready, 4 * (n + 1))
                for k in range(KD):
                    ins = v.scalar_tensor_tensor(x_lo[:, k, :], ps[:, 4 + k // 2, (k % 2) * T:(k % 2 + 1) * T], gcol[:, g + k:g + k + 1],
                                                 x_hi[:, k, :].bitcast(F32), ALU.mult, ALU.subtract)
                ins.then_inc(x_lo_ready, 1)
                i1 = CHUNK_AT[f"up{layer}"]
                for c in range(FCH):
                    dve.wait_ge(unit_done, layer * FCH + c + 1)
                    split(j + 2 * c + 2)
                    u_, v_ = (grid(pair(PLAN[i1 + c][0])[:, 512 * m:512 * m + 512], 2, T) for m in range(2))
                    e = conv[:, c % 2]

                    def tap(m, f):
                        return cw[:, layer, m * FT + 2 * c + f:m * FT + 2 * c + f + 1]

                    for f in range(2):
                        ins = v.tensor_scalar(e[:, f, :], u_[:, f, :], tap(2, f), tap(3, f), ALU.mult, ALU.add)
                    link(ins)
                    for back in (1, 2):
                        for f in range(2):
                            ins = v.scalar_tensor_tensor(e[:, f, back:T], u_[:, f, 0:T - back], tap(2 - back, f), e[:, f, back:T], ALU.mult, ALU.add)
                        if back == 1:
                            link(ins)
                    ins.then_inc(conv_ready, 1)
                    dve.wait_ge(chunk_done, i1 + c + 1)
                    split(j + 2 * c + 3)
                    dve.wait_ge(conv_silu, layer * FCH + c + 1)
                    v.tensor_tensor(e, e, v_, ALU.mult).then_inc(pair_read[PLAN[i1 + c][0]], 1)
                    dve.wait_ge(*read_out(i1 + c))
                    two = slice(2 * c, 2 * c + 2)
                    link(v.tensor_copy(g_hi[:, two, :], e))
                    v.tensor_tensor(g_lo[:, two, :], e, g_hi[:, two, :].bitcast(F32), ALU.subtract).then_inc(hidden_ready, 1)
                for k in range(2 * FCH + 2, FUNITS):
                    split(j + k)
                dve.wait_ge(chunk_done, CHUNK_AT[f"down{layer}"] + FCH)
                for tt in range(TT):
                    v.tensor_tensor(h[:, tt, :], h[:, tt, :], pair(tt), ALU.add).then_inc(pair_read[tt], 1)

            conv_ffn(0)
            norm("mix2b")
            turn("mix2b")
            i1 = CHUNK_AT["odd_w_in"]
            dve.wait_ge(alpha_done, 1)
            for hd in range(HH):
                ins = v.tensor_scalar(block(1)[:, hd * T:(hd + 1) * T], psf[:, 2048 + T * hd:2048 + T * (hd + 1)],
                                      gcol[:, G_BAL + hd:G_BAL + hd + 1], None, ALU.add)
            ins.then_inc(cl_forget, 1)
            dve.wait_ge(cl_forget, 2)
            v.tensor_scalar(block(6), block(1), 0.0, 1.0 / 16.0, ALU.min, ALU.mult).then_inc(alpha_read, 1)
            dve.wait_ge(alpha_read, 1)
            dve.wait_ge(cl_log, 2)
            link(v.scalar_tensor_tensor(block(3), block(5), -1.0 / 16.0, block(6), ALU.mult, ALU.add))
            chunk_decays(1)
            for c in (4, 5):
                dve.wait_ge(sig_ready, 5 + c - 4)
                g_ = tokens(512 * c, 512)
                src = pair(PLAN[i1 + c + 1][0]).rearrange("p (t n) -> p t n", t=TT)
                v.tensor_tensor(g_, src, g_, ALU.mult).then_inc(pair_read[PLAN[i1 + c + 1][0]], 1)
            chunk_states(1, GLA_DV, [[4, 7], [5, 6], [4, 7]])
            dve.wait_ge(cl_o_done, 4)
            link(v.tensor_copy(block(4, 2), psf[:, 0:2048]))
            r = heads_rms("gla", block(4, 2), block(6, 2), TT * HH, GLA_DV)
            o = grid(block(4, 2), TT * HH, GLA_DV)
            v.tensor_tensor(o, o, over(r, (P, TT * HH, GLA_DV)), ALU.mult).then_inc(cl_o_read, 1)
            dve.wait_ge(cl_o_read, 2)
            v.tensor_tensor(mixed[:], grid(block(4, 2), TT, 1024), tokens(2048, 1024), ALU.mult).then_inc(src_ready, 1)
            turn("out3")
            residual("odd_w_out")
            conv_ffn(1)

        @blockctx.gpsimd
        def _(pool):
            pool.memset(rows[:, 0:5 * P], 1.0).then_inc(rows_blank, 1)
            pool.wait_ge(rows_blank, 1)
            n_rows = 0

            def to_rows(dst, src):
                nonlocal n_rows
                pool.dma_start(dst, src).then_inc(rows_in, 16)
                n_rows += 1

            def lines(col, n, src):
                to_rows(g_rows[col - FIRST_ROWS:col - FIRST_ROWS + n, :], src)

            for col, n, src in ((G_OUT1, 4, a["hg_out_norm"][0]), (G_OUT1 + 4, 4, a["nsa_out_norm"][0]),
                                (G_PLE, KD, a["ple_gate_norm"][0]), (G_BAL, HH, a["gla_b_alpha_2"][0])):
                lines(col, n, src.rearrange("(r c) -> r c", c=P))
            for col, src in ((G_MIX2[0], a["mix_norm_g_2"]), (G_FFN2[0], a["ffn_norm_g_2"])):
                lines(col, 2 * KD, src.rearrange("l (r c) -> (l r) c", c=P))
            lines(G_OUT2 + HH, HH, a["ret_out_gain_2"][0].partition_broadcast(HH))
            for j in range(HH):
                lines(G_OUT3 + 2 * j, 2, a["gla_out_gain_2"][0].rearrange("(r c) -> r c", c=P))
            for col, n, src in ((G_SBQ, 1, a["sb_q_gain_2"]), (G_SBK, 1, a["sb_k_gain_2"]), (G_NQ, 1, a["nsa_q_norm"]),
                                (G_KC, 3, a["nsa_k_norm"][0])):
                for half_ in range(2):
                    to_rows(g_rows[col - FIRST_ROWS:col - FIRST_ROWS + n, DH * half_:DH * half_ + DH], src)
            for layer in range(2):
                to_rows(cw_rows[0:3 * FT, layer, :], a["ffn_conv_w_2"][layer].rearrange("j (f c) -> (j f) c", c=P))
            to_rows(cw_rows[3 * FT:4 * FT, :, :], a["ffn_conv_b_2"].rearrange("l (f c) -> f l c", c=P))
            for half_ in range(2):
                to_rows(pe_rows[0:CMP_LEN, :, DH * half_:DH * half_ + DH], a["cmp_pe"][0].rearrange("k l d -> l k d"))
            assert n_rows == N_ROW_DMAS
            for half_ in range(2):
                for kind in range(2):
                    pool.dma_start(w1[DH * half_:DH * half_ + DH, kind], a["cmp_w1"][0, kind].rearrange("(l d) m -> d l m", d=DH)).then_inc(w1_in, 16)
            pool.dma_start(w2[:], a["cmp_w2"][0].rearrange("k d m -> d k m")).then_inc(small_in, 16)
            pool.dma_start(walpha[:], a["gla_w_alpha_2"][0]).then_inc(small_in, 16)
            pool.wait_ge(hid_done, 1)
            pool.dma_start(keys_raw, a["peer_keys"][0].rearrange("h c k d -> k (h c) d")).then_inc(keys_in, 16)
            pool.dma_start(gbc, a["ffn_norm"][0].partition_broadcast(P)).then_inc(gain_in, 16)
            pool.wait_ge(src_ready, 2)
            pool.dma_start(p_raw, a["p"][0, 0].rearrange("(t p) d -> p t d", p=P)).then_inc(p_in, 16)
            def gather(side, u, first, steps):
                table = a[("peer_u", "peer_v")[side]][0]
                for half_ in range(UROWS // TOPK):
                    pool.tensor_copy(stage[:, half_, :], routes[:, bass.ds(u * UROWS + half_ * TOPK, TOPK)]).then_inc(pool_chain, 1)
                    pool.wait_ge(pool_chain, steps + (half_ + 1))
                    for k in range(TOPK):
                        b = half_ * TOPK + k
                        pool.wait_ge(rows_used, first + (b + 1))
                        pool.sem_inc(slots_taken, 1)
                        pool.indirect_dma_start(arena[:, b % GATHER_SLOTS, :], None, table,
                                                bass.IndirectOffsetOnAxis(ap=stage[:, half_, k:k + 1], axis=0))\
                            .then_inc(gathered[b % GATHER_SLOTS], 16)

            pool.wait_ge(idx_ready, 1)
            gather(0, 0, 0, 0)
            with pool.Fori(0, UNITS - 1) as i:
                pool.wait_ge(idx_ready, i + 2)
                pool.sem_inc(units_taken, 1)
                gather(0, i + 1, i * (2 * UROWS) + rows_before(0, 1), i * 4 + 2)
                gather(1, i, i * (2 * UROWS) + rows_before(1, 0), i * 4 + 4)
            gather(1, UNITS - 1, rows_before(1, UNITS - 1), 4 * UNITS - 2)
            for j in range(2 * FUNITS):
                w = unit_weights(j)[1]
                part = slice(FHALF // 2, FHALF)
                pool.wait_ge(hi_ready, j + 1)
                nc.gpsimd.tensor_tensor(w_lo[j % 2][:, part], w[:, part], w_hi[j % 2][:, part].bitcast(F32), ALU.subtract).then_inc(lo2_ready, 1)


def kernel(**inputs):
    import concourse.bacc as bacc
    from concourse.bass_utils import run_bass_kernel_spmd

    nc = bacc.Bacc("TRN2", target_bir_lowering=False, num_devices=1)
    arrays, aps = {}, {}
    for name, value in inputs.items():
        value = np.ascontiguousarray(value)
        arrays["in_" + name] = value
        aps[name] = nc.dram_tensor("in_" + name, value.shape, mybir.dt.from_np(value.dtype), kind="ExternalInput").ap()
    arrays["shape_constants"] = shape_constants()
    consts = nc.dram_tensor("shape_constants", (P, C_WIDTH), F32, kind="ExternalInput").ap()
    out = nc.dram_tensor("out", (1, T, D), F32, kind="ExternalOutput").ap()
    two_blocks(nc, aps, consts, out)
    r = run_bass_kernel_spmd(nc, [arrays], core_ids=[0])
    return r.results[0]["out"]
```
